# Optimizing a Trainium2 kernel written in Bass

```python
import jax, jax.numpy as jnp
from jax import lax
import numpy as np

D_MODEL = 1024
BATCH = 1
SEQ = 512
DEPTH = 1

CHUNK = 64
D_MIX = D_MODEL
SSD_HEADS = 8
SSD_HEAD_DIM = 64
SSD_INNER = SSD_HEADS * SSD_HEAD_DIM
SSD_GROUPS = 2
SSD_STATE = 128
CONV_WIDTH = 4
SSD_CONV_DIM = SSD_INNER + 2 * SSD_GROUPS * SSD_STATE
ATT_HEADS = 8
ATT_HEAD_DIM = 64
ATT_INNER = ATT_HEADS * ATT_HEAD_DIM
Q_BLOCK = 128
N_EXPERT_GROUPS = 4
EXPERTS_PER_GROUP = 4
N_EXPERTS = N_EXPERT_GROUPS * EXPERTS_PER_GROUP
TOP_K = 2
D_FF_EXPERT = 512
DEEPNORM_ALPHA = (2.0 * DEPTH) ** 0.25
DEEPNORM_BETA = (8.0 * DEPTH) ** -0.25
LN_EPS = 1e-5
RMS_EPS = 1e-5
IN_SIZES = (SSD_INNER, SSD_CONV_DIM, SSD_HEADS, ATT_INNER, ATT_INNER, ATT_INNER, ATT_HEADS)
D_IN_PROJ = SSD_INNER + SSD_CONV_DIM + SSD_HEADS + 3 * ATT_INNER + ATT_HEADS


def _split_cols(u, sizes):
    idx = np.cumsum(np.array(sizes))[:-1].tolist()
    return jnp.split(u, idx, axis=-1)

def _layer_norm(u, g, b):
    uf = u.astype(jnp.float32)
    mu = jnp.mean(uf, axis=-1, keepdims=True)
    var = jnp.mean(jnp.square(uf - mu), axis=-1, keepdims=True)
    return ((uf - mu) * lax.rsqrt(var + LN_EPS) * g + b).astype(u.dtype)

def _causal_dwconv(u, w, b):
    s = u.shape[1]
    up = jnp.pad(u, ((0, 0), (CONV_WIDTH - 1, 0), (0, 0)))
    out = b
    for k in range(CONV_WIDTH):
        out = out + up[:, k:k + s, :] * w[k]
    return out

def _ssd_scan(xs, dt, a, bm, cm, d_skip):
    f32 = jnp.float32
    xs, dt, bm, cm = xs.astype(f32), dt.astype(f32), bm.astype(f32), cm.astype(f32)
    b, s, h, p = xs.shape
    nc = s // CHUNK
    r = h // SSD_GROUPS
    xdt = (xs * dt[..., None]).reshape(b, nc, CHUNK, SSD_GROUPS, r, p)
    da = (dt * a.astype(f32)).reshape(b, nc, CHUNK, SSD_GROUPS, r)
    bc = bm.reshape(b, nc, CHUNK, SSD_GROUPS, SSD_STATE)
    cc = cm.reshape(b, nc, CHUNK, SSD_GROUPS, SSD_STATE)
    a_cum = jnp.cumsum(da, axis=2)
    seg = a_cum[:, :, :, None] - a_cum[:, :, None, :]
    tri = jnp.tril(jnp.ones((CHUNK, CHUNK), dtype=bool))[None, None, :, :, None, None]
    lmat = jnp.exp(jnp.where(tri, seg, -jnp.inf))
    cb = jnp.einsum('bclgn,bcsgn->bclsg', cc, bc)
    y_diag = jnp.einsum('bclsg,bclsgr,bcsgrp->bclgrp', cb, lmat, xdt)
    decay_to_end = jnp.exp(a_cum[:, :, -1:] - a_cum)
    chunk_states = jnp.einsum('bclgn,bclgr,bclgrp->bcgrpn', bc, decay_to_end, xdt)
    chunk_decay = jnp.exp(a_cum[:, :, -1])

    def step(state, inp):
        st, dec = inp
        return state * dec[..., None, None] + st, state

    init = jnp.zeros((b, SSD_GROUPS, r, p, SSD_STATE), f32)
    _, states_in = lax.scan(step, init, (jnp.moveaxis(chunk_states, 1, 0),
                                         jnp.moveaxis(chunk_decay, 1, 0)))
    states_in = jnp.moveaxis(states_in, 0, 1)
    y_off = jnp.einsum('bclgn,bcgrpn,bclgr->bclgrp', cc, states_in, jnp.exp(a_cum))
    y = (y_diag + y_off).reshape(b, s, h, p)
    return y + xs * d_skip.astype(f32)[:, None]

def _forgetting_attention(q, k, v, log_f):
    b, s, h, d = q.shape
    fcum = jnp.transpose(jnp.cumsum(log_f, axis=1), (0, 2, 1))
    scale = d ** -0.5
    outs = []
    for blk in range(s // Q_BLOCK):
        q0, q1 = blk * Q_BLOCK, (blk + 1) * Q_BLOCK
        logits = jnp.einsum('bqhd,bkhd->bhqk', q[:, q0:q1], k[:, :q1]).astype(jnp.float32) * scale
        logits = logits + fcum[:, :, q0:q1, None] - fcum[:, :, None, :q1]
        qpos = jnp.arange(q0, q1)[:, None]
        kpos = jnp.arange(q1)[None, :]
        logits = jnp.where(qpos >= kpos, logits, -jnp.inf)
        probs = jax.nn.softmax(logits, axis=-1)
        outs.append(jnp.einsum('bhqk,bkhd->bqhd', probs.astype(v.dtype), v[:, :q1]))
    return jnp.concatenate(outs, axis=1)

def _hybrid_mixer(h, w_in, b_in, conv_w, conv_b, a_log, d_skip, ssd_norm_g, w_out):
    bsz, s, _ = h.shape
    proj = jnp.einsum('bsd,de->bse', h, w_in) + b_in
    z, xbc, dt_raw, q, k, v, f_raw = _split_cols(proj, IN_SIZES)
    xbc = jax.nn.silu(_causal_dwconv(xbc, conv_w, conv_b))
    xs, bm, cm = _split_cols(xbc, (SSD_INNER, SSD_GROUPS * SSD_STATE, SSD_GROUPS * SSD_STATE))
    xs = xs.reshape(bsz, s, SSD_HEADS, SSD_HEAD_DIM)
    bm = bm.reshape(bsz, s, SSD_GROUPS, SSD_STATE)
    cm = cm.reshape(bsz, s, SSD_GROUPS, SSD_STATE)
    dt = jax.nn.softplus(dt_raw.astype(jnp.float32))
    a = -jnp.exp(a_log.astype(jnp.float32))
    y = _ssd_scan(xs, dt, a, bm, cm, d_skip).reshape(bsz, s, SSD_INNER)
    y = (y * jax.nn.silu(z.astype(jnp.float32))).reshape(bsz, s, SSD_GROUPS, SSD_INNER // SSD_GROUPS)
    y = y * lax.rsqrt(jnp.mean(jnp.square(y), axis=-1, keepdims=True) + RMS_EPS)
    y_ssd = (y.reshape(bsz, s, SSD_INNER) * ssd_norm_g).astype(h.dtype)
    q = q.reshape(bsz, s, ATT_HEADS, ATT_HEAD_DIM)
    k = k.reshape(bsz, s, ATT_HEADS, ATT_HEAD_DIM)
    v = v.reshape(bsz, s, ATT_HEADS, ATT_HEAD_DIM)
    log_f = jax.nn.log_sigmoid(f_raw.astype(jnp.float32))
    y_att = _forgetting_attention(q, k, v, log_f).reshape(bsz, s, ATT_INNER)
    merged = jnp.concatenate([y_ssd, y_att.astype(h.dtype)], axis=-1)
    return jnp.einsum('bse,ed->bsd', merged, w_out)

def _hier_moe(h, rg_w, rg_b, re_w, re_b, w_gate, w_up, w_down):
    bsz, s, d = h.shape
    hf = h.reshape(bsz * s, d)
    g_logits = (hf @ rg_w + rg_b).astype(jnp.float32)
    g_val, g_idx = lax.top_k(jax.nn.softmax(g_logits, axis=-1), 1)
    g_val, g_idx = g_val[:, 0], g_idx[:, 0]
    e_all = (jnp.einsum('td,gde->tge', hf, re_w) + re_b).astype(jnp.float32)
    e_logits = jnp.take_along_axis(e_all, g_idx[:, None, None], axis=1)[:, 0]
    e_val, e_idx = lax.top_k(jax.nn.softmax(e_logits, axis=-1), TOP_K)
    e_val = e_val / jnp.sum(e_val, axis=-1, keepdims=True)
    weights = g_val[:, None] * e_val
    expert_id = g_idx[:, None] * EXPERTS_PER_GROUP + e_idx
    combine = jnp.sum(jax.nn.one_hot(expert_id, N_EXPERTS, dtype=jnp.float32) * weights[..., None], axis=1)
    out = jnp.zeros((bsz * s, d), jnp.float32)
    for e in range(N_EXPERTS):
        act = jax.nn.silu(hf @ w_gate[e]) * (hf @ w_up[e])
        out = out + combine[:, e:e + 1] * (act @ w_down[e]).astype(jnp.float32)
    return out.astype(h.dtype).reshape(bsz, s, d)

def first_inputs(seed: int = 0) -> dict:
    key = jax.random.key(seed)
    ks = jax.random.split(key, 20)
    f32 = jnp.float32
    x = jax.random.normal(ks[0], (BATCH, SEQ, D_MODEL), f32)
    col_scale = np.concatenate([
        np.ones(SSD_INNER + SSD_CONV_DIM), np.full(SSD_HEADS, 0.1),
        np.ones(2 * ATT_INNER), np.full(ATT_INNER, DEEPNORM_BETA), np.full(ATT_HEADS, 0.1)]).astype(np.float32)
    w_in = jax.random.normal(ks[1], (DEPTH, D_MODEL, D_IN_PROJ), f32) * (D_MODEL ** -0.5) * jnp.asarray(col_scale)
    b_in = 0.01 * jax.random.normal(ks[2], (DEPTH, D_IN_PROJ), f32)
    dt0 = jnp.exp(jax.random.uniform(ks[3], (DEPTH, SSD_HEADS), f32, np.log(1e-3), np.log(1e-1)))
    dt_bias = dt0 + jnp.log(-jnp.expm1(-dt0))
    off_dt = SSD_INNER + SSD_CONV_DIM
    b_in = b_in.at[:, off_dt:off_dt + SSD_HEADS].set(dt_bias)
    f_bias = jax.random.uniform(ks[4], (DEPTH, ATT_HEADS), f32, 1.0, 5.0)
    b_in = b_in.at[:, D_IN_PROJ - ATT_HEADS:].set(f_bias)
    conv_w = jax.random.normal(ks[5], (DEPTH, CONV_WIDTH, SSD_CONV_DIM), f32) * (CONV_WIDTH ** -0.5)
    conv_b = 0.01 * jax.random.normal(ks[6], (DEPTH, SSD_CONV_DIM), f32)
    a_log = jnp.log(jax.random.uniform(ks[7], (DEPTH, SSD_HEADS), f32, 1.0, 16.0))
    d_skip = 1.0 + 0.1 * jax.random.normal(ks[8], (DEPTH, SSD_HEADS), f32)
    ssd_norm_g = 1.0 + 0.05 * jax.random.normal(ks[9], (DEPTH, SSD_INNER), f32)
    w_out = jax.random.normal(ks[10], (DEPTH, D_MIX, D_MODEL), f32) * (D_MIX ** -0.5) * DEEPNORM_BETA
    ln1_g = 1.0 + 0.05 * jax.random.normal(ks[11], (DEPTH, D_MODEL), f32)
    ln1_b = 0.02 * jax.random.normal(ks[12], (DEPTH, D_MODEL), f32)
    router_group_w = jax.random.normal(ks[13], (DEPTH, D_MODEL, N_EXPERT_GROUPS), f32) * (D_MODEL ** -0.5)
    router_group_b = 0.01 * jax.random.normal(ks[14], (DEPTH, N_EXPERT_GROUPS), f32)
    router_expert_w = jax.random.normal(ks[15], (DEPTH, N_EXPERT_GROUPS, D_MODEL, EXPERTS_PER_GROUP), f32) * (D_MODEL ** -0.5)
    router_expert_b = 0.01 * jax.random.normal(ks[16], (DEPTH, N_EXPERT_GROUPS, EXPERTS_PER_GROUP), f32)
    kw = jax.random.split(ks[17], 3)
    w_gate = jax.random.normal(kw[0], (DEPTH, N_EXPERTS, D_MODEL, D_FF_EXPERT), f32) * (D_MODEL ** -0.5)
    w_up = jax.random.normal(kw[1], (DEPTH, N_EXPERTS, D_MODEL, D_FF_EXPERT), f32) * (D_MODEL ** -0.5)
    w_down = jax.random.normal(kw[2], (DEPTH, N_EXPERTS, D_FF_EXPERT, D_MODEL), f32) * (D_FF_EXPERT ** -0.5) * DEEPNORM_BETA
    ln2_g = 1.0 + 0.05 * jax.random.normal(ks[18], (DEPTH, D_MODEL), f32)
    ln2_b = 0.02 * jax.random.normal(ks[19], (DEPTH, D_MODEL), f32)
    return {"x": x, "w_in": w_in, "b_in": b_in, "conv_w": conv_w, "conv_b": conv_b,
            "a_log": a_log, "d_skip": d_skip, "ssd_norm_g": ssd_norm_g, "w_out": w_out,
            "ln1_g": ln1_g, "ln1_b": ln1_b, "router_group_w": router_group_w,
            "router_group_b": router_group_b, "router_expert_w": router_expert_w,
            "router_expert_b": router_expert_b, "w_gate": w_gate, "w_up": w_up,
            "w_down": w_down, "ln2_g": ln2_g, "ln2_b": ln2_b}

def first_block(x, w_in, b_in, conv_w, conv_b, a_log, d_skip, ssd_norm_g, w_out,
              ln1_g, ln1_b, router_group_w, router_group_b, router_expert_w,
              router_expert_b, w_gate, w_up, w_down, ln2_g, ln2_b):
    h = x
    for l in range(DEPTH):
        mix = _hybrid_mixer(h, w_in[l], b_in[l], conv_w[l], conv_b[l], a_log[l],
                            d_skip[l], ssd_norm_g[l], w_out[l])
        h = _layer_norm(DEEPNORM_ALPHA * h + mix, ln1_g[l], ln1_b[l])
        ffn = _hier_moe(h, router_group_w[l], router_group_b[l], router_expert_w[l],
                        router_expert_b[l], w_gate[l], w_up[l], w_down[l])
        h = _layer_norm(DEEPNORM_ALPHA * h + ffn, ln2_g[l], ln2_b[l])
    return h


DEPTH_2 = 2

GRID_W = 64
CTX_LEN = 256
HEAD_DIM = 64
ATTN_SCALE = HEAD_DIM ** -0.5
CONV_A_CH = D_MODEL // 2
CONV_A_WIDTH = 31
CONV_B_CH = D_MODEL // 2
CONV_B_WIDTH = 3
CONV_SPLITS = [CONV_A_CH, 2 * CONV_A_CH, 2 * CONV_A_CH + CONV_B_CH, 2 * CONV_A_CH + 2 * CONV_B_CH]
CONV_IN_COLS = 2 * CONV_A_CH + 3 * CONV_B_CH
CONV_OUT_ROWS = CONV_A_CH + CONV_B_CH
GQA_Q_HEADS = (D_MODEL // 2) // HEAD_DIM
GQA_KV_HEADS = GQA_Q_HEADS // 4
NA_HEADS = (D_MODEL // 2) // HEAD_DIM
NA_WIN_ROWS = 8
NA_WIN_COLS = 16
ROPE_THETA = 10000.0
ROPE_AXIS_DIM = HEAD_DIM // 2
Q_COLS_C = GQA_Q_HEADS * HEAD_DIM
KV_COLS_C = GQA_KV_HEADS * HEAD_DIM
COLS_D = NA_HEADS * HEAD_DIM
ATTN_SPLITS = [Q_COLS_C, Q_COLS_C + KV_COLS_C, Q_COLS_C + 2 * KV_COLS_C,
               Q_COLS_C + 2 * KV_COLS_C + COLS_D, Q_COLS_C + 2 * KV_COLS_C + 2 * COLS_D]
ATTN_IN_COLS = Q_COLS_C + 2 * KV_COLS_C + 3 * COLS_D
ATTN_OUT_ROWS = Q_COLS_C + COLS_D
N_GROUPS = 4
EXPERTS_PER_GROUP_2 = 8
N_EXPERTS_2 = N_GROUPS * EXPERTS_PER_GROUP_2
TOP_K_INNER = 2
EXPERT_HIDDEN = D_MODEL // 2
DISPATCH_BLOCK = 128
DEEPNORM_ALPHA_2 = (2 * DEPTH_2) ** 0.25
DEEPNORM_BETA_2 = (8 * DEPTH_2) ** -0.25
N_EVEN = (DEPTH_2 + 1) // 2
N_ODD = DEPTH_2 // 2
RMS_EPS_2 = 1e-6


def layer_norm(x, g, b):
    xf = x.astype(jnp.float32)
    mu = jnp.mean(xf, axis=-1, keepdims=True)
    var = jnp.mean(jnp.square(xf - mu), axis=-1, keepdims=True)
    return ((xf - mu) * lax.rsqrt(var + LN_EPS) * g + b).astype(x.dtype)

def rms_norm(x, g):
    xf = x.astype(jnp.float32)
    return (xf * lax.rsqrt(jnp.mean(xf * xf, axis=-1, keepdims=True) + RMS_EPS_2) * g).astype(x.dtype)

def ada_split(cond, w, b):
    return jnp.split(jax.nn.silu(cond) @ w + b, 6, axis=-1)

def depthwise_conv(h, w):
    k = w.shape[0]
    return lax.conv_general_dilated(h, w[:, None, :].astype(h.dtype), (1,), [(k // 2, k // 2)],
                                    dimension_numbers=('NWC', 'WIO', 'NWC'),
                                    feature_group_count=h.shape[-1])

def split_heads(z, n):
    b, l, _ = z.shape
    return z.reshape(b, l, n, HEAD_DIM).transpose(0, 2, 1, 3)

def merge_heads(o):
    b, n, l, d = o.shape
    return o.transpose(0, 2, 1, 3).reshape(b, l, n * d)

def axial_rope_tables(n_tokens):
    t = jnp.arange(n_tokens)
    row = (t // GRID_W).astype(jnp.float32)
    col = (t % GRID_W).astype(jnp.float32)
    inv = ROPE_THETA ** (-jnp.arange(0, ROPE_AXIS_DIM, 2, dtype=jnp.float32) / ROPE_AXIS_DIM)
    ar = row[:, None] * inv
    ac = col[:, None] * inv
    return jnp.cos(ar), jnp.sin(ar), jnp.cos(ac), jnp.sin(ac)

def rotate(x, cos, sin):
    x1, x2 = jnp.split(x, 2, axis=-1)
    return jnp.concatenate([x1 * cos - x2 * sin, x1 * sin + x2 * cos], axis=-1)

def apply_axial_rope(x, tables):
    cr, sr, cc, sc = [t.astype(x.dtype) for t in tables]
    xr, xc = jnp.split(x, 2, axis=-1)
    return jnp.concatenate([rotate(xr, cr, sr), rotate(xc, cc, sc)], axis=-1)

def softmax_attention(q, k, v):
    s = jnp.einsum('bkgqd,bksd->bkgqs', q, k, preferred_element_type=jnp.float32) * ATTN_SCALE
    p = jax.nn.softmax(s, axis=-1).astype(v.dtype)
    return jnp.einsum('bkgqs,bksd->bkgqd', p, v)

def gqa_latent(q, k_all, v_all):
    b, hk, g, s, d = q.shape
    nb = s // Q_BLOCK
    qb = jnp.moveaxis(q.reshape(b, hk, g, nb, Q_BLOCK, d), 3, 0)
    o = lax.map(lambda qi: softmax_attention(qi, k_all, v_all), qb)
    return jnp.moveaxis(o, 0, 3).reshape(b, hk * g, s, d)

def neighbourhood_latent(q, k, v, k_ctx, v_ctx, rel_bias):
    b, h, s, d = q.shape
    rows = s // GRID_W
    kr = min(NA_WIN_ROWS, rows)
    n_ctx = k_ctx.shape[2]
    qg = jnp.moveaxis(q.reshape(b, h, rows, GRID_W, d), 2, 0)
    kg = k.reshape(b, h, rows, GRID_W, d)
    vg = v.reshape(b, h, rows, GRID_W, d)
    qcol = jnp.arange(GRID_W)
    cstart = jnp.clip(qcol - NA_WIN_COLS // 2, 0, GRID_W - NA_WIN_COLS)
    in_win = (qcol[None, :] >= cstart[:, None]) & (qcol[None, :] < cstart[:, None] + NA_WIN_COLS)
    col_idx = jnp.clip(qcol[None, :] - qcol[:, None] + NA_WIN_COLS - 1, 0, 2 * NA_WIN_COLS - 2)
    bias_cols = rel_bias[:, :, col_idx]

    def one_row(args):
        qr, r = args
        rs = jnp.clip(r - kr // 2, 0, rows - kr)
        kb = lax.dynamic_slice_in_dim(kg, rs, kr, axis=2)
        vb = lax.dynamic_slice_in_dim(vg, rs, kr, axis=2)
        s_lat = jnp.einsum('bhqd,bhrkd->bhqrk', qr, kb, preferred_element_type=jnp.float32) * ATTN_SCALE
        row_idx = rs + jnp.arange(kr) - r + NA_WIN_ROWS - 1
        bias = jnp.take(bias_cols, row_idx, axis=1).transpose(0, 2, 1, 3).astype(jnp.float32)
        s_lat = jnp.where(in_win[:, None, :], s_lat + bias, -jnp.inf).reshape(b, h, GRID_W, kr * GRID_W)
        s_ctx = jnp.einsum('bhqd,bhcd->bhqc', qr, k_ctx, preferred_element_type=jnp.float32) * ATTN_SCALE
        p = jax.nn.softmax(jnp.concatenate([s_ctx, s_lat], axis=-1), axis=-1).astype(v.dtype)
        p_ctx = p[..., :n_ctx]
        p_lat = p[..., n_ctx:].reshape(b, h, GRID_W, kr, GRID_W)
        return (jnp.einsum('bhqc,bhcd->bhqd', p_ctx, v_ctx)
                + jnp.einsum('bhqrk,bhrkd->bhqd', p_lat, vb))

    o = lax.map(one_row, (qg, jnp.arange(rows)))
    return jnp.moveaxis(o, 0, 2).reshape(b, h, s, d)

def conv_mixers(h, w_in, w_out, a_dw_w, a_dw_b, a_ln_g, a_ln_b, b_dw_w):
    z = h @ w_in
    a_val, a_gate, b_gate, c_gate, b_val = jnp.split(z, CONV_SPLITS, axis=-1)
    ya = a_val * jax.nn.sigmoid(a_gate)
    ya = depthwise_conv(ya, a_dw_w) + a_dw_b
    ya = jax.nn.silu(layer_norm(ya, a_ln_g, a_ln_b))
    yb = b_gate * depthwise_conv(c_gate * b_val, b_dw_w)
    return jnp.concatenate([ya, yb], axis=-1) @ w_out

def attn_mixers(h_lat, h_ctx, w_in, w_out, q_g, k_g, rel_bias, with_ctx_out):
    b, s, _ = h_lat.shape
    n_ctx = h_ctx.shape[1]
    group = GQA_Q_HEADS // GQA_KV_HEADS
    ql_c, kl_c, vl_c, ql_d, kl_d, vl_d = jnp.split(h_lat @ w_in, ATTN_SPLITS, axis=-1)
    qc_c, kc_c, vc_c, qc_d, kc_d, vc_d = jnp.split(h_ctx @ w_in, ATTN_SPLITS, axis=-1)
    tables = axial_rope_tables(s)
    q_lat = apply_axial_rope(rms_norm(split_heads(ql_c, GQA_Q_HEADS), q_g), tables)
    q_lat = q_lat.reshape(b, GQA_KV_HEADS, group, s, HEAD_DIM)
    k_lat = apply_axial_rope(rms_norm(split_heads(kl_c, GQA_KV_HEADS), k_g), tables)
    v_lat = split_heads(vl_c, GQA_KV_HEADS)
    k_ctx = rms_norm(split_heads(kc_c, GQA_KV_HEADS), k_g)
    v_ctx = split_heads(vc_c, GQA_KV_HEADS)
    o_c = gqa_latent(q_lat, jnp.concatenate([k_ctx, k_lat], axis=2), jnp.concatenate([v_ctx, v_lat], axis=2))
    kd_ctx = split_heads(kc_d, NA_HEADS)
    vd_ctx = split_heads(vc_d, NA_HEADS)
    o_d = neighbourhood_latent(split_heads(ql_d, NA_HEADS), split_heads(kl_d, NA_HEADS),
                               split_heads(vl_d, NA_HEADS), kd_ctx, vd_ctx, rel_bias)
    y_lat = jnp.concatenate([merge_heads(o_c), merge_heads(o_d)], axis=-1) @ w_out
    if not with_ctx_out:
        return y_lat, None
    q_ctx = rms_norm(split_heads(qc_c, GQA_Q_HEADS), q_g).reshape(b, GQA_KV_HEADS, group, n_ctx, HEAD_DIM)
    oc_c = softmax_attention(q_ctx, k_ctx, v_ctx).reshape(b, GQA_Q_HEADS, n_ctx, HEAD_DIM)
    oc_d = softmax_attention(split_heads(qc_d, NA_HEADS)[:, :, None], kd_ctx, vd_ctx)[:, :, 0]
    y_ctx = jnp.concatenate([merge_heads(oc_c), merge_heads(oc_d)], axis=-1) @ w_out
    return y_lat, y_ctx

def grouped_experts(x, expert, gate, w_gate, w_up, w_down):
    n, d = x.shape
    k = expert.shape[1]
    m = n * k
    flat_e = expert.reshape(m)
    flat_tok = jnp.arange(m) // k
    flat_w = gate.reshape(m)
    order = jnp.argsort(flat_e)
    se = flat_e[order]
    counts = jnp.bincount(flat_e, length=N_EXPERTS_2)
    padded = (counts + DISPATCH_BLOCK - 1) // DISPATCH_BLOCK * DISPATCH_BLOCK
    pad_end = jnp.cumsum(padded)
    pad_start = pad_end - padded
    start = jnp.cumsum(counts) - counts
    dest = pad_start[se] + jnp.arange(m) - start[se]
    n_blocks = -(-m // DISPATCH_BLOCK) + N_EXPERTS_2
    cap = n_blocks * DISPATCH_BLOCK
    slot_tok = jnp.full((cap,), n, jnp.int32).at[dest].set(flat_tok[order])
    slot_w = jnp.zeros((cap,), x.dtype).at[dest].set(flat_w[order])
    xs = jnp.concatenate([x, jnp.zeros((1, d), x.dtype)], axis=0)[slot_tok].reshape(n_blocks, DISPATCH_BLOCK, d)
    block_e = jnp.minimum(jnp.searchsorted(pad_end, jnp.arange(n_blocks) * DISPATCH_BLOCK, side='right'),
                          N_EXPERTS_2 - 1)

    def run(args):
        xb, e = args
        return (jax.nn.silu(xb @ w_gate[e]) * (xb @ w_up[e])) @ w_down[e]

    ys = lax.map(run, (xs, block_e)).reshape(cap, d)
    return jnp.zeros((n + 1, d), x.dtype).at[slot_tok].add(ys * slot_w[:, None])[:n]

def hier_moe(tokens, w1, b1, w2, b2, w_gate, w_up, w_down):
    n = tokens.shape[0]
    p1 = jax.nn.softmax((tokens @ w1 + b1).astype(jnp.float32), axis=-1)
    p_grp, grp = lax.top_k(p1, 1)
    lg2 = (tokens @ w2 + b2).astype(jnp.float32).reshape(n, N_GROUPS, EXPERTS_PER_GROUP_2)
    lg2 = jnp.take_along_axis(lg2, grp[:, :, None], axis=1)[:, 0]
    top_val, top_idx = lax.top_k(lg2, TOP_K_INNER)
    gate = p_grp * jax.nn.softmax(top_val, axis=-1)
    expert = grp * EXPERTS_PER_GROUP_2 + top_idx
    return grouped_experts(tokens, expert, gate.astype(tokens.dtype), w_gate, w_up, w_down)

def second_inputs(seed: int = 0) -> dict:
    key = jax.random.key(seed)
    keys = jax.random.split(key, 32)
    counter = [0]
    D = D_MODEL

    def nrm(shape, scale):
        kk = keys[counter[0]]
        counter[0] += 1
        return jax.random.normal(kk, shape, jnp.float32) * scale

    return {
        'x': nrm((BATCH, SEQ, D), 1.0),
        'c': nrm((BATCH, D), 1.0),
        'ctx': nrm((BATCH, CTX_LEN, D), 1.0),
        'c_ctx': nrm((D,), 1.0),
        'ada_w': nrm((DEPTH_2, D, 6 * D), 0.5 * D ** -0.5),
        'ada_b': nrm((DEPTH_2, 6 * D), 0.02),
        'ln1_g': 1.0 + nrm((DEPTH_2, D), 0.02),
        'ln1_b': nrm((DEPTH_2, D), 0.02),
        'ln2_g': 1.0 + nrm((DEPTH_2, D), 0.02),
        'ln2_b': nrm((DEPTH_2, D), 0.02),
        'conv_w_in': nrm((N_EVEN, D, CONV_IN_COLS), D ** -0.5),
        'conv_w_out': nrm((N_EVEN, CONV_OUT_ROWS, D), DEEPNORM_BETA_2 * CONV_OUT_ROWS ** -0.5),
        'conv_a_dw_w': nrm((N_EVEN, CONV_A_WIDTH, CONV_A_CH), CONV_A_WIDTH ** -0.5),
        'conv_a_dw_b': nrm((N_EVEN, CONV_A_CH), 0.02),
        'conv_a_ln_g': 1.0 + nrm((N_EVEN, CONV_A_CH), 0.02),
        'conv_a_ln_b': nrm((N_EVEN, CONV_A_CH), 0.02),
        'conv_b_dw_w': nrm((N_EVEN, CONV_B_WIDTH, CONV_B_CH), CONV_B_WIDTH ** -0.5),
        'attn_w_in': nrm((N_ODD, D, ATTN_IN_COLS), D ** -0.5),
        'attn_w_out': nrm((N_ODD, ATTN_OUT_ROWS, D), DEEPNORM_BETA_2 * ATTN_OUT_ROWS ** -0.5),
        'q_norm_g': 1.0 + nrm((N_ODD, HEAD_DIM), 0.02),
        'k_norm_g': 1.0 + nrm((N_ODD, HEAD_DIM), 0.02),
        'na_rel_bias': nrm((N_ODD, NA_HEADS, 2 * NA_WIN_ROWS - 1, 2 * NA_WIN_COLS - 1), 0.05),
        'router_w1': nrm((DEPTH_2, D, N_GROUPS), D ** -0.5),
        'router_b1': nrm((DEPTH_2, N_GROUPS), 0.01),
        'router_w2': nrm((DEPTH_2, D, N_EXPERTS_2), D ** -0.5),
        'router_b2': nrm((DEPTH_2, N_EXPERTS_2), 0.01),
        'expert_w_gate': nrm((DEPTH_2, N_EXPERTS_2, D, EXPERT_HIDDEN), D ** -0.5),
        'expert_w_up': nrm((DEPTH_2, N_EXPERTS_2, D, EXPERT_HIDDEN), D ** -0.5),
        'expert_w_down': nrm((DEPTH_2, N_EXPERTS_2, EXPERT_HIDDEN, D), DEEPNORM_BETA_2 * EXPERT_HIDDEN ** -0.5),
    }

def second_block(x, c, ctx, c_ctx, ada_w, ada_b, ln1_g, ln1_b, ln2_g, ln2_b,
              conv_w_in, conv_w_out, conv_a_dw_w, conv_a_dw_b, conv_a_ln_g, conv_a_ln_b, conv_b_dw_w,
              attn_w_in, attn_w_out, q_norm_g, k_norm_g, na_rel_bias,
              router_w1, router_b1, router_w2, router_b2, expert_w_gate, expert_w_up, expert_w_down):
    d = x.shape[-1]
    x_lat, x_ctx = x, ctx
    for i in range(DEPTH_2):
        last = i == DEPTH_2 - 1
        odd = i % 2 == 1
        j = i // 2
        sh1, sc1, g1, sh2, sc2, g2 = [m[:, None, :] for m in ada_split(c, ada_w[i], ada_b[i])]
        csh1, csc1, cg1, csh2, csc2, cg2 = ada_split(c_ctx, ada_w[i], ada_b[i])
        moe_w = (router_w1[i], router_b1[i], router_w2[i], router_b2[i],
                 expert_w_gate[i], expert_w_up[i], expert_w_down[i])
        h_lat = x_lat * (1.0 + sc1) + sh1
        h_ctx = x_ctx * (1.0 + csc1) + csh1 if (odd or not last) else None
        if odd:
            y_lat, y_ctx = attn_mixers(h_lat, h_ctx, attn_w_in[j], attn_w_out[j], q_norm_g[j], k_norm_g[j],
                                       na_rel_bias[j], not last)
        else:
            conv_w = (conv_w_in[j], conv_w_out[j], conv_a_dw_w[j], conv_a_dw_b[j],
                      conv_a_ln_g[j], conv_a_ln_b[j], conv_b_dw_w[j])
            y_lat = conv_mixers(h_lat, *conv_w)
            y_ctx = None if last else conv_mixers(h_ctx, *conv_w)
        x_lat = layer_norm(DEEPNORM_ALPHA_2 * x_lat + g1 * y_lat, ln1_g[i], ln1_b[i])
        h_lat = x_lat * (1.0 + sc2) + sh2
        if last:
            y = hier_moe(h_lat.reshape(-1, d), *moe_w).reshape(x_lat.shape)
            x_lat = layer_norm(DEEPNORM_ALPHA_2 * x_lat + g2 * y, ln2_g[i], ln2_b[i])
        else:
            x_ctx = layer_norm(DEEPNORM_ALPHA_2 * x_ctx + cg1 * y_ctx, ln1_g[i], ln1_b[i])
            h_ctx = x_ctx * (1.0 + csc2) + csh2
            n_lat = h_lat.shape[0] * h_lat.shape[1]
            y = hier_moe(jnp.concatenate([h_lat.reshape(-1, d), h_ctx.reshape(-1, d)], axis=0), *moe_w)
            x_lat = layer_norm(DEEPNORM_ALPHA_2 * x_lat + g2 * y[:n_lat].reshape(x_lat.shape), ln2_g[i], ln2_b[i])
            x_ctx = layer_norm(DEEPNORM_ALPHA_2 * x_ctx + cg2 * y[n_lat:].reshape(x_ctx.shape), ln2_g[i], ln2_b[i])
    return x_lat


def setup_inputs(seed=0):
    out = dict(first_inputs(seed))
    for name, value in second_inputs(seed + 1).items():
        if name != "x":
            out[name + "_2"] = value
    return out


def reference(
    x, w_in, b_in, conv_w, conv_b, a_log, d_skip, ssd_norm_g, w_out, ln1_g, ln1_b,
    router_group_w, router_group_b, router_expert_w, router_expert_b, w_gate, w_up, w_down,
    ln2_g, ln2_b, c_2, ctx_2, c_ctx_2, ada_w_2, ada_b_2, ln1_g_2, ln1_b_2, ln2_g_2, ln2_b_2,
    conv_w_in_2, conv_w_out_2, conv_a_dw_w_2, conv_a_dw_b_2, conv_a_ln_g_2, conv_a_ln_b_2,
    conv_b_dw_w_2, attn_w_in_2, attn_w_out_2, q_norm_g_2, k_norm_g_2, na_rel_bias_2,
    router_w1_2, router_b1_2, router_w2_2, router_b2_2, expert_w_gate_2, expert_w_up_2,
    expert_w_down_2,
):
    x = first_block(
        x, w_in, b_in, conv_w, conv_b, a_log, d_skip, ssd_norm_g, w_out, ln1_g, ln1_b,
        router_group_w, router_group_b, router_expert_w, router_expert_b, w_gate, w_up, w_down,
        ln2_g, ln2_b,
    )
    return second_block(
        x, c_2, ctx_2, c_ctx_2, ada_w_2, ada_b_2, ln1_g_2, ln1_b_2, ln2_g_2, ln2_b_2,
        conv_w_in_2, conv_w_out_2, conv_a_dw_w_2, conv_a_dw_b_2, conv_a_ln_g_2, conv_a_ln_b_2,
        conv_b_dw_w_2, attn_w_in_2, attn_w_out_2, q_norm_g_2, k_norm_g_2, na_rel_bias_2,
        router_w1_2, router_b1_2, router_w2_2, router_b2_2, expert_w_gate_2, expert_w_up_2,
        expert_w_down_2,
    )


_drawn_inputs = setup_inputs


def setup_inputs(seed=0):
    import zlib

    import numpy as np

    out = dict(_drawn_inputs(seed))
    spreads = {}
    factors = {'conv_b': 6.637,
     'router_group_b': 6.862,
     'router_expert_b': 21.654,
     'ln2_b': 2.736,
     'ctx_2': 7.434,
     'c_ctx_2': 3.051,
     'ada_b_2': 4.689,
     'conv_a_dw_b_2': 8.0,
     'conv_a_ln_g_2': 37.83,
     'conv_a_ln_b_2': 40.591,
     'q_norm_g_2': 35.79,
     'k_norm_g_2': 31.633,
     'na_rel_bias_2': 64.0,
     'router_b1_2': 42.05,
     'router_b2_2': 24.516}
    for name, (base, spread) in spreads.items():
        noise = np.random.default_rng([zlib.crc32(name.encode()), seed]).standard_normal(out[name].shape)
        drawn = base * np.exp(spread * noise) if base else spread * noise
        out[name] = __import__('jax').numpy.asarray(drawn.astype(out[name].dtype))
    for name, factor in factors.items():
        out[name] = (out[name] * factor).astype(out[name].dtype)
    return out
```

```python
from contextlib import ExitStack

import numpy as np

import concourse.bass as bass
from concourse import mybir

F32 = mybir.dt.float32
I32 = mybir.dt.int32
ALU = mybir.AluOpType
ACT = mybir.ActivationFunctionType
AX = mybir.AxisListType

P = 128
D = 1024
KT = D // P
SEQ, CTX = 512, 256
TL, TC = SEQ // P, CTX // P
TA = TL + TC
NTOK = SEQ + CTX
HEADS, HD = 8, 64
FF = 512
CONV_A_W = 31
PAD = CONV_A_W // 2
CTX_AT = SEQ + PAD
SPAN = CTX_AT + CTX
PADDED = SPAN + 2 * PAD
NEG = -1.0e30
ATT_SCALE = HD ** -0.5
ALPHA_1 = 2.0 ** 0.25
ALPHA_2 = 4.0 ** 0.25
EPS = 1e-5
EPS_RMS = 1e-6
RING = 4
SLOT = 4096

C_ID, C_TRI, C_TRIS, C_ONE, C_MASK = 0, 128, 256, 384, 512
C_IOTA = 640
C_EPS = 688
C_COUNT = 690

FC = {}
_at = 0
for _n, _w in (("b_in", 24), ("conv_w", 32), ("conv_b", 8), ("d_skip", 4), ("norm_g", 4), ("a_dw_w", 4 * CONV_A_W),
               ("a_dw_b", 4), ("a_ln_g", 4), ("a_ln_b", 4), ("b_dw_w", 12), ("cond", 16)):
    FC[_n] = _at
    _at += _w
FC_COUNT = _at
RC = {}
_at = 0
for _n, _w in (("dt_f_bias", 16), ("a_log", 8), ("router1_b", 20), ("router2_b", 72), ("q_g", 64), ("k_g", 64)):
    RC[_n] = _at
    _at += _w
RC_COUNT = _at


class Moe:

    def __init__(self, tiles, groups, per_group):
        self.T, self.G, self.EP = tiles, groups, per_group
        self.E = groups * per_group
        self.blocks = -(-(self.E + (tiles * P * 2 - self.E) // P) // 4) * 4


def spread(ap, axis, n):
    wide = ap.unsqueeze(axis)
    shape = list(wide.shape)
    shape[axis] = n
    return wide.broadcast_to(shape)


def build(nc, d):
    es = ExitStack()
    with es:
        def sb(name, shape, dt=F32):
            return es.enter_context(nc.sbuf_tensor(name, shape, dt))

        def sem(name):
            return es.enter_context(nc.semaphore(name))

        w_ring = sb("w_ring", [P, RING, SLOT])
        x_tok = sb("x_tok", [P, TA, D])
        x_feat = sb("x_feat", [P, KT, NTOK])
        cst = sb("cst", [P, C_COUNT])
        fcol = sb("fcol", [P, FC_COUNT])
        frow = sb("frow", [P, RC_COUNT])
        ARENA = 23010
        arena = sb("arena", [P, ARENA])
        ps = es.enter_context(nc.psum_tensor("ps", [P, 8 * 512], F32))

        def bank(i, n=512):
            return ps[:, 512 * i:512 * i + n]

        def region(at, *shape):
            n = int(np.prod(shape))
            assert at + n <= ARENA, (at, n, ARENA)
            flat = arena[:, at:at + n]
            if len(shape) == 1:
                return flat
            names = "abcd"[:len(shape)]
            return flat.rearrange(f"p ({' '.join(names)}) -> p {' '.join(names)}",
                                  **{k: v for k, v in zip(names[1:], shape[1:])})

        ident = cst[:, C_ID:C_ID + P]
        tri = cst[:, C_TRI:C_TRI + P]
        tri_strict = cst[:, C_TRIS:C_TRIS + P]
        ones = cst[:, C_ONE:C_ONE + P]
        causal = cst[:, C_MASK:C_MASK + P]

        stage_passed = sem("stage_passed")
        w_landed = [sem(f"w_landed{i}") for i in range(RING)]
        w_free = sem("w_free")
        passed = {"pe": [], "act": [], "dve": [], "pool": []}

        def stage(eng, who, name):
            passed[who].append(name)
            eng.drain().then_inc(stage_passed, 1)
            eng.wait_ge(stage_passed, 4 * len(passed[who]))

        class Chunks:
            def __init__(self, n=0):
                self.n = n

            def take(self):
                n = self.n
                self.n += 1
                return n

        def chunk_view(slot, n, k=KT):
            return w_ring[:, slot, 0:k * n].rearrange("p (k n) -> p k n", n=n)

        def load_columns(sp, chunks, w, c0, n):
            c = chunks.take()
            if c >= RING:
                sp.wait_ge(w_free, c - RING + 1)
            sp.dma_start(chunk_view(c % RING, n), w[:, c0:c0 + n].rearrange("(k p) n -> p k n", p=P)
                         ).then_inc(w_landed[c % RING], 16)

        def await_chunk(pe, c):
            pe.wait_ge(w_landed[c % RING], 16 * (c // RING + 1))

        params_here = sem("params_here")
        params = {"out1": 1, "out2": 2, "h2": 3, "out3": 4, "h3": 5}

        summed = {}

        start = {}

        def new_sems(name, *parts):
            for p in parts:
                summed[f"{name}.{p}"] = sem(f"{name}_{p}")
                start[f"{name}.{p}"] = 0

        def count(key, value):
            return summed[key], value + start[key]

        PAIRS = 4

        def pair(j, n=NTOK):
            at = (j % PAIRS) * 1024
            return ps[:, at:at + n]

        def by_parity(name):
            return lambda j: count(f"{name}.read{j % 2}", j // 2 + 1)

        def linear_pe(pe, name, jobs, chunks, reader):
            c = None
            for j, (first, last, products) in enumerate(jobs):
                if first:
                    c = chunks.take()
                    await_chunk(pe, c)
                if j >= PAIRS:
                    pe.wait_ge(*reader(j - PAIRS))
                mm = products(j, c % RING)
                mm.then_inc(summed[f"{name}.ready"], 1)
                if last:
                    pe.drain().then_inc(w_free, 1)

        def linear_take(eng, name, parity, takes):
            for j, take in enumerate(takes):
                if j % 2 != parity:
                    continue
                eng.wait_ge(*count(f"{name}.ready", j + 1))
                take(j).then_inc(summed[f"{name}.read{parity}"], 1)

        def feature_products(c0, tokens, halves=True, n=512):
            def products(j, slot):
                w = chunk_view(slot, n)
                for t0 in range(0, tokens, 512):
                    t1 = min(t0 + 512, tokens)
                    for k in range(KT):
                        mm = nc.tensor.matmul(pair(j)[:, t0:t1], w[:, k, c0:c0 + P], x_feat[:, k, t0:t1],
                                              start=k == 0, stop=k == KT - 1)
                return mm
            return products

        def token_products(tile, n, bias=None):
            def products(j, slot):
                w = chunk_view(slot, n)
                for k in range(KT):
                    mm = nc.tensor.matmul(pair(j, n), x_feat[:, k, P * tile:P * (tile + 1)], w[:, k, :],
                                          start=k == 0, stop=k == KT - 1 and bias is None)
                if bias is not None:
                    mm = nc.tensor.matmul(pair(j, n), ones[0:1, :], bias, start=False, stop=True)
                return mm
            return products

        def transpose_pe(pe, name, tiles, source=None):
            j = 0
            for t in tiles:
                for half in range(2):
                    if j >= 8:
                        pe.wait_ge(*count(f"{name}.read{j % 2}", (j - 8) // 2 + 1))
                    for q in range(4):
                        k = 4 * half + q
                        src = (source or x_tok)[:, t, P * k:P * (k + 1)]
                        mm = nc.tensor.transpose(bank(j % 8)[:, P * q:P * (q + 1)], src, ident)
                    mm.then_inc(summed[f"{name}.ready"], 1)
                    j += 1

        def transpose_take(eng, name, parity, tiles, dest, scale=None, shift=None):
            j = 0
            for t in tiles:
                for half in range(2):
                    if j % 2 == parity:
                        eng.wait_ge(*count(f"{name}.ready", j + 1))
                        src = bank(j % 8).rearrange("p (q n) -> p q n", q=4)
                        if scale is None:
                            out = dest[:, 4 * half:4 * half + 4, P * t:P * (t + 1)]
                            if parity:
                                ins = nc.scalar.activation(out, src, ACT.Copy)
                            else:
                                ins = nc.vector.tensor_copy(out, src)
                        else:
                            for q in range(4):
                                k = 4 * half + q
                                out = dest[:, k, P * t:P * (t + 1)]
                                sc, sh = scale(t)[:, k:k + 1], shift(t)[:, k:k + 1]
                                if parity:
                                    ins = nc.scalar.activation(out, src[:, q, :], ACT.Identity, bias=sh, scale=sc)
                                else:
                                    ins = nc.vector.tensor_scalar(out, src[:, q, :], sc, sh, ALU.mult, ALU.add)
                        ins.then_inc(summed[f"{name}.read{parity}"], 1)
                    j += 1

        ln_stats = sb("ln_stats", [P, TA, 16])

        def normalise(dve, name, i, t, g, b):
            s = ln_stats[:, t, :]
            x = x_tok[:, t, :]
            for half in range(2):
                nc.vector.bn_stats(s[:, 6 * half:6 * half + 6], x[:, 512 * half:512 * half + 512])
            dve.drain()
            nc.vector.bn_aggr(s[:, 12:14], s[:, 0:12]).then_inc(summed[f"{name}.var"], 1)
            dve.wait_ge(*count(f"{name}.root", i + 1))
            nc.vector.reciprocal(s[:, 15:16], s[:, 14:15])
            dve.drain()
            nc.vector.tensor_scalar(x, x, s[:, 12:13], s[:, 15:16], ALU.subtract, ALU.mult)
            dve.drain()
            nc.vector.tensor_tensor(x, x, g, ALU.mult)
            dve.drain()
            return nc.vector.tensor_tensor(x, x, b, ALU.add)

        def normalise_roots(act, name, tiles):
            for i, t in enumerate(tiles):
                act.wait_ge(*count(f"{name}.var", i + 1))
                nc.scalar.activation(ln_stats[:, t, 14:15], ln_stats[:, t, 13:14], ACT.Sqrt,
                                     bias=cst[:, C_EPS:C_EPS + 1]).then_inc(summed[f"{name}.root"], 1)

        def out_proj_pe(pe, name, tiles, chunks):
            halves = [chunks.take(), chunks.take()]
            for c in halves:
                await_chunk(pe, c)
            for i, t in enumerate(tiles):
                if i >= PAIRS:
                    pe.wait_ge(*count(f"{name}.read", i - PAIRS + 1))
                for half, c in enumerate(halves):
                    for k in range(KT):
                        mm = nc.tensor.matmul(pair(i, D)[:, 512 * half:512 * half + 512],
                                              x_feat[:, k, P * t:P * (t + 1)], chunk_view(c % RING, 512)[:, k, :],
                                              start=k == 0, stop=k == KT - 1)
                mm.then_inc(summed[f"{name}.ready"], 1)
            pe.drain().then_inc(w_free, 2)

        def out_proj_dve(dve, name, tiles, alpha, gate, g, b):
            dve.wait_ge(params_here, params[name])
            for i, t in enumerate(tiles):
                dve.wait_ge(*count(f"{name}.ready", i + 1))
                x = x_tok[:, t, :]
                y = pair(i, 1024)
                if gate is not None:
                    nc.vector.tensor_tensor(y, y, gate(t), ALU.mult)
                    dve.drain()
                nc.vector.scalar_tensor_tensor(x, x, alpha, y, ALU.mult, ALU.add).then_inc(summed[f"{name}.read"], 1)
                dve.drain()
                normalise(dve, name, i, t, g, b)
            dve.drain()

        A_ROWS = 0
        A_TOK = 6 * D
        A_BLK = A_TOK + TA * D
        A_SMALL = A_BLK + 3072
        rows = region(A_ROWS, 6, D)
        h_tok = region(A_TOK, TA, D)
        blk_rows = region(A_TOK, 2, D)
        blk_feat = region(A_TOK + 2 * D, 2, 8, P)
        blk_out = region(A_TOK + 4 * D, 2, D)
        picked = region(A_TOK, 4, D)
        blk_gate = region(A_BLK, 2, FF)
        blk_hid = region(A_BLK + 2 * FF, 2, FF)
        blk_hidT = region(A_BLK + 4 * FF, 2, 4, P)
        slots_i = sb("slots_i", [P, 2, TA], I32)
        gate_w = sb("gate_w", [P, 2, TA])
        expert_of = sb("expert_of", [1, 48], I32)
        used_blocks = sb("used_blocks", [1, 1], I32)

        def moe_counts(m):
            T, n = m.T, m.blocks
            return {"t.ready": 2 * T, "t.read0": T, "t.read1": T, "logits": 1, "exps": 2, "exps_done": 2, "ranks_in": 1,
                    "ranks": 1, "table": 1, "scattered": 32 * T, "rows0": 8 * n + 16, "rows1": 8 * n + 16,
                    "turned": n + 1, "feat": n + 1, "silu": n, "hid": n, "hid_turned": n, "hid_feat": n,
                    "y_copied": n + 1, "out_free": n + 2, "gathered": 32 * T, "both_rows": T,
                    "picked_free": T, "var": T, "root": T}

        def moe_sems(*mixtures):
            at = {}
            for name, m in mixtures:
                for part, total in moe_counts(m).items():
                    if part not in at:
                        at[part] = (sem(f"moe_{part}"), 0)
                    summed[f"{name}.{part}"], start[f"{name}.{part}"] = at[part]
                    at[part] = (at[part][0], at[part][1] + total)
                new_sems(name, "stored")

        def moe_router_pe(pe, name, m, wr):
            n = m.G + m.E
            for t in range(m.T):
                for k in range(KT):
                    mm = nc.tensor.matmul(bank(0)[:, t * n:(t + 1) * n], x_feat[:, k, P * t:P * (t + 1)],
                                          wr[:, k, 0:n], start=k == 0, stop=k == KT - 1)
            mm.then_inc(summed[f"{name}.logits"], 1)
            pe.wait_ge(*count(f"{name}.ranks_in", 1))
            chosen = moe_arrays(m)["both"]
            for t in range(m.T):
                for s in range(t + 1):
                    nc.tensor.matmul(bank(1)[:, t * m.E:(t + 1) * m.E], ones if s < t else tri_strict,
                                     chosen[:, s, :], start=s == 0, stop=s == t)
            for s in range(m.T):
                mm = nc.tensor.matmul(bank(2)[:, 0:m.E], ones, chosen[:, s, :], start=s == 0, stop=s == m.T - 1)
            mm.then_inc(summed[f"{name}.ranks"], 1)

        def moe_arrays(m):
            T, G, E, EP = m.T, m.G, m.E, m.EP
            at = [A_SMALL]

            def arr(*shape):
                r = region(at[0], *shape)
                at[0] += int(np.prod(shape))
                return r
            return {"lg": arr(T, G + E), "gmax": arr(T), "gexp": arr(T, G), "gone": arr(T, G), "el": arr(T, EP),
                    "tmp": arr(T, G, EP), "m1": arr(T), "m2": arr(T), "one1": arr(T, EP), "one2": arr(T, EP),
                    "pg": arr(T), "k": arr(T, 8), "km": arr(T), "all1": arr(T, E), "all2": arr(T, E),
                    "both": arr(T, E), "slot": arr(T, E), "cnt": arr(E), "blocks": arr(E), "sums": arr(2, E),
                    "tab": arr(m.blocks, E), "tabr": arr(48), "sl": arr(2, T), "wr": arr(KT, G + E)}

        def moe_router_act(act, name, m):
            a = moe_arrays(m)
            act.wait_ge(*count(f"{name}.exps", 1))
            nc.scalar.activation(a["gexp"], a["gexp"], ACT.Exp)
            act.drain().then_inc(summed[f"{name}.exps_done"], 1)
            act.wait_ge(*count(f"{name}.exps", 2))
            nc.scalar.activation(a["m2"], a["m2"], ACT.Exp).then_inc(summed[f"{name}.exps_done"], 1)

        def moe_router_dve(dve, name, m, bias):
            T, G, E, EP = m.T, m.G, m.E, m.EP
            a = moe_arrays(m)
            v = nc.vector

            def then(_):
                dve.drain()

            def first_max(x, n, mx, one):
                then(v.tensor_reduce(mx, x, axis=AX.X, op=ALU.max))
                k = a["k"][:, :, 0:n]
                then(v.tensor_tensor(k, x, spread(mx, 2, n), ALU.is_equal))
                then(v.tensor_tensor(one, spread(cst[:, C_IOTA:C_IOTA + n], 1, T), k, ALU.mult))
                then(v.scalar_tensor_tensor(k, k, float(n), one, ALU.mult, ALU.subtract))
                then(v.tensor_reduce(a["km"], k, axis=AX.X, op=ALU.max))
                then(v.tensor_tensor(one, k, spread(a["km"], 2, n), ALU.is_equal))

            dve.wait_ge(*count(f"{name}.logits", 1))
            lg = a["lg"]
            then(v.tensor_tensor(lg, bank(0)[:, 0:T * (G + E)].rearrange("p (t n) -> p t n", t=T),
                                 spread(bias, 1, T), ALU.add))
            glog = lg[:, :, 0:G]
            elog = lg[:, :, G:G + E].rearrange("p t (g e) -> p t g e", g=G)
            first_max(glog, G, a["gmax"], a["gone"])
            v.tensor_tensor(a["gexp"], glog, spread(a["gmax"], 2, G), ALU.subtract)
            dve.drain().then_inc(summed[f"{name}.exps"], 1)
            for t in range(T):
                v.tensor_tensor(a["tmp"][:, t], elog[:, t], spread(a["gone"][:, t, :], 2, EP), ALU.mult)
            dve.drain()
            then(v.tensor_reduce(a["el"], a["tmp"].rearrange("p t g e -> p t e g"), axis=AX.X, op=ALU.add))
            first_max(a["el"], EP, a["m1"], a["one1"])
            then(v.scalar_tensor_tensor(a["el"], a["one1"], NEG, a["el"], ALU.mult, ALU.add))
            first_max(a["el"], EP, a["m2"], a["one2"])
            v.tensor_tensor(a["m2"], a["m2"], a["m1"], ALU.subtract)
            for t in range(T):
                for one, every in (("one1", "all1"), ("one2", "all2")):
                    v.tensor_tensor(a[every][:, t, :].rearrange("p (g e) -> p g e", g=G),
                                    spread(a["gone"][:, t, :], 2, EP), spread(a[one][:, t, :], 1, G), ALU.mult)
            dve.drain().then_inc(summed[f"{name}.exps"], 1)
            v.tensor_tensor(a["both"], a["all1"], a["all2"], ALU.add).then_inc(summed[f"{name}.ranks_in"], 1)
            dve.wait_ge(*count(f"{name}.exps_done", 2))
            then(v.tensor_reduce(a["pg"], a["gexp"], axis=AX.X, op=ALU.add))
            then(v.tensor_scalar(a["m1"], a["m2"], 1.0, None, ALU.add))
            then(v.tensor_tensor(a["pg"], a["pg"], a["m1"], ALU.mult))
            then(v.reciprocal(gate_w[:, 0, 0:T], a["pg"]))
            v.tensor_tensor(gate_w[:, 1, 0:T], gate_w[:, 0, 0:T], a["m2"], ALU.mult)
            dve.wait_ge(*count(f"{name}.ranks", 1))
            then(v.tensor_copy(a["cnt"], bank(2)[:, 0:E]))
            then(v.tensor_scalar(a["blocks"], a["cnt"], 0.0, None, ALU.is_gt))
            for k in range(1, T):
                then(v.scalar_tensor_tensor(a["blocks"], a["cnt"], float(P * k), a["blocks"], ALU.is_gt, ALU.add))
            src = a["blocks"]
            step, side = 1, 0
            while step < E:
                dst = a["sums"][:, side]
                v.tensor_copy(dst[:, 0:step], src[:, 0:step])
                then(v.tensor_tensor(dst[:, step:E], src[:, step:E], src[:, 0:E - step], ALU.add))
                src, step, side = dst, step * 2, 1 - side
            ends = src
            starts = a["sums"][:, side]
            then(v.tensor_tensor(starts, ends, a["blocks"], ALU.subtract))
            rank = bank(1)[:, 0:T * E].rearrange("p (t e) -> p t e", t=T)
            then(v.tensor_scalar(starts, starts, float(P), None, ALU.mult))
            then(v.tensor_tensor(a["slot"], rank, spread(starts, 1, T), ALU.add))
            v.tensor_tensor(a["all1"], a["all1"], a["slot"], ALU.mult)
            v.tensor_tensor(a["all2"], a["all2"], a["slot"], ALU.mult)
            v.tensor_tensor(a["tab"][0:1], spread(ends[0:1, :], 1, m.blocks),
                            spread(cst[0:1, C_IOTA:C_IOTA + m.blocks], 2, E), ALU.is_le)
            dve.drain()
            v.tensor_reduce(a["sl"][:, 0], a["all1"], axis=AX.X, op=ALU.add)
            v.tensor_reduce(a["sl"][:, 1], a["all2"], axis=AX.X, op=ALU.add)
            v.tensor_reduce(a["tabr"][0:1, 0:m.blocks], a["tab"][0:1], axis=AX.X, op=ALU.add)
            dve.drain()
            v.tensor_copy(slots_i[:, :, 0:T], a["sl"])
            then(v.tensor_scalar(a["tabr"][0:1, 0:m.blocks], a["tabr"][0:1, 0:m.blocks], float(E - 1), None, ALU.min))
            v.tensor_copy(expert_of[0:1, 0:m.blocks], a["tabr"][0:1, 0:m.blocks])
            v.tensor_copy(used_blocks[0:1, 0:1], ends[0:1, E - 1:E])
            dve.drain().then_inc(summed[f"{name}.table"], 1)

        def moe_scatter(pool, name, m, src):
            pool.wait_ge(*count(f"{name}.table", 1))
            for t in range(m.T):
                for c in range(2):
                    nc.gpsimd.indirect_dma_start(
                        out=d["xs"][:, :], out_offset=bass.IndirectOffsetOnAxis(ap=slots_i[:, c, t:t + 1], axis=0),
                        in_=src[:, t, :], in_offset=None).then_inc(summed[f"{name}.scattered"], 16)
            pool.wait_ge(*count(f"{name}.scattered", 32 * m.T))

        def used(eng, m):
            return eng.value_load(used_blocks[0:1, 0:1], min_val=1, max_val=m.blocks)

        def moe_sp(sp, name, m, w, chunks):
            base = chunks.n
            sp.wait_ge(*count(f"{name}.table", 1))
            n_used = used(sp, m)
            with sp.Fori(0, m.blocks // 4) as turn:
                for b in range(4):
                    slots = [(base + 3 * b + part) % RING for part in range(3)]
                    with sp.If(turn * 4 + b < n_used):
                        e = sp.value_load(expert_of[0:1, bass.ds(turn * 4 + b, 1)], min_val=0, max_val=m.E - 1)
                        for part in range(3):
                            mat = w[part][bass.ds(e, 1), :, :].rearrange("a (p k) n -> p (a k n)", p=P)
                            sp.wait_ge(w_free, turn * 12 + (base + 3 * b + part - RING + 1))
                            sp.dma_start(w_ring[:, slots[part], :], mat).then_inc(w_landed[slots[part]], 16)
                    with sp.Else():
                        for part in range(3):
                            sp.wait_ge(w_free, turn * 12 + (base + 3 * b + part - RING + 1))
                            sp.sem_inc(w_landed[slots[part]], 16)
            chunks.n += 3 * m.blocks

        def moe_blocks_pe(pe, name, m, chunks):
            base = chunks.n

            def turn_rows(s, rows_value):
                pe.wait_ge(*count(f"{name}.rows{s}", rows_value))
                rows_k = blk_rows[:, s, :].rearrange("p (f k) -> p k f", k=KT)
                for k in range(KT):
                    mm = nc.tensor.transpose(bank(k // 4)[:, P * (k % 4):P * (k % 4 + 1)], rows_k[:, k, :], ident)
                mm.then_inc(summed[f"{name}.turned"], 1)

            n_used = used(pe, m)
            turn_rows(0, 16)
            with pe.Fori(0, m.blocks // 4) as turn:
                for b in range(4):
                    s = b % 2
                    n = turn * 4 + b
                    with pe.If(n < n_used):
                        pe.wait_ge(*count(f"{name}.feat", n + 1))
                        for part in range(2):
                            c = base + 3 * b + part
                            pe.wait_ge(w_landed[c % RING], turn * 48 + 16 * (c // RING + 1))
                            for k in range(KT):
                                mm = nc.tensor.matmul(bank(2 + part), blk_feat[:, s, k, :],
                                                      chunk_view(c % RING, FF)[:, k, :], start=k == 0, stop=k == KT - 1)
                            mm.then_inc(w_free, 1)
                        turn_rows(1 - s, turn * 32 + 16 * ((b + 1) // 2 + 1))
                        pe.wait_ge(*count(f"{name}.hid", n + 1))
                        hid_k = blk_hid[:, s, :].rearrange("p (f k) -> p k f", k=4)
                        for k in range(4):
                            mm = nc.tensor.transpose(bank(4)[:, P * k:P * (k + 1)], hid_k[:, k, :], ident)
                        mm.then_inc(summed[f"{name}.hid_turned"], 1)
                        pe.wait_ge(*count(f"{name}.hid_feat", n + 1))
                        pe.wait_ge(*count(f"{name}.y_copied", n + 1))
                        c = base + 3 * b + 2
                        pe.wait_ge(w_landed[c % RING], turn * 48 + 16 * (c // RING + 1))
                        for half in range(2):
                            for k in range(4):
                                mm = nc.tensor.matmul(bank(5 + half), blk_hidT[:, s, k, :],
                                                      chunk_view(c % RING, D, 4)[:, k, 512 * half:512 * half + 512],
                                                      start=k == 0, stop=k == 3)
                        mm.then_inc(w_free, 1)
                    with pe.Else():
                        pe.drain().then_inc(w_free, 3)
                        pe.sem_inc(summed[f"{name}.turned"], 1)
                        pe.sem_inc(summed[f"{name}.hid_turned"], 1)
            chunks.n += 3 * m.blocks

        def moe_blocks_act(act, name, m, chunks):
            base = chunks.n

            def load_rows(block, s):
                act.dma_start(blk_rows[:, s, :], d["xs"][bass.ds(block * P, P), :]).then_inc(
                    summed[f"{name}.rows{s}"], 16)

            def take_features(s):
                nc.scalar.activation(blk_feat[:, s], ps[:, 0:1024].rearrange("p (k n) -> p k n", n=P),
                                     ACT.Copy).then_inc(summed[f"{name}.feat"], 1)

            n_used = used(act, m)
            load_rows(0, 0)
            load_rows(1, 1)
            act.wait_ge(*count(f"{name}.turned", 1))
            take_features(0)
            with act.Fori(0, m.blocks // 4) as turn:
                for b in range(4):
                    s = b % 2
                    n = turn * 4 + b
                    with act.If(n < n_used):
                        act.wait_ge(w_free, turn * 12 + (base + 3 * b + 1))
                        nc.scalar.activation(blk_gate[:, s, :], bank(2), ACT.Silu).then_inc(summed[f"{name}.silu"], 1)
                        act.wait_ge(*count(f"{name}.turned", n + 2))
                        take_features(1 - s)
                        load_rows(n + 2, s)
                        act.wait_ge(*count(f"{name}.hid_turned", n + 1))
                        nc.scalar.activation(blk_hidT[:, s], bank(4).rearrange("p (k n) -> p k n", n=P),
                                             ACT.Copy).then_inc(summed[f"{name}.hid_feat"], 1)
                    with act.Else():
                        act.drain().then_inc(summed[f"{name}.silu"], 1)
                        act.sem_inc(summed[f"{name}.feat"], 1)
                        act.sem_inc(summed[f"{name}.hid_feat"], 1)
                        act.sem_inc(summed[f"{name}.rows{s}"], 16)
            for s in range(2):
                act.wait_ge(*count(f"{name}.rows{s}", 16 * (m.blocks // 2 + 1)))
            chunks.n += 3 * m.blocks

        def moe_blocks_dve(dve, name, m, chunks):
            base = chunks.n
            n_used = used(dve, m)
            dve.sem_inc(summed[f"{name}.y_copied"], 1)
            with dve.Fori(0, m.blocks // 4) as turn:
                for b in range(4):
                    s = b % 2
                    n = turn * 4 + b
                    with dve.If(n < n_used):
                        dve.wait_ge(*count(f"{name}.silu", n + 1))
                        dve.wait_ge(w_free, turn * 12 + (base + 3 * b + 2))
                        nc.vector.tensor_tensor(blk_hid[:, s, :], blk_gate[:, s, :], bank(3), ALU.mult).then_inc(
                            summed[f"{name}.hid"], 1)
                        dve.wait_ge(w_free, turn * 12 + (base + 3 * b + 3))
                        dve.wait_ge(*count(f"{name}.out_free", n + 1))
                        nc.vector.tensor_copy(blk_out[:, s, :], ps[:, 2560:3584]).then_inc(summed[f"{name}.y_copied"], 1)
                    with dve.Else():
                        dve.drain().then_inc(summed[f"{name}.hid"], 1)
                        dve.sem_inc(summed[f"{name}.y_copied"], 1)
            chunks.n += 3 * m.blocks

        def moe_blocks_pool(pool, name, m):
            n_used = used(pool, m)
            pool.sem_inc(summed[f"{name}.out_free"], 2)
            with pool.Fori(0, m.blocks // 4) as turn:
                for b in range(4):
                    n = turn * 4 + b
                    with pool.If(n < n_used):
                        pool.wait_ge(*count(f"{name}.y_copied", n + 2))
                        pool.dma_start(d["ys"][bass.ds(n * P, P), :], blk_out[:, b % 2, :]).then_inc(
                            summed[f"{name}.stored"], 16)
                        pool.wait_ge(*count(f"{name}.stored", n * 16 + 16))
                        pool.sem_inc(summed[f"{name}.out_free"], 1)
                    with pool.Else():
                        pool.sem_inc(summed[f"{name}.out_free"], 1)

        def moe_gather_pool(pool, name, m):
            for t in range(m.T):
                if t >= 2:
                    pool.wait_ge(*count(f"{name}.picked_free", t - 1))
                for c in range(2):
                    nc.gpsimd.indirect_dma_start(
                        out=picked[:, 2 * (t % 2) + c, :], out_offset=None, in_=d["ys"][0:P * m.blocks, :],
                        in_offset=bass.IndirectOffsetOnAxis(ap=slots_i[:, c, t:t + 1], axis=0)
                    ).then_inc(summed[f"{name}.gathered"], 16)
                pool.wait_ge(*count(f"{name}.gathered", 32 * (t + 1)))
                pool.sem_inc(summed[f"{name}.both_rows"], 1)

        def moe_combine_dve(dve, name, m, alpha, gate, g, b):
            for t in range(m.T):
                dve.wait_ge(*count(f"{name}.both_rows", t + 1))
                y1, y2 = picked[:, 2 * (t % 2), :], picked[:, 2 * (t % 2) + 1, :]
                nc.vector.tensor_scalar(y1, y1, gate_w[:, 0, t:t + 1], None, ALU.mult)
                dve.drain()
                nc.vector.scalar_tensor_tensor(y1, y2, gate_w[:, 1, t:t + 1], y1, ALU.mult, ALU.add)
                dve.drain()
                if gate is not None:
                    nc.vector.tensor_tensor(y1, y1, gate(t), ALU.mult)
                    dve.drain()
                x = x_tok[:, t, :]
                nc.vector.scalar_tensor_tensor(x, x, alpha, y1, ALU.mult, ALU.add).then_inc(
                    summed[f"{name}.picked_free"], 1)
                dve.drain()
                normalise(dve, name, t, t, g, b)
            dve.drain()

        def ada_pe(pe, chunks, n):
            c = chunks.take()
            await_chunk(pe, c)
            if n >= 2:
                pe.wait_ge(*count("ada.read", n - 1))
            for k in range(KT):
                mm = nc.tensor.matmul(bank(6 + n % 2)[0:2, :], fcol[:, FC["cond"] + 2 * k:FC["cond"] + 2 * k + 2],
                                      chunk_view(c % RING, 512)[:, k, :], start=k == 0, stop=k == KT - 1)
            mm.then_inc(summed["ada.ready"], 1)
            pe.drain().then_inc(w_free, 1)

        def ada_act(act, n, buffers):
            act.wait_ge(*count("ada.ready", n + 1))
            if n >= 2:
                act.wait_ge(*count(f"ada.sent{n % 2}", 16 * (n // 2)))
            nc.scalar.activation(buffers[n % 2][0:2, :], bank(6 + n % 2)[0:2, :], ACT.Copy).then_inc(
                summed["ada.read"], 1)

        def ada_pool(pool, n, buffers):
            pool.wait_ge(*count("ada.read", n + 1))
            pool.dma_start(d["mods"][:, 512 * n:512 * n + 512], buffers[n % 2][0:2, :], accum_op=ALU.add).then_inc(
                summed[f"ada.sent{n % 2}"], 16)

        def attention_pe(pe, name, jobs, probs, probsT):
            n = len(jobs)
            for step in range(n + 3):
                if step < n:
                    jb = jobs[step]
                    if step >= 2:
                        pe.wait_ge(*count(f"{name}.exped", step - 1))
                    for lo, hi in jb["spans"]:
                        terms = jb["terms"](lo, hi)
                        for k, (q, kk) in enumerate(terms):
                            mm = nc.tensor.matmul(ps[:, 1024 * (step % 2) + lo:1024 * (step % 2) + hi], q, kk,
                                                  start=k == 0, stop=k == len(terms) - 1)
                    mm.then_inc(summed[f"{name}.scores"], 1)
                if 0 <= step - 2 < n:
                    j = step - 2
                    pe.wait_ge(*count(f"{name}.exped", j + 1))
                    if j >= 1:
                        pe.wait_ge(*count(f"{name}.turned_read", j))
                    for k in range(jobs[j]["keys"] // P):
                        mm = nc.tensor.transpose(ps[:, 2048 + P * k:2048 + P * (k + 1)],
                                                 probs[:, j % 2, P * k:P * (k + 1)], ident)
                    mm.then_inc(summed[f"{name}.turned"], 1)
                if 0 <= step - 3 < n:
                    j = step - 3
                    pe.wait_ge(*count(f"{name}.turned_read", j + 1))
                    if j >= 2:
                        pe.wait_ge(*count(f"{name}.out_read", j - 1))
                    kt = jobs[j]["keys"] // P
                    for k in range(kt):
                        mm = nc.tensor.matmul(bank(6 + j % 2, HD), probsT[:, j % 2, P * k:P * (k + 1)],
                                              jobs[j]["values"](k), start=k == 0, stop=k == kt - 1)
                    mm.then_inc(summed[f"{name}.out"], 1)

        def attention_dve(dve, name, jobs, stat):
            n = len(jobs)
            for step in range(n + 3):
                if step < n:
                    jb = jobs[step]
                    s = ps[:, 1024 * (step % 2):1024 * (step % 2) + jb["keys"]]
                    dve.wait_ge(*count(f"{name}.scores", step + 1))
                    if jb["adjust"]:
                        jb["adjust"](dve, s)
                        dve.drain()
                    nc.vector.tensor_reduce(stat[:, step % 4, 0:1], s, axis=AX.X, op=ALU.max, negate=True
                                            ).then_inc(summed[f"{name}.shift"], 1)
                if step >= 3:
                    j = step - 3
                    nc.vector.reciprocal(stat[:, j % 4, 2:3], stat[:, j % 4, 1:2])
                    dve.drain()
                    dve.wait_ge(*count(f"{name}.out", j + 1))
                    nc.vector.tensor_scalar(jobs[j]["dest"], bank(6 + j % 2, HD), stat[:, j % 4, 2:3], None,
                                            ALU.mult).then_inc(summed[f"{name}.out_read"], 1)

        def attention_act(act, name, jobs, probs, probsT, stat):
            n = len(jobs)
            for step in range(n + 2):
                if 0 <= step - 2 < n:
                    j = step - 2
                    act.wait_ge(*count(f"{name}.turned", j + 1))
                    if j >= 2:
                        act.wait_ge(*count(f"{name}.out", j - 1))
                    nc.scalar.activation(probsT[:, j % 2, 0:jobs[j]["keys"]], ps[:, 2048:2048 + jobs[j]["keys"]],
                                         ACT.Copy).then_inc(summed[f"{name}.turned_read"], 1)
                if step < n:
                    keys = jobs[step]["keys"]
                    act.wait_ge(*count(f"{name}.shift", step + 1))
                    if step >= 4:
                        act.wait_ge(*count(f"{name}.out_read", step - 3))
                    nc.scalar.activation(probs[:, step % 2, 0:keys], ps[:, 1024 * (step % 2):1024 * (step % 2) + keys],
                                         ACT.Exp, bias=stat[:, step % 4, 0:1], accum_out=stat[:, step % 4, 1:2])
                    act.drain().then_inc(summed[f"{name}.exped"], 1)

        def attended_pe(pe, name, sources):
            for j, (t, part) in enumerate((t, part) for t in range(TL) for part in range(len(sources))):
                for q in range(4):
                    mm = nc.tensor.transpose(bank(j)[:, P * q:P * (q + 1)],
                                             sources[part][1][:, t, P * q:P * (q + 1)], ident)
                mm.then_inc(summed[f"{name}.ready"], 1)

        def attended_take(eng, name, parity, sources):
            for j, (t, part) in enumerate((t, part) for t in range(TL) for part in range(len(sources))):
                if j % 2 == parity:
                    eng.wait_ge(*count(f"{name}.ready", j + 1))
                    out = x_feat[:, sources[part][0]:sources[part][0] + 4, P * t:P * (t + 1)]
                    src = bank(j).rearrange("p (q n) -> p q n", q=4)
                    if parity:
                        nc.scalar.activation(out, src, ACT.Copy)
                    else:
                        nc.vector.tensor_copy(out, src)

        def attention_sems(name):
            new_sems(name, "scores", "shift", "exped", "turned", "turned_read", "out", "out_read", "ready")

        MOE1 = Moe(TL, 4, 4)
        MOE2 = Moe(TA, 4, 8)
        MOE3 = Moe(TL, 4, 8)
        MOE1_AT = 6 + 12 + 2
        MOE2_AT = MOE1_AT + 3 * MOE1.blocks + 5 + 12 + 2
        MOE3_AT = MOE2_AT + 3 * MOE2.blocks + 5 + 2
        loads = sem("loads")
        filled = sem("filled")
        fill = x_feat[:, 0:2, SEQ:NTOK]
        XS_BLOCKS = MOE2.blocks + 2

        z_feat = region(0, 4, SEQ)
        q_feat = region(2048, 4, SEQ)
        k_feat = region(4096, 4, SEQ)
        v_tok = region(6144, TL, 512)
        xdt_tok = region(8192, TL, 512)
        xbc = region(10240, 8, SEQ)
        xbc_in = region(14336, 8, SEQ + 3)
        decay = region(14336, 2, 1280)
        mixed = x_feat[:, 4:8, :].rearrange("p k n -> p (k n)")[:, 0:2560].rearrange("p (b n) -> p b n", b=2)
        TRI_AT = [0, 512, 896, 1152]
        cb = region(18456, 2, 1280)
        dtf = region(21016, TL, 16)
        dts = region(21080, 3, TL, 16)
        cum = region(21272, TL, 16)
        a_row = region(21336, 8)
        w_dtf = region(21344, KT, 16)
        v_bias = region(8192, 512)
        cum_row = region(21984, SEQ)
        fneg_row = region(22496, SEQ)
        rms1 = region(8192, 2, SEQ)
        probs1 = region(14336, 2, 512)
        probsT1 = region(15360, 2, 512)
        stat = sb("stat", [P, 4, 4])

        new_sems("x0", "ready", "read0", "read1")
        new_sems("in1", "ready", "read0", "read1", "dtf", "dt1", "dt2", "cum", "cumd", "cumt")
        new_sems("conv1", "silu", "acc")
        new_sems("ssd", "cb", "cbd", "xs", "xsd", "row", "arg", "exp", "mix", "y", "y_read", "var_in", "var", "root")
        attention_sems("att1")
        new_sems("out1", "ready", "read", "var", "root")
        moe_sems(("moe1", MOE1), ("moe2", MOE2), ("moe3", MOE3))
        new_sems("ada", "ready", "read", "sent0", "sent1")
        new_sems("x2", "ready", "read0", "read1")
        new_sems("in2", "ready", "read0", "read1", "read2", "read3", "read4", "sig")
        new_sems("ca", "mean_in", "mean", "root", "sq", "silu")
        new_sems("out2", "ready", "read", "var", "root")
        new_sems("x3", "ready", "read0", "read1")
        new_sems("in3", "ready", "read0", "read1")
        new_sems("rope", "sq", "root", "done", "turned", "turned_read", "g_here0", "g_here1", "g_free")
        attention_sems("att2")
        new_sems("out3", "ready", "read", "var", "root")

        IN1 = []
        for chunk in range(5):
            for i in range(4):
                IN1.append((i == 0, i == 3, feature_products(P * i, SEQ)))
        for t in range(TL):
            IN1.append((t == 0, t == TL - 1, token_products(t, 512, v_bias[0:1, :])))
        IN1_COLS = [0, 512, 1024, 1544, 2056, 2568]

        def in1_take(v):
            def take(j):
                src = pair(j, 512)
                chunk, i = j // 4, j % 4
                bias = fcol[:, FC["b_in"] + j:FC["b_in"] + j + 1]
                if chunk == 0:
                    if v:
                        return nc.vector.tensor_scalar(z_feat[:, i, :], src, bias, None, ALU.add)
                    return nc.scalar.activation(z_feat[:, i, :], src, ACT.Identity, bias=bias)
                if chunk in (1, 2):
                    out = xbc_in[:, 4 * (chunk - 1) + i, 3:]
                elif chunk == 3:
                    if v:
                        return nc.vector.tensor_scalar(q_feat[:, i, :], src, ATT_SCALE, bias, ALU.mult, ALU.add)
                    return nc.scalar.activation(q_feat[:, i, :], src, ACT.Identity, bias=bias, scale=ATT_SCALE)
                elif chunk == 4:
                    out = k_feat[:, i, :]
                else:
                    out = v_tok[:, i, :]
                    return (nc.vector.tensor_copy(out, src) if v else nc.scalar.activation(out, src, ACT.Copy))
                if v:
                    return nc.vector.tensor_scalar(out, src, bias, None, ALU.add)
                return nc.scalar.activation(out, src, ACT.Identity, bias=bias)
            return take

        att1_tok = region(16384, TL, 512)
        ATT1 = [(4, att1_tok)]

        def att1_jobs():
            jobs = []
            for h in range(HEADS):
                half = HD * (h % 2)
                for i in range(TL):
                    keys = P * (i + 1)

                    def terms(lo, hi, h=h, i=i, half=half):
                        return [(q_feat[half:half + HD, h // 2, P * i:P * (i + 1)], k_feat[half:half + HD, h // 2, lo:hi]),
                                (ident[0:16, 8 + h:9 + h].broadcast_to([16, P]), fneg_row[0:16, lo:hi])]

                    def adjust(dve, s, i=i):
                        nc.vector.tensor_tensor(s[:, P * i:], s[:, P * i:], causal, ALU.add)

                    jobs.append({"spans": [(0, keys)], "terms": terms, "keys": keys, "adjust": adjust,
                                 "values": lambda k, h=h: v_tok[:, k, HD * h:HD * (h + 1)],
                                 "dest": att1_tok[:, i, HD * h:HD * (h + 1)]})
            return jobs

        sig = region(0, 2, NTOK)
        ya_in = region(1536, 4, PADDED)
        yb_in = region(1536 + 4 * PADDED, 4, PADDED)
        o2 = 1536 + 8 * PADDED
        b_gate = region(o2, 4, NTOK)
        ya = region(o2 + 4 * NTOK, 4, SPAN)
        yb = region(o2 + 4 * NTOK + 4 * SPAN, 4, SPAN)
        col2 = region(22978, 2, 2, 8)
        mean2 = region(1536, SPAN)
        cen2 = region(1536 + SPAN + 1, 2, SPAN)
        IN2_COLS = [512, 0, 1536, 2048, 1024]
        IN2 = [(i == 0, i == 3, feature_products(P * i, NTOK)) for _ in range(5) for i in range(4)]

        def padded(buf, i):
            return ((buf[:, i, PAD:PAD + SEQ], slice(0, SEQ)), (buf[:, i, PAD + CTX_AT:PAD + CTX_AT + CTX], slice(SEQ, NTOK)))

        qk_tok = region(0, TA, 10, HD)
        rp = region(3840, 4, 320)
        probs3 = region(0, 2, NTOK)
        probsT3 = region(2 * NTOK, 2, NTOK)
        qc_feat = region(5120, 4, SEQ)
        kc_feat = region(7168, 2, NTOK)
        qd_feat = region(8704, 4, SEQ)
        kd_feat = region(10752, 4, NTOK)
        vc_tok = region(13824, TA, P)
        vd_tok = region(14592, TA, 512)
        g_bias = region(17664, 2, 16, HD)
        rope_cs = region(19712, TL, 2, 32)
        rr = region(19968, TA, 10)
        col3 = region(22978, 2, 2, 8)
        kdup = region(20064, 256)
        sq3 = region(20320, 640)

        IN3 = ([(t == 0, t == TL - 1, token_products(t, 512)) for t in range(TL)]
               + [(t == 0, t == TA - 1, token_products(t, 256)) for t in range(TA)]
               + [(i == 0, i == 3, feature_products(P * i, SEQ)) for i in range(4)]
               + [(i == 0, i == 3, feature_products(P * i, NTOK)) for i in range(4)]
               + [(t == 0, t == TA - 1, token_products(t, 512)) for t in range(TA)])
        IN3_COLS = [(0, 512), (512, 256), (768, 512), (1280, 512), (1792, 512)]

        def in3_take(v):
            def take(j):
                def copy(out, src):
                    return nc.vector.tensor_copy(out, src) if v else nc.scalar.activation(out, src, ACT.Copy)
                if j < TL:
                    return copy(qk_tok[:, j, 0:8, :], pair(j, 512).rearrange("p (h e) -> p h e", h=8))
                j0 = j - TL
                if j0 < TA:
                    copy(qk_tok[:, j0, 8:10, :], pair(j, P).rearrange("p (h e) -> p h e", h=2))
                    return copy(vc_tok[:, j0, :], pair(j, 256)[:, P:])
                j0 -= TA
                if j0 < 4:
                    if v:
                        return nc.vector.tensor_scalar(qd_feat[:, j0, :], pair(j, SEQ), ATT_SCALE, None, ALU.mult)
                    return nc.scalar.activation(qd_feat[:, j0, :], pair(j, SEQ), ACT.Copy, scale=ATT_SCALE)
                j0 -= 4
                if j0 < 4:
                    return copy(kd_feat[:, j0, :], pair(j, NTOK))
                return copy(vd_tok[:, j0 - 4, :], pair(j, 512))
            return take

        attc_tok = region(3072, TL, 512)
        attd_tok = region(20928, TL, 512)
        ATT2 = [(0, attc_tok), (4, attd_tok)]

        def att2_jobs():
            jobs = []
            for h in range(HEADS):
                half = HD * (h % 2)
                for i in range(TL):
                    jobs.append({
                        "spans": [(0, 512), (512, NTOK)],
                        "terms": lambda lo, hi, h=h, i=i, half=half: [
                            (qc_feat[half:half + HD, h // 2, P * i:P * (i + 1)], kc_feat[half:half + HD, h // 4, lo:hi])],
                        "keys": NTOK, "adjust": None,
                        "values": lambda k, h=h: vc_tok[:, k, HD * (h // 4):HD * (h // 4 + 1)],
                        "dest": attc_tok[:, i, HD * h:HD * (h + 1)]})
            for h in range(HEADS):
                half = HD * (h % 2)
                for i in range(TL):
                    def adjust(dve, s, h=h, i=i):
                        if i == 0:
                            dve.wait_ge(*count(f"rope.g_here{h % 2}", 32 * (h // 2 + 1)))
                        b = g_bias[:, h % 2, 7 - 2 * i:15 - 2 * i, :].rearrange("p r c -> p (r c)")
                        ins = nc.vector.tensor_tensor(s[:, 0:SEQ], b, s[:, 0:SEQ], ALU.add)
                        if i == TL - 1:
                            ins.then_inc(summed["rope.g_free"], 1)
                    jobs.append({
                        "spans": [(0, 512), (512, NTOK)],
                        "terms": lambda lo, hi, h=h, i=i, half=half: [
                            (qd_feat[half:half + HD, h // 2, P * i:P * (i + 1)], kd_feat[half:half + HD, h // 2, lo:hi])],
                        "keys": NTOK, "adjust": adjust,
                        "values": lambda k, h=h: vd_tok[:, k, HD * h:HD * (h + 1)],
                        "dest": attd_tok[:, i, HD * h:HD * (h + 1)]})
            return jobs

        ada_early = [region(21472, 512), x_feat[:, 7, NTOK - 512:NTOK]]
        ada_late = [region(17400, 512), region(17912, 512)]
        ADA_FIRST = 3

        def mixed_sq(c):
            return region(10240 + 2048 + 512 * c, SEQ)

        def kdup_of(t):
            return region(20064 + 256 * (t % 2), 256)

        block = es.enter_context(nc.Block())

        @block.sync
        def _(sp):
            chunks = Chunks()
            for c0 in IN1_COLS:
                load_columns(sp, chunks, d["w_in"], c0, 512)
            for c in range(12):
                load_columns(sp, chunks, d["ada_w"][0], 512 * c, 512)
            for c0 in (0, 512):
                load_columns(sp, chunks, d["w_out"], c0, 512)
            moe_sp(sp, "moe1", MOE1, (d["w_gate"], d["w_up"], d["w_down"]), chunks)
            for c0 in IN2_COLS:
                load_columns(sp, chunks, d["conv_w_in"], c0, 512)
            for c in range(12):
                load_columns(sp, chunks, d["ada_w"][1], 512 * c, 512)
            for c0 in (0, 512):
                load_columns(sp, chunks, d["conv_w_out"], c0, 512)
            moe_sp(sp, "moe2", MOE2, tuple(d[k][0] for k in ("e_gate", "e_up", "e_down")), chunks)
            for c0, n in IN3_COLS:
                load_columns(sp, chunks, d["attn_w_in"], c0, n)
            for c0 in (0, 512):
                load_columns(sp, chunks, d["attn_w_out"], c0, 512)
            moe_sp(sp, "moe3", MOE3, tuple(d[k][1] for k in ("e_gate", "e_up", "e_down")), chunks)

        @block.tensor
        def _(pe):
            chunks = Chunks()
            stage(pe, "pe", "loaded")
            transpose_pe(pe, "x0", range(TL))
            stage(pe, "pe", "x1")
            for t in range(TL):
                for k in range(KT):
                    mm = nc.tensor.matmul(bank(7)[:, 16 * t:16 * t + 16], x_feat[:, k, P * t:P * (t + 1)],
                                          w_dtf[:, k, :], start=k == 0, stop=k == KT - 1)
            mm.then_inc(summed["in1.dtf"], 1)
            pe.wait_ge(*count("in1.dt1", 1))
            linear_pe(pe, "in1", IN1, chunks, by_parity("in1"))
            stage(pe, "pe", "in1")
            for t in range(TL):
                for s in range(t + 1):
                    mm = nc.tensor.matmul(bank(0)[:, 16 * t:16 * t + 16], ones if s < t else tri, dtf[:, s, :],
                                          start=s == 0, stop=s == t)
            mm.then_inc(summed["in1.cum"], 1)
            pe.wait_ge(*count("in1.cumd", 1))
            for t in range(TL):
                mm = nc.tensor.transpose(bank(1)[0:16, P * t:P * (t + 1)], cum[:, t, :], ident)
            mm.then_inc(summed["in1.cumt"], 1)
            pe.wait_ge(*count("conv1.silu", 8))
            for g in range(2):
                for s in range(TL):
                    n = SEQ - P * s
                    if g:
                        pe.wait_ge(*count("ssd.cbd", s + 1))
                    nc.tensor.matmul(bank(2 + s, n), xbc[:, 4 + g, P * s:P * (s + 1)], xbc[:, 6 + g, P * s:SEQ],
                                     start=True, stop=True).then_inc(summed["ssd.cb"], 1)
            for t in range(TL):
                if t >= 2:
                    pe.wait_ge(*count("ssd.xsd", t - 1))
                for c in range(4):
                    mm = nc.tensor.transpose(bank(6 + t % 2)[:, P * c:P * (c + 1)], xbc[:, c, P * t:P * (t + 1)], ident)
                mm.then_inc(summed["ssd.xs"], 1)
            pe.wait_ge(*count("ssd.xsd", TL))
            for n in range(ADA_FIRST):
                ada_pe(pe, chunks, n)
            stage(pe, "pe", "ssd_in")
            for step in range(HEADS + 1):
                if step < HEADS:
                    if step >= 2:
                        pe.wait_ge(*count("ssd.arg", step - 1))
                    nc.tensor.matmul(bank(step % 2), ident[0:16, step:step + 1].broadcast_to([16, P]),
                                     cum_row[0:16, :], start=True, stop=True).then_inc(summed["ssd.row"], 1)
                if step >= 1:
                    h = step - 1
                    pe.wait_ge(*count("ssd.mix", h + 1))
                    if h >= 4 and h % 2 == 0:
                        pe.wait_ge(*count("ssd.y_read", (h - 4) // 2 + 1))
                    half = HD * (h % 2)
                    for s in range(TL):
                        mm = nc.tensor.matmul(bank(2 + (h // 2) % 2)[half:half + HD, P * s:SEQ],
                                              xdt_tok[:, s, HD * h:HD * (h + 1)],
                                              mixed[:, h % 2, TRI_AT[s]:TRI_AT[s] + SEQ - P * s],
                                              start=s == 0, stop=s == TL - 1)
                    mm.then_inc(summed["ssd.y"], 1)
                ada_pe(pe, chunks, ADA_FIRST + step)
            for g in range(2):
                pe.wait_ge(*count("ssd.var_in", 2 * (g + 1)))
                for c in range(2):
                    mm = nc.tensor.matmul(bank(4 + g), ones, mixed_sq(2 * g + c), start=c == 0, stop=c == 1)
                mm.then_inc(summed["ssd.var"], 1)
            stage(pe, "pe", "ssd")
            attention_pe(pe, "att1", att1_jobs(), probs1, probsT1)
            stage(pe, "pe", "att1")
            attended_pe(pe, "att1", ATT1)
            stage(pe, "pe", "att1t")
            out_proj_pe(pe, "out1", range(TL), chunks)
            stage(pe, "pe", "out1")
            transpose_pe(pe, "moe1.t", range(TL))
            stage(pe, "pe", "h1")
            moe_router_pe(pe, "moe1", MOE1, moe_arrays(MOE1)["wr"])
            stage(pe, "pe", "route1")
            moe_blocks_pe(pe, "moe1", MOE1, chunks)
            stage(pe, "pe", "experts1")
            stage(pe, "pe", "combine1")
            transpose_pe(pe, "x2", range(TA))
            stage(pe, "pe", "x2")
            linear_pe(pe, "in2", IN2, chunks, lambda j: count(f"in2.read{j // 4}", j % 4 + 1))
            pe.wait_ge(*count("in2.read4", 4))
            for n in range(12, 24):
                ada_pe(pe, chunks, n)
            stage(pe, "pe", "in2")
            for j in range(2):
                for i in range(4):
                    pe.wait_ge(*count("ca.mean_in", 4 * j + i + 1))
                    src = ya[:, i] if j == 0 else cen2[:, i % 2]
                    for lo, hi in ((0, 512), (512, SPAN)):
                        mm = nc.tensor.matmul(ps[:, 1024 * j + lo:1024 * j + hi], ones, src[:, lo:hi],
                                              start=i == 0, stop=i == 3)
                    mm.then_inc(summed["ca.mean"], 1)
            stage(pe, "pe", "conv")
            out_proj_pe(pe, "out2", range(TA), chunks)
            stage(pe, "pe", "out2")
            stage(pe, "pe", "h2")
            transpose_pe(pe, "moe2.t", range(TA), h_tok)
            stage(pe, "pe", "h2t")
            moe_router_pe(pe, "moe2", MOE2, moe_arrays(MOE2)["wr"])
            stage(pe, "pe", "route2")
            moe_blocks_pe(pe, "moe2", MOE2, chunks)
            stage(pe, "pe", "experts2")
            stage(pe, "pe", "combine2")
            transpose_pe(pe, "x3", range(TA))
            stage(pe, "pe", "x3")
            linear_pe(pe, "in3", IN3, chunks, by_parity("in3"))
            stage(pe, "pe", "in3")
            for t in range(TA):
                pe.wait_ge(*count("rope.done", t + 1))
                if t >= 2:
                    pe.wait_ge(*count("rope.turned_read", t - 1))
                b = 2 * (t % 2)
                for c in range(4 if t < TL else 0):
                    nc.tensor.transpose(bank(b)[:, P * c:P * (c + 1)],
                                        qk_tok[:, t, 2 * c:2 * c + 2, :].rearrange("p h e -> p (h e)"), ident)
                for c in range(2):
                    mm = nc.tensor.transpose(bank(b + 1)[:, P * c:P * (c + 1)], kdup_of(t)[:, P * c:P * (c + 1)], ident)
                mm.then_inc(summed["rope.turned"], 1)
            stage(pe, "pe", "rope")
            attention_pe(pe, "att2", att2_jobs(), probs3, probsT3)
            stage(pe, "pe", "att2")
            attended_pe(pe, "att2", ATT2)
            stage(pe, "pe", "att2t")
            out_proj_pe(pe, "out3", range(TL), chunks)
            stage(pe, "pe", "out3")
            stage(pe, "pe", "h3")
            transpose_pe(pe, "moe3.t", range(TL), h_tok)
            stage(pe, "pe", "h3t")
            moe_router_pe(pe, "moe3", MOE3, moe_arrays(MOE3)["wr"])
            stage(pe, "pe", "route3")
            moe_blocks_pe(pe, "moe3", MOE3, chunks)
            stage(pe, "pe", "experts3")
            stage(pe, "pe", "combine3")

        @block.scalar
        def _(act):
            stage(act, "act", "loaded")
            transpose_take(act, "x0", 1, range(TL), x_feat)
            nc.scalar.activation(fcol[:, FC["cond"]:FC["cond"] + 16], fcol[:, FC["cond"]:FC["cond"] + 16], ACT.Silu)
            stage(act, "act", "x1")
            linear_take(act, "in1", 1, [in1_take(False)] * len(IN1))
            act.wait_ge(*count("in1.dt1", 1))
            nc.scalar.activation(dts[:, 1], dts[:, 1], ACT.Exp)
            act.drain()
            nc.scalar.activation(dts[:, 2], dts[:, 1], ACT.Identity, bias=ones[:, 0:1])
            act.drain()
            nc.scalar.activation(dtf[:, :, :], dts[:, 2], ACT.Ln)
            nc.scalar.activation(a_row, frow[:, RC["a_log"]:RC["a_log"] + 8], ACT.Exp)
            act.drain().then_inc(summed["in1.dt2"], 1)
            stage(act, "act", "in1")
            for i in range(4):
                nc.scalar.activation(z_feat[:, i, :], z_feat[:, i, :], ACT.Silu)
            for i in range(8):
                act.wait_ge(*count("conv1.acc", i + 1))
                nc.scalar.activation(xbc[:, i, :], xbc[:, i, :], ACT.Silu).then_inc(summed["conv1.silu"], 1)
            for n in range(ADA_FIRST):
                ada_act(act, n, ada_early)
            stage(act, "act", "ssd_in")
            for h in range(HEADS):
                act.wait_ge(*count("ssd.arg", h + 1))
                nc.scalar.activation(decay[:, h % 2], decay[:, h % 2], ACT.Exp).then_inc(summed["ssd.exp"], 1)
                ada_act(act, ADA_FIRST + h, ada_early)
            ada_act(act, ADA_FIRST + HEADS, ada_early)
            for c in range(4):
                act.wait_ge(*count("ssd.y_read", 4 + c + 1))
                nc.scalar.activation(mixed_sq(c), z_feat[:, c, :], ACT.Square).then_inc(summed["ssd.var_in"], 1)
            for g in range(2):
                act.wait_ge(*count("ssd.var", g + 1))
                nc.scalar.activation(rms1[:, g], bank(4 + g), ACT.Sqrt, bias=cst[:, C_EPS:C_EPS + 1],
                                     scale=1.0 / 256).then_inc(summed["ssd.root"], 1)
            stage(act, "act", "ssd")
            attention_act(act, "att1", att1_jobs(), probs1, probsT1, stat)
            stage(act, "act", "att1")
            attended_take(act, "att1", 1, ATT1)
            stage(act, "act", "att1t")
            normalise_roots(act, "out1", range(TL))
            stage(act, "act", "out1")
            transpose_take(act, "moe1.t", 1, range(TL), x_feat)
            stage(act, "act", "h1")
            moe_router_act(act, "moe1", MOE1)
            stage(act, "act", "route1")
            moe_blocks_act(act, "moe1", MOE1, Chunks(MOE1_AT))
            stage(act, "act", "experts1")
            normalise_roots(act, "moe1", range(TL))
            stage(act, "act", "combine1")
            transpose_take(act, "x2", 1, range(TA), x_feat, lambda t: col2[:, t // TL, 0, :], lambda t: col2[:, t // TL, 1, :])
            stage(act, "act", "x2")
            sigs = 0
            for j in range(len(IN2)):
                if j < 4:
                    act.wait_ge(*count("in2.ready", j + 1))
                    nc.scalar.activation(b_gate[:, j, :], pair(j), ACT.Sigmoid).then_inc(
                        summed[f"in2.read{j // 4}"], 1)
                    if j == 3:
                        act.drain().then_inc(summed["in2.sig"], 1)
                elif 8 <= j < 12:
                    act.wait_ge(*count("in2.ready", j + 1))
                    for dst, span in padded(yb_in, j - 8):
                        ins = nc.scalar.activation(dst, pair(j)[:, span], ACT.Copy)
                    ins.then_inc(summed[f"in2.read{j // 4}"], 1)
                    if j == 11:
                        act.drain().then_inc(summed["in2.sig"], 1)
                elif j >= 16:
                    act.wait_ge(*count("in2.ready", j + 1))
                    act.wait_ge(*count("in2.sig", 3))
                    nc.scalar.activation(b_gate[:, j - 16, :], pair(j), ACT.Copy).then_inc(
                        summed[f"in2.read{j // 4}"], 1)
            for n in range(12, 24):
                ada_act(act, n, ada_late)
            stage(act, "act", "in2")
            for i in range(4):
                act.wait_ge(*count("ca.sq", i + 1))
                if i >= 2:
                    act.wait_ge(*count("ca.mean", 4 + i - 1))
                nc.scalar.activation(cen2[:, i % 2], ya[:, i], ACT.Square).then_inc(summed["ca.mean_in"], 1)
            act.wait_ge(*count("ca.mean", 8))
            nc.scalar.activation(mean2, ps[:, 1024:1024 + SPAN], ACT.Sqrt, bias=cst[:, C_EPS:C_EPS + 1],
                                 scale=1.0 / 512).then_inc(summed["ca.root"], 1)
            for i in range(4):
                act.wait_ge(*count("ca.silu", i + 1))
                g, b = (fcol[:, FC[k] + i:FC[k] + i + 1] for k in ("a_ln_g", "a_ln_b"))
                for span, out in (((0, SEQ), (0, SEQ)), ((CTX_AT, SPAN), (SEQ, NTOK))):
                    nc.scalar.activation(x_feat[:, i, out[0]:out[1]], ya[:, i, span[0]:span[1]], ACT.Silu,
                                         bias=b, scale=g)
            stage(act, "act", "conv")
            normalise_roots(act, "out2", range(TA))
            stage(act, "act", "out2")
            stage(act, "act", "h2")
            transpose_take(act, "moe2.t", 1, range(TA), x_feat)
            stage(act, "act", "h2t")
            moe_router_act(act, "moe2", MOE2)
            stage(act, "act", "route2")
            moe_blocks_act(act, "moe2", MOE2, Chunks(MOE2_AT))
            stage(act, "act", "experts2")
            normalise_roots(act, "moe2", range(TA))
            stage(act, "act", "combine2")
            transpose_take(act, "x3", 1, range(TA), x_feat, lambda t: col3[:, t // TL, 0, :], lambda t: col3[:, t // TL, 1, :])
            stage(act, "act", "x3")
            linear_take(act, "in3", 1, [in3_take(False)] * len(IN3))
            stage(act, "act", "in3")
            act.wait_ge(*count("rope.sq", 1))
            for lo, hi, h0 in ((0, TL, 0), (TL, TA, 8)):
                ins = nc.scalar.activation(rr[:, lo:hi, h0:10], rr[:, lo:hi, h0:10], ACT.Sqrt,
                                           bias=cst[:, C_EPS + 1:C_EPS + 2], scale=1.0 / HD)
            act.drain().then_inc(summed["rope.root"], 1)
            for t in range(TA):
                act.wait_ge(*count("rope.turned", t + 1))
                b = 2 * (t % 2)
                if t < TL:
                    nc.scalar.activation(qc_feat[:, :, P * t:P * (t + 1)], bank(b).rearrange("p (c n) -> p c n", c=4),
                                         ACT.Copy)
                nc.scalar.activation(kc_feat[:, :, P * t:P * (t + 1)], bank(b + 1, 256).rearrange("p (c n) -> p c n", c=2),
                                     ACT.Copy)
                act.drain().then_inc(summed["rope.turned_read"], 1)
            stage(act, "act", "rope")
            attention_act(act, "att2", att2_jobs(), probs3, probsT3, stat)
            stage(act, "act", "att2")
            attended_take(act, "att2", 1, ATT2)
            stage(act, "act", "att2t")
            normalise_roots(act, "out3", range(TL))
            stage(act, "act", "out3")
            stage(act, "act", "h3")
            transpose_take(act, "moe3.t", 1, range(TL), x_feat)
            stage(act, "act", "h3t")
            moe_router_act(act, "moe3", MOE3)
            stage(act, "act", "route3")
            moe_blocks_act(act, "moe3", MOE3, Chunks(MOE3_AT))
            stage(act, "act", "experts3")
            normalise_roots(act, "moe3", range(TL))
            stage(act, "act", "combine3")

        @block.vector
        def _(dve):
            v = nc.vector
            stage(dve, "dve", "loaded")
            transpose_take(dve, "x0", 0, range(TL), x_feat)
            for i in range(8):
                v.memset(xbc_in[:, i, 0:3], 0.0)
            for what in (fcol[:, FC["b_in"] + 12:FC["b_in"] + 16], frow[:, RC["q_g"]:RC["q_g"] + HD]):
                v.tensor_scalar(what, what, ATT_SCALE, None, ALU.mult)
            stage(dve, "dve", "x1")
            dve.wait_ge(*count("in1.dtf", 1))
            raw = bank(7, 64).rearrange("p (t n) -> p t n", t=TL)
            v.tensor_tensor(dtf[:, :, :], raw, spread(frow[:, RC["dt_f_bias"]:RC["dt_f_bias"] + 16], 1, TL), ALU.add)
            dve.drain()
            v.tensor_scalar(dtf[:, :, 8:16], dtf[:, :, 8:16], -1.0, None, ALU.mult)
            dve.drain()
            v.tensor_scalar(dts[:, 0], dtf[:, :, :], 0.0, None, ALU.max)
            v.tensor_scalar(dts[:, 2], dtf[:, :, :], 0.0, None, ALU.min)
            dve.drain()
            v.scalar_tensor_tensor(dts[:, 1], dts[:, 0], -1.0, dts[:, 2], ALU.mult, ALU.add)
            dve.drain().then_inc(summed["in1.dt1"], 1)
            linear_take(dve, "in1", 0, [in1_take(True)] * len(IN1))
            dve.wait_ge(*count("in1.dt2", 1))
            v.tensor_tensor(dtf[:, :, :], dtf[:, :, :], dts[:, 1], ALU.mult)
            one = cum
            v.tensor_scalar(one, dts[:, 2], 1.0, None, ALU.is_equal)
            v.tensor_scalar(dts[:, 2], dts[:, 2], 1.0, 1e-30, ALU.subtract, ALU.max)
            dve.drain()
            v.tensor_tensor(one, one, dts[:, 1], ALU.mult)
            v.reciprocal(dts[:, 2], dts[:, 2])
            dve.drain()
            v.tensor_tensor(dtf[:, :, :], dtf[:, :, :], dts[:, 2], ALU.mult)
            dve.drain()
            v.tensor_tensor(dtf[:, :, :], dtf[:, :, :], one, ALU.add)
            dve.drain()
            v.tensor_tensor(dts[:, 0], dts[:, 0], dtf[:, :, :], ALU.add)
            dve.drain()
            v.scalar_tensor_tensor(dtf[:, :, 0:8], dts[:, 0, :, 0:8], -1.0, spread(a_row, 1, TL), ALU.mult, ALU.mult)
            v.tensor_scalar(dtf[:, :, 8:16], dts[:, 0, :, 8:16], -1.0, None, ALU.mult)
            stage(dve, "dve", "in1")
            dve.wait_ge(*count("in1.cum", 1))
            v.tensor_copy(cum, bank(0, 64).rearrange("p (t n) -> p t n", t=TL))
            dve.drain().then_inc(summed["in1.cumd"], 1)
            dve.wait_ge(*count("in1.cumt", 1))
            v.tensor_copy(cum_row[0:16, :], bank(1)[0:16, :])
            v.tensor_scalar(fneg_row[0:16, :], bank(1)[0:16, :], -1.0, None, ALU.mult)
            for i in range(8):
                col = lambda k: fcol[:, FC["conv_w"] + 4 * i + k:FC["conv_w"] + 4 * i + k + 1]
                v.tensor_scalar(xbc[:, i, :], xbc_in[:, i, 0:SEQ], col(0), fcol[:, FC["conv_b"] + i:FC["conv_b"] + i + 1],
                                ALU.mult, ALU.add)
                for k in range(1, 4):
                    dve.drain()
                    ins = v.scalar_tensor_tensor(xbc[:, i, :], xbc_in[:, i, k:k + SEQ], col(k), xbc[:, i, :],
                                                 ALU.mult, ALU.add)
                ins.then_inc(summed["conv1.acc"], 1)
            for g in range(2):
                for s in range(TL):
                    dve.wait_ge(*count("ssd.cb", 4 * g + s + 1))
                    n = SEQ - P * s
                    at = TRI_AT[s]
                    v.tensor_tensor(cb[:, g, at:at + P], bank(2 + s, P), tri, ALU.mult)
                    if n > P:
                        v.tensor_copy(cb[:, g, at + P:at + n], bank(2 + s, n)[:, P:])
                    dve.drain().then_inc(summed["ssd.cbd"], 1)
            for t in range(TL):
                dve.wait_ge(*count("ssd.xs", t + 1))
                v.tensor_tensor(xdt_tok[:, t, :].rearrange("p (h e) -> p h e", h=HEADS),
                                bank(6 + t % 2).rearrange("p (h e) -> p h e", h=HEADS),
                                spread(dts[:, 0, t, 0:8], 2, HD), ALU.mult).then_inc(summed["ssd.xsd"], 1)
            stage(dve, "dve", "ssd_in")
            for step in range(HEADS + 1):
                if step < HEADS:
                    h = step
                    dve.wait_ge(*count("ssd.row", h + 1))
                    if h >= 2:
                        dve.wait_ge(*count("ssd.mix", h - 1))
                    for s in range(TL):
                        at = TRI_AT[s]
                        v.tensor_scalar(decay[:, h % 2, at:at + SEQ - P * s], bank(h % 2)[:, P * s:SEQ],
                                        cum[:, s, h:h + 1], 0.0, ALU.subtract, ALU.min)
                    dve.drain().then_inc(summed["ssd.arg"], 1)
                if step >= 1:
                    h = step - 1
                    dve.wait_ge(*count("ssd.exp", h + 1))
                    if h >= 2:
                        dve.wait_ge(*count("ssd.y", h - 1))
                    v.tensor_tensor(mixed[:, h % 2], decay[:, h % 2], cb[:, h // 4], ALU.mult).then_inc(
                        summed["ssd.mix"], 1)
                if step >= 2 and step % 2 == 0:
                    c = (step - 2) // 2
                    dve.wait_ge(*count("ssd.y", 2 * c + 2))
                    v.scalar_tensor_tensor(xbc[:, c, :], xbc[:, c, :], fcol[:, FC["d_skip"] + c:FC["d_skip"] + c + 1],
                                           bank(2 + c % 2), ALU.mult, ALU.add).then_inc(summed["ssd.y_read"], 1)
            dve.drain()
            for c in range(4):
                v.tensor_tensor(z_feat[:, c, :], z_feat[:, c, :], xbc[:, c, :], ALU.mult).then_inc(summed["ssd.y_read"], 1)
            dve.drain()
            for g in range(2):
                dve.wait_ge(*count("ssd.root", g + 1))
                v.reciprocal(rms1[:, g], rms1[:, g])
                dve.drain()
                for c in (2 * g, 2 * g + 1):
                    v.scalar_tensor_tensor(x_feat[:, c, 0:SEQ], z_feat[:, c, :],
                                           fcol[:, FC["norm_g"] + c:FC["norm_g"] + c + 1], rms1[:, g], ALU.mult, ALU.mult)
            stage(dve, "dve", "ssd")
            attention_dve(dve, "att1", att1_jobs(), stat)
            stage(dve, "dve", "att1")
            attended_take(dve, "att1", 0, ATT1)
            stage(dve, "dve", "att1t")
            out_proj_dve(dve, "out1", range(TL), ALPHA_1, None, rows[:, 0], rows[:, 1])
            stage(dve, "dve", "out1")
            transpose_take(dve, "moe1.t", 0, range(TL), x_feat)
            stage(dve, "dve", "h1")
            moe_router_dve(dve, "moe1", MOE1, frow[:, RC["router1_b"]:RC["router1_b"] + 20])
            stage(dve, "dve", "route1")
            moe_blocks_dve(dve, "moe1", MOE1, Chunks(MOE1_AT))
            stage(dve, "dve", "experts1")
            moe_combine_dve(dve, "moe1", MOE1, ALPHA_1, None, rows[:, 0], rows[:, 1])
            stage(dve, "dve", "combine1")
            transpose_take(dve, "x2", 0, range(TA), x_feat, lambda t: col2[:, t // TL, 0, :], lambda t: col2[:, t // TL, 1, :])
            for buf in (ya_in, yb_in):
                v.memset(buf[:, :, :], 0.0)
            stage(dve, "dve", "x2")
            for j in range(4, 8):
                if j == 4:
                    dve.wait_ge(*count("in2.sig", 1))
                dve.wait_ge(*count("in2.ready", j + 1))
                for dst, span in padded(ya_in, j - 4):
                    ins = v.tensor_tensor(dst, pair(j)[:, span], b_gate[:, j - 4, span], ALU.mult)
                ins.then_inc(summed[f"in2.read{j // 4}"], 1)
            for j in range(12, 16):
                if j == 12:
                    dve.wait_ge(*count("in2.sig", 2))
                    dve.drain().then_inc(summed["in2.sig"], 1)
                dve.wait_ge(*count("in2.ready", j + 1))
                for dst, span in padded(yb_in, j - 12):
                    ins = v.tensor_tensor(dst, pair(j)[:, span], dst, ALU.mult)
                ins.then_inc(summed[f"in2.read{j // 4}"], 1)
            dve.drain()
            for i in range(4):
                col = lambda k: fcol[:, FC["a_dw_w"] + CONV_A_W * i + k:FC["a_dw_w"] + CONV_A_W * i + k + 1]
                v.tensor_scalar(ya[:, i], ya_in[:, i, 0:SPAN], col(0), fcol[:, FC["a_dw_b"] + i:FC["a_dw_b"] + i + 1],
                                ALU.mult, ALU.add)
                for k in range(1, CONV_A_W):
                    dve.drain()
                    v.scalar_tensor_tensor(ya[:, i], ya_in[:, i, k:k + SPAN], col(k), ya[:, i], ALU.mult, ALU.add)
                colb = lambda k: fcol[:, FC["b_dw_w"] + 3 * i + k:FC["b_dw_w"] + 3 * i + k + 1]
                v.tensor_scalar(yb[:, i], yb_in[:, i, PAD - 1:PAD - 1 + SPAN], colb(0), None, ALU.mult)
                for k in (1, 2):
                    dve.drain()
                    v.scalar_tensor_tensor(yb[:, i], yb_in[:, i, PAD - 1 + k:PAD - 1 + k + SPAN], colb(k), yb[:, i],
                                           ALU.mult, ALU.add)
            stage(dve, "dve", "in2")
            dve.sem_inc(summed["ca.mean_in"], 4)
            for i in range(4):
                for (lo, hi), (t0, t1) in (((0, SEQ), (0, SEQ)), ((CTX_AT, SPAN), (SEQ, NTOK))):
                    v.tensor_tensor(x_feat[:, 4 + i, t0:t1], yb[:, i, lo:hi], b_gate[:, i, t0:t1], ALU.mult)
            dve.wait_ge(*count("ca.mean", 4))
            for i in range(4):
                v.scalar_tensor_tensor(ya[:, i], ps[:, 0:SPAN], -1.0 / 512, ya[:, i], ALU.mult, ALU.add).then_inc(
                    summed["ca.sq"], 1)
            dve.wait_ge(*count("ca.root", 1))
            v.reciprocal(mean2, mean2)
            dve.drain()
            for i in range(4):
                v.tensor_tensor(ya[:, i], ya[:, i], mean2, ALU.mult).then_inc(summed["ca.silu"], 1)
            stage(dve, "dve", "conv")
            out_proj_dve(dve, "out2", range(TA), ALPHA_2, lambda t: rows[:, 2 + t // TL], rows[:, 0], rows[:, 1])
            stage(dve, "dve", "out2")
            dve.wait_ge(params_here, params["h2"])
            for t in range(TA):
                v.scalar_tensor_tensor(h_tok[:, t, :], rows[:, 2 + t // TL], 1.0, x_tok[:, t, :], ALU.add, ALU.mult)
            dve.drain()
            for t in range(TA):
                v.tensor_tensor(h_tok[:, t, :], h_tok[:, t, :], rows[:, 4 + t // TL], ALU.add)
            stage(dve, "dve", "h2")
            transpose_take(dve, "moe2.t", 0, range(TA), x_feat)
            stage(dve, "dve", "h2t")
            moe_router_dve(dve, "moe2", MOE2, frow[:, RC["router2_b"]:RC["router2_b"] + 36])
            stage(dve, "dve", "route2")
            moe_blocks_dve(dve, "moe2", MOE2, Chunks(MOE2_AT))
            stage(dve, "dve", "experts2")
            moe_combine_dve(dve, "moe2", MOE2, ALPHA_2, lambda t: rows[:, 2 + t // TL], rows[:, 0], rows[:, 1])
            stage(dve, "dve", "combine2")
            transpose_take(dve, "x3", 0, range(TA), x_feat, lambda t: col3[:, t // TL, 0, :], lambda t: col3[:, t // TL, 1, :])
            stage(dve, "dve", "x3")
            linear_take(dve, "in3", 0, [in3_take(True)] * len(IN3))
            stage(dve, "dve", "in3")
            for t in range(TA):
                h0 = 0 if t < TL else 8
                n = 10 - h0
                sqv = sq3[:, 0:n * HD].rearrange("p (h e) -> p h e", h=n)
                v.tensor_tensor(sqv, qk_tok[:, t, h0:10, :], qk_tok[:, t, h0:10, :], ALU.mult)
                dve.drain()
                v.tensor_reduce(rr[:, t, h0:10], sqv, axis=AX.X, op=ALU.add)
                dve.drain()
            dve.drain().then_inc(summed["rope.sq"], 1)
            dve.wait_ge(*count("rope.root", 1))
            for lo, hi, h0 in ((0, TL, 0), (TL, TA, 8)):
                v.reciprocal(rr[:, lo:hi, h0:10], rr[:, lo:hi, h0:10])
            dve.drain()
            for t in range(TA):
                h0 = 0 if t < TL else 8
                x = qk_tok[:, t, h0:10, :]
                v.tensor_tensor(x, x, spread(rr[:, t, h0:10], 2, HD), ALU.mult)
                dve.drain()
                if t < TL:
                    v.tensor_tensor(qk_tok[:, t, 0:8, :], qk_tok[:, t, 0:8, :],
                                    spread(frow[:, RC["q_g"]:RC["q_g"] + HD], 1, 8), ALU.mult)
                v.tensor_tensor(qk_tok[:, t, 8:10, :], qk_tok[:, t, 8:10, :],
                                spread(frow[:, RC["k_g"]:RC["k_g"] + HD], 1, 2), ALU.mult)
                dve.drain()
                if t < TL:
                    for axis in range(2):
                        x1 = qk_tok[:, t, :, 32 * axis:32 * axis + 16]
                        x2 = qk_tok[:, t, :, 32 * axis + 16:32 * axis + 32]
                        cos = spread(rope_cs[:, t, 0, 16 * axis:16 * axis + 16], 1, 10)
                        sin = spread(rope_cs[:, t, 1, 16 * axis:16 * axis + 16], 1, 10)
                        a = [rp[:, k, 0:160].rearrange("p (h e) -> p h e", h=10) for k in range(4)]
                        v.tensor_tensor(a[0], x1, cos, ALU.mult)
                        v.tensor_tensor(a[1], x2, sin, ALU.mult)
                        v.tensor_tensor(a[2], x1, sin, ALU.mult)
                        v.tensor_tensor(a[3], x2, cos, ALU.mult)
                        dve.drain()
                        v.tensor_tensor(x1, a[0], a[1], ALU.subtract)
                        v.tensor_tensor(x2, a[2], a[3], ALU.add)
                        dve.drain()
                if t >= 2:
                    dve.wait_ge(*count("rope.turned", t - 1))
                kd = kdup_of(t).rearrange("p (h two e) -> p h two e", h=2, two=2)
                for two in range(2):
                    v.tensor_copy(kd[:, :, two, :], qk_tok[:, t, 8:10, :])
                dve.drain().then_inc(summed["rope.done"], 1)
            stage(dve, "dve", "rope")
            attention_dve(dve, "att2", att2_jobs(), stat)
            stage(dve, "dve", "att2")
            attended_take(dve, "att2", 0, ATT2)
            stage(dve, "dve", "att2t")
            out_proj_dve(dve, "out3", range(TL), ALPHA_2, lambda t: rows[:, 2], rows[:, 0], rows[:, 1])
            stage(dve, "dve", "out3")
            dve.wait_ge(params_here, params["h3"])
            for t in range(TL):
                v.scalar_tensor_tensor(h_tok[:, t, :], rows[:, 2], 1.0, x_tok[:, t, :], ALU.add, ALU.mult)
            dve.drain()
            for t in range(TL):
                v.tensor_tensor(h_tok[:, t, :], h_tok[:, t, :], rows[:, 4], ALU.add)
            stage(dve, "dve", "h3")
            transpose_take(dve, "moe3.t", 0, range(TL), x_feat)
            stage(dve, "dve", "h3t")
            moe_router_dve(dve, "moe3", MOE3, frow[:, RC["router2_b"] + 36:RC["router2_b"] + 72])
            stage(dve, "dve", "route3")
            moe_blocks_dve(dve, "moe3", MOE3, Chunks(MOE3_AT))
            stage(dve, "dve", "experts3")
            moe_combine_dve(dve, "moe3", MOE3, ALPHA_2, lambda t: rows[:, 2], rows[:, 0], rows[:, 1])
            stage(dve, "dve", "combine3")

        @block.gpsimd
        def _(pool):
            sent = [0]

            def load(out, in_, by_element=False):
                sent[0] += 16
                pool.dma_start(out, in_, allow_slow_non_contiguous=by_element).then_inc(loads, 16)

            def loaded():
                pool.wait_ge(loads, sent[0])

            def load_rows(*pairs):
                for i, row in pairs:
                    load(rows[:, i, :], row.partition_broadcast(P))

            def mod(layer, cond, part):
                return d["mods"][cond, (6 * layer + part) * D:(6 * layer + part + 1) * D]

            def load_columns_of_mods(dest, layer):
                for cond in range(2):
                    for what, part in ((0, 1), (1, 0)):
                        load(dest[:, cond, what, :], mod(layer, cond, part).rearrange("(k p) -> p k", p=P), True)

            def load_router(m, parts):
                at = 0
                for w in parts:
                    n = w.shape[-1]
                    load(moe_arrays(m)["wr"][:, :, at:at + n], w.rearrange("(k p) n -> p k n", p=P))
                    at += n

            load(cst[:, :], d["consts"])
            load(fcol[:, :], d["fcols"])
            load(frow[:, :], d["frows"].partition_broadcast(P))
            load(x_tok[:, 0:TL, :], d["x"].rearrange("(t p) e -> p t e", p=P))
            load(x_tok[:, TL:TA, :], d["ctx"].rearrange("(t p) e -> p t e", p=P))
            load(w_dtf[:, :, 0:8], d["w_in"][:, 1536:1544].rearrange("(k p) n -> p k n", p=P))
            load(w_dtf[:, :, 8:16], d["w_in"][:, 3080:3088].rearrange("(k p) n -> p k n", p=P))
            load(v_bias[0:1, :], d["b_v"])
            nc.gpsimd.memset(fill[:, 0, :], 0.0)
            nc.gpsimd.memset(fill[:, 1, :], NEG)
            loaded()
            stage(pool, "pool", "loaded")
            stage(pool, "pool", "x1")
            for what in ("xs", "ys"):
                for b in range(XS_BLOCKS):
                    pool.dma_start(d[what][P * b:P * (b + 1), :].rearrange("p (a n) -> p a n", n=256),
                                   spread(fill[:, 0, :], 1, 4)).then_inc(filled, 16)
            for b in range(4):
                pool.dma_start(d["g"][:, 1920 * b:1920 * (b + 1)].rearrange("c (a n) -> c a n", n=240),
                               spread(fill[0:64, 1, 0:240], 1, 8)).then_inc(filled, 16)
            for cond in range(2):
                pool.dma_start(d["mods"][cond, :], d["ada_b"].rearrange("l n -> (l n)")).then_inc(filled, 16)
            stage(pool, "pool", "in1")
            pool.wait_ge(filled, 16 * (2 * XS_BLOCKS + 6))
            for n in range(ADA_FIRST):
                ada_pool(pool, n, ada_early)
            stage(pool, "pool", "ssd_in")
            for n in range(ADA_FIRST, 12):
                ada_pool(pool, n, ada_early)
            for i in range(2):
                pool.wait_ge(*count(f"ada.sent{i}", 96))
            stage(pool, "pool", "ssd")
            rb = d["rel_bias"]
            for c in list(range(8)) + list(range(57, 64)):
                w0 = 0 if c < 8 else HD - 16
                load(d["g"][c].rearrange("(a n) -> a n", n=HD)[:, w0:w0 + 16], rb[:, w0 - c + 15:w0 - c + 31])
            for c in range(8, 57):
                load(d["g"][c].rearrange("(a n) -> a n", n=HD)[:, c - 8:c + 8], rb[:, 7:23])
                if c % 8 == 0:
                    loaded()
            loaded()
            stage(pool, "pool", "att1")
            stage(pool, "pool", "att1t")
            load_rows((0, d["ln"][0]), (1, d["ln"][1]))
            load_router(MOE1, [d["rg_w"]] + [d["re_w"][g] for g in range(4)])
            loaded()
            pool.sem_inc(params_here, 1)
            stage(pool, "pool", "out1")
            stage(pool, "pool", "h1")
            moe_scatter(pool, "moe1", MOE1, x_tok)
            stage(pool, "pool", "route1")
            load_rows((0, d["ln"][2]), (1, d["ln"][3]))
            load_columns_of_mods(col2, 0)
            moe_blocks_pool(pool, "moe1", MOE1)
            loaded()
            nc.gpsimd.tensor_scalar(col2[:, :, 0, :], col2[:, :, 0, :], 1.0, None, ALU.add)
            stage(pool, "pool", "experts1")
            moe_gather_pool(pool, "moe1", MOE1)
            stage(pool, "pool", "combine1")
            stage(pool, "pool", "x2")
            for n in range(12, 24):
                ada_pool(pool, n, ada_late)
            for i in range(2):
                pool.wait_ge(*count(f"ada.sent{i}", 192))
            stage(pool, "pool", "in2")
            stage(pool, "pool", "conv")
            load_rows((0, d["ln"][4]), (1, d["ln"][5]), (2, mod(0, 0, 2)), (3, mod(0, 1, 2)),
                      (4, mod(0, 0, 3)), (5, mod(0, 1, 3)))
            load_router(MOE2, [d["router_w1"][0], d["router_w2"][0]])
            loaded()
            pool.sem_inc(params_here, 1)
            stage(pool, "pool", "out2")
            load_rows((2, mod(0, 0, 4)), (3, mod(0, 1, 4)))
            loaded()
            pool.sem_inc(params_here, 1)
            stage(pool, "pool", "h2")
            stage(pool, "pool", "h2t")
            moe_scatter(pool, "moe2", MOE2, h_tok)
            stage(pool, "pool", "route2")
            load_rows((0, d["ln"][6]), (1, d["ln"][7]), (2, mod(0, 0, 5)), (3, mod(0, 1, 5)))
            load_columns_of_mods(col3, 1)
            moe_blocks_pool(pool, "moe2", MOE2)
            loaded()
            nc.gpsimd.tensor_scalar(col3[:, :, 0, :], col3[:, :, 0, :], 1.0, None, ALU.add)
            stage(pool, "pool", "experts2")
            moe_gather_pool(pool, "moe2", MOE2)
            stage(pool, "pool", "combine2")
            stage(pool, "pool", "x3")
            load(rope_cs, d["rope"].rearrange("(t p) a n -> p t a n", p=P))
            loaded()
            stage(pool, "pool", "in3")
            stage(pool, "pool", "rope")
            for h in range(HEADS):
                if h >= 2:
                    pool.wait_ge(*count("rope.g_free", h - 1))
                src = d["g"][:, 960 * h:960 * (h + 1)].rearrange("c (r n) -> c r n", n=HD)
                pool.dma_start(g_bias[0:64, h % 2, 0:15, :], src).then_inc(summed[f"rope.g_here{h % 2}"], 16)
                pool.dma_start(g_bias[64:128, h % 2, 1:16, :], src).then_inc(summed[f"rope.g_here{h % 2}"], 16)
            stage(pool, "pool", "att2")
            stage(pool, "pool", "att2t")
            load_rows((0, d["ln"][8]), (1, d["ln"][9]), (2, mod(1, 0, 2)), (4, mod(1, 0, 3)))
            load_router(MOE3, [d["router_w1"][1], d["router_w2"][1]])
            loaded()
            pool.sem_inc(params_here, 1)
            stage(pool, "pool", "out3")
            load_rows((2, mod(1, 0, 4)))
            loaded()
            pool.sem_inc(params_here, 1)
            stage(pool, "pool", "h3")
            stage(pool, "pool", "h3t")
            moe_scatter(pool, "moe3", MOE3, h_tok)
            stage(pool, "pool", "route3")
            load_rows((0, d["ln"][10]), (1, d["ln"][11]), (2, mod(1, 0, 5)))
            moe_blocks_pool(pool, "moe3", MOE3)
            loaded()
            stage(pool, "pool", "experts3")
            moe_gather_pool(pool, "moe3", MOE3)
            stage(pool, "pool", "combine3")
            load(d["out"].rearrange("(t p) e -> p t e", p=P), x_tok[:, 0:TL, :])
            loaded()


def tables():
    c = np.zeros((P, C_COUNT), np.float32)
    r, n = np.arange(P)[:, None], np.arange(P)[None, :]
    c[:, C_ID:C_ID + P] = r == n
    c[:, C_TRI:C_TRI + P] = r <= n
    c[:, C_TRIS:C_TRIS + P] = r < n
    c[:, C_ONE:C_ONE + P] = 1.0
    c[:, C_MASK:C_MASK + P] = np.where(n > r, NEG, 0.0)
    c[:, C_IOTA:C_IOTA + 48] = np.arange(48)
    c[:, C_EPS] = EPS
    c[:, C_EPS + 1] = EPS_RMS
    t = np.arange(SEQ)
    inv = (10000.0 ** (-np.arange(0, 32, 2, dtype=np.float32) / 32)).astype(np.float32)
    row = (t // 64).astype(np.float32)[:, None] * inv
    col = (t % 64).astype(np.float32)[:, None] * inv
    angles = np.concatenate([row, col], axis=1)
    rope = np.stack([np.cos(angles), np.sin(angles)], axis=1).astype(np.float32)
    return c, rope


def kernel(**inputs):
    import concourse.bacc as bacc
    from concourse.bass_utils import run_bass_kernel_spmd as run

    a = {k: np.ascontiguousarray(v) for k, v in inputs.items()}

    def cols(v):
        return v.reshape(-1, P).T

    def taps(w):
        return w.reshape(w.shape[0], -1, P).transpose(2, 1, 0).reshape(P, -1)

    b = a["b_in"][0]
    b_feat = np.concatenate([b[0:1536], b[1544:2568], b[2568:3080]])
    cond = np.stack([cols(a["c_2"][0]), cols(a["c_ctx_2"])], axis=2).reshape(P, -1)
    fcols = np.concatenate([
        cols(b_feat), taps(a["conv_w"][0]), cols(a["conv_b"][0]), cols(np.repeat(a["d_skip"][0], HD)),
        cols(a["ssd_norm_g"][0]), taps(a["conv_a_dw_w_2"][0]), cols(a["conv_a_dw_b_2"][0]), cols(a["conv_a_ln_g_2"][0]),
        cols(a["conv_a_ln_b_2"][0]), taps(a["conv_b_dw_w_2"][0]), cond], axis=1)
    frows = np.concatenate([
        b[1536:1544], b[3080:3088], a["a_log"][0], a["router_group_b"][0], a["router_expert_b"][0].reshape(-1),
        a["router_b1_2"][0], a["router_b2_2"][0], a["router_b1_2"][1], a["router_b2_2"][1],
        a["q_norm_g_2"][0], a["k_norm_g_2"][0]])
    ln = [a[k][0] for k in ("ln1_g", "ln1_b", "ln2_g", "ln2_b")]
    ln += [a[k + "_2"][i] for i in range(2) for k in ("ln1_g", "ln1_b", "ln2_g", "ln2_b")]
    consts, rope = tables()
    arrays = {
        "consts": consts, "rope": rope, "fcols": fcols, "frows": frows, "ln": np.stack(ln),
        "x": a["x"][0], "ctx": a["ctx_2"][0], "w_in": a["w_in"][0], "b_v": b[2568:3080].reshape(1, 512),
        "w_out": a["w_out"][0], "rg_w": a["router_group_w"][0], "re_w": a["router_expert_w"][0],
        "w_gate": a["w_gate"][0], "w_up": a["w_up"][0], "w_down": a["w_down"][0],
        "ada_w": a["ada_w_2"], "ada_b": a["ada_b_2"], "conv_w_in": a["conv_w_in_2"][0], "conv_w_out": a["conv_w_out_2"][0],
        "attn_w_in": a["attn_w_in_2"][0], "attn_w_out": a["attn_w_out_2"][0],
        "rel_bias": a["na_rel_bias_2"][0].reshape(120, 31), "router_w1": a["router_w1_2"], "router_w2": a["router_w2_2"],
        "e_gate": a["expert_w_gate_2"], "e_up": a["expert_w_up_2"], "e_down": a["expert_w_down_2"],
    }
    nc = bacc.Bacc("TRN2", target_bir_lowering=False, num_devices=1)
    ins, d = {}, {}
    for name, v in arrays.items():
        ins[f"in_{name}"] = np.ascontiguousarray(v)
        d[name] = nc.dram_tensor(f"in_{name}", v.shape, F32, kind="ExternalInput").ap()
    d["out"] = nc.dram_tensor("out", (SEQ, D), F32, kind="ExternalOutput").ap()
    rows = P * (Moe(TA, 4, 8).blocks + 2)
    d["xs"] = nc.dram_tensor("expert_rows", (rows, D), F32, kind="Internal").ap()
    d["ys"] = nc.dram_tensor("expert_outputs", (rows, D), F32, kind="Internal").ap()
    d["g"] = nc.dram_tensor("window_bias", (HD, 120 * HD), F32, kind="Internal").ap()
    d["mods"] = nc.dram_tensor("modulations", (2, 12 * D), F32, kind="Internal").ap()
    build(nc, d)
    r = run(nc, [ins], core_ids=[0])
    return r.results[0]["out"].reshape(1, SEQ, D)
```

```python
from contextlib import ExitStack

import numpy as np

import concourse.bass as bass
from concourse import mybir

F32 = mybir.dt.float32
I32 = mybir.dt.int32
ALU = mybir.AluOpType
ACT = mybir.ActivationFunctionType
AX = mybir.AxisListType

P = 128
D = 1024
KT = D // P
SEQ, CTX = 512, 256
TL, TC = SEQ // P, CTX // P
TA = TL + TC
NTOK = SEQ + CTX
HEADS, HD = 8, 64
FF = 512
CONV_A_W = 31
PAD = CONV_A_W // 2
CTX_AT = SEQ + PAD
SPAN = CTX_AT + CTX
PADDED = SPAN + 2 * PAD
NEG = -1.0e30
ATT_SCALE = HD ** -0.5
ALPHA_1 = 2.0 ** 0.25
ALPHA_2 = 4.0 ** 0.25
EPS = 1e-5
EPS_RMS = 1e-6
RING = 4
SLOT = 4096

C_ID, C_TRI, C_TRIS, C_ONE, C_MASK = 0, 128, 256, 384, 512
C_IOTA = 640
C_EPS = 688
C_COUNT = 690

FC = {}
_at = 0
for _n, _w in (("b_in", 24), ("conv_w", 32), ("conv_b", 8), ("d_skip", 4), ("norm_g", 4), ("a_dw_w", 4 * CONV_A_W),
               ("a_dw_b", 4), ("a_ln_g", 4), ("a_ln_b", 4), ("b_dw_w", 12), ("cond", 16)):
    FC[_n] = _at
    _at += _w
FC_COUNT = _at
RC = {}
_at = 0
for _n, _w in (("dt_f_bias", 16), ("a_log", 8), ("router1_b", 20), ("router2_b", 72), ("q_g", 64), ("k_g", 64)):
    RC[_n] = _at
    _at += _w
RC_COUNT = _at


class Moe:

    def __init__(self, tiles, groups, per_group):
        self.T, self.G, self.EP = tiles, groups, per_group
        self.E = groups * per_group
        most = self.E + (tiles * P * 2 - self.E) // P
        self.blocks = -(-(most + 1) // 4) * 4


def spread(ap, axis, n):
    wide = ap.unsqueeze(axis)
    shape = list(wide.shape)
    shape[axis] = n
    return wide.broadcast_to(shape)


def build(nc, d):
    es = ExitStack()
    with es:
        def sb(name, shape, dt=F32):
            return es.enter_context(nc.sbuf_tensor(name, shape, dt))

        def sem(name):
            return es.enter_context(nc.semaphore(name))

        w_ring = sb("w_ring", [P, RING, SLOT])
        x_tok = sb("x_tok", [P, TA, D])
        x_feat = sb("x_feat", [P, KT, NTOK])
        cst = sb("cst", [P, C_COUNT])
        fcol = sb("fcol", [P, FC_COUNT])
        frow = sb("frow", [P, RC_COUNT])
        ARENA = 23010
        arena = sb("arena", [P, ARENA])
        ps = es.enter_context(nc.psum_tensor("ps", [P, 8 * 512], F32))

        def bank(i, n=512):
            return ps[:, 512 * i:512 * i + n]

        def region(at, *shape):
            n = int(np.prod(shape))
            assert at + n <= ARENA, (at, n, ARENA)
            flat = arena[:, at:at + n]
            if len(shape) == 1:
                return flat
            names = "abcd"[:len(shape)]
            return flat.rearrange(f"p ({' '.join(names)}) -> p {' '.join(names)}",
                                  **{k: v for k, v in zip(names[1:], shape[1:])})

        ident = cst[:, C_ID:C_ID + P]
        tri = cst[:, C_TRI:C_TRI + P]
        tri_strict = cst[:, C_TRIS:C_TRIS + P]
        ones = cst[:, C_ONE:C_ONE + P]
        causal = cst[:, C_MASK:C_MASK + P]

        stage_passed = sem("stage_passed")
        w_landed = [sem(f"w_landed{i}") for i in range(RING)]
        w_free = sem("w_free")
        passed = {"pe": [], "act": [], "dve": [], "pool": []}

        def stage(eng, who, name):
            passed[who].append(name)
            eng.drain().then_inc(stage_passed, 1)
            eng.wait_ge(stage_passed, 4 * len(passed[who]))

        class Chunks:
            def __init__(self, n=0):
                self.n = n

            def take(self):
                n = self.n
                self.n += 1
                return n

        def chunk_view(slot, n, k=KT):
            return w_ring[:, slot, 0:k * n].rearrange("p (k n) -> p k n", n=n)

        def load_columns(sp, chunks, w, c0, n):
            c = chunks.take()
            if c >= RING:
                sp.wait_ge(w_free, c - RING + 1)
            sp.dma_start(chunk_view(c % RING, n), w[:, c0:c0 + n].rearrange("(k p) n -> p k n", p=P)
                         ).then_inc(w_landed[c % RING], 16)

        def await_chunk(pe, c):
            pe.wait_ge(w_landed[c % RING], 16 * (c // RING + 1))

        params_here = sem("params_here")
        params = {"out1": 1, "out2": 2, "h2": 3, "out3": 4, "h3": 5}

        summed = {}

        start = {}

        def new_sems(name, *parts):
            for p in parts:
                summed[f"{name}.{p}"] = sem(f"{name}_{p}")
                start[f"{name}.{p}"] = 0

        def count(key, value):
            return summed[key], value + start[key]

        PAIRS = 4

        def pair(j, n=NTOK):
            at = (j % PAIRS) * 1024
            return ps[:, at:at + n]

        def by_parity(name):
            return lambda j: count(f"{name}.read{j % 2}", j // 2 + 1)

        def linear_pe(pe, name, jobs, chunks, reader):
            c = None
            for j, (first, last, products) in enumerate(jobs):
                if first:
                    c = chunks.take()
                    await_chunk(pe, c)
                if j >= PAIRS:
                    pe.wait_ge(*reader(j - PAIRS))
                mm = products(j, c % RING)
                mm.then_inc(summed[f"{name}.ready"], 1)
                if last:
                    pe.drain().then_inc(w_free, 1)

        def linear_take(eng, name, parity, takes):
            for j, take in enumerate(takes):
                if j % 2 != parity:
                    continue
                eng.wait_ge(*count(f"{name}.ready", j + 1))
                take(j).then_inc(summed[f"{name}.read{parity}"], 1)

        def feature_products(c0, tokens, halves=True, n=512):
            def products(j, slot):
                w = chunk_view(slot, n)
                for t0 in range(0, tokens, 512):
                    t1 = min(t0 + 512, tokens)
                    for k in range(KT):
                        mm = nc.tensor.matmul(pair(j)[:, t0:t1], w[:, k, c0:c0 + P], x_feat[:, k, t0:t1],
                                              start=k == 0, stop=k == KT - 1)
                return mm
            return products

        def token_products(tile, n, bias=None):
            def products(j, slot):
                w = chunk_view(slot, n)
                for k in range(KT):
                    mm = nc.tensor.matmul(pair(j, n), x_feat[:, k, P * tile:P * (tile + 1)], w[:, k, :],
                                          start=k == 0, stop=k == KT - 1 and bias is None)
                if bias is not None:
                    mm = nc.tensor.matmul(pair(j, n), ones[0:1, :], bias, start=False, stop=True)
                return mm
            return products

        def transpose_pe(pe, name, tiles, source=None):
            j = 0
            for t in tiles:
                for half in range(2):
                    if j >= 8:
                        pe.wait_ge(*count(f"{name}.read{j % 2}", (j - 8) // 2 + 1))
                    for q in range(4):
                        k = 4 * half + q
                        src = (source or x_tok)[:, t, P * k:P * (k + 1)]
                        mm = nc.tensor.transpose(bank(j % 8)[:, P * q:P * (q + 1)], src, ident)
                    mm.then_inc(summed[f"{name}.ready"], 1)
                    j += 1

        def transpose_take(eng, name, parity, tiles, dest, scale=None, shift=None):
            j = 0
            for t in tiles:
                for half in range(2):
                    if j % 2 == parity:
                        eng.wait_ge(*count(f"{name}.ready", j + 1))
                        src = bank(j % 8).rearrange("p (q n) -> p q n", q=4)
                        if scale is None:
                            out = dest[:, 4 * half:4 * half + 4, P * t:P * (t + 1)]
                            if parity:
                                ins = nc.scalar.activation(out, src, ACT.Copy)
                            else:
                                ins = nc.vector.tensor_copy(out, src)
                        else:
                            for q in range(4):
                                k = 4 * half + q
                                out = dest[:, k, P * t:P * (t + 1)]
                                sc, sh = scale(t)[:, k:k + 1], shift(t)[:, k:k + 1]
                                if parity:
                                    ins = nc.scalar.activation(out, src[:, q, :], ACT.Identity, bias=sh, scale=sc)
                                else:
                                    ins = nc.vector.tensor_scalar(out, src[:, q, :], sc, sh, ALU.mult, ALU.add)
                        ins.then_inc(summed[f"{name}.read{parity}"], 1)
                    j += 1

        ln_stats = sb("ln_stats", [P, TA, 16])

        def normalise(dve, name, i, t, g, b):
            s = ln_stats[:, t, :]
            x = x_tok[:, t, :]
            for half in range(2):
                nc.vector.bn_stats(s[:, 6 * half:6 * half + 6], x[:, 512 * half:512 * half + 512])
            dve.drain()
            nc.vector.bn_aggr(s[:, 12:14], s[:, 0:12]).then_inc(summed[f"{name}.var"], 1)
            dve.drain()
            nc.vector.scalar_tensor_tensor(x, x, s[:, 12:13], g, ALU.subtract, ALU.mult)
            dve.wait_ge(*count(f"{name}.root", i + 1))
            nc.vector.reciprocal(s[:, 15:16], s[:, 14:15])
            dve.drain()
            nc.vector.scalar_tensor_tensor(x, x, s[:, 15:16], b, ALU.mult, ALU.add)

        def normalise_roots(act, name, tiles):
            for i, t in enumerate(tiles):
                act.wait_ge(*count(f"{name}.var", i + 1))
                nc.scalar.activation(ln_stats[:, t, 14:15], ln_stats[:, t, 13:14], ACT.Sqrt,
                                     bias=cst[:, C_EPS:C_EPS + 1]).then_inc(summed[f"{name}.root"], 1)

        def out_proj_pe(pe, name, tiles, chunks):
            halves = [chunks.take(), chunks.take()]
            for c in halves:
                await_chunk(pe, c)
            for i, t in enumerate(tiles):
                if i >= PAIRS:
                    pe.wait_ge(*count(f"{name}.read", i - PAIRS + 1))
                for half, c in enumerate(halves):
                    for k in range(KT):
                        mm = nc.tensor.matmul(pair(i, D)[:, 512 * half:512 * half + 512],
                                              x_feat[:, k, P * t:P * (t + 1)], chunk_view(c % RING, 512)[:, k, :],
                                              start=k == 0, stop=k == KT - 1)
                mm.then_inc(summed[f"{name}.ready"], 1)
            pe.drain().then_inc(w_free, 2)

        def out_proj_dve(dve, name, tiles, alpha, gate, g, b, modulated=None):
            dve.wait_ge(params_here, params[name])
            for i, t in enumerate(tiles):
                dve.wait_ge(*count(f"{name}.ready", i + 1))
                x = x_tok[:, t, :]
                y = pair(i, 1024)
                if gate is not None:
                    nc.vector.tensor_tensor(y, y, gate(t), ALU.mult)
                    dve.drain()
                nc.vector.scalar_tensor_tensor(x, x, alpha, y, ALU.mult, ALU.add).then_inc(summed[f"{name}.read"], 1)
                dve.drain()
                normalise(dve, name, i, t, g, b)
                if modulated is not None:
                    if i == 0:
                        dve.wait_ge(params_here, params[modulated])
                    dve.drain()
                    nc.vector.scalar_tensor_tensor(h_tok[:, t, :], scale_rows[:, t // TL], 1.0, x, ALU.add, ALU.mult)
                    dve.drain()
                    nc.vector.tensor_tensor(h_tok[:, t, :], h_tok[:, t, :], rows[:, 4 + t // TL], ALU.add)
            dve.drain()

        A_ROWS = 0
        A_TOK = 6 * D
        A_BLK = A_TOK + TA * D
        A_SMALL = A_BLK + 3072
        rows = region(A_ROWS, 6, D)
        h_tok = region(A_TOK, TA, D)
        blk_rows = region(A_TOK, 2, D)
        blk_feat = region(A_TOK + 2 * D, 2, 8, P)
        blk_out = region(A_TOK + 4 * D, 2, D)
        picked = region(A_TOK, 4, D)
        blk_gate = region(A_BLK, 2, FF)
        blk_hid = region(A_BLK + 2 * FF, 2, FF)
        scale_rows = region(A_BLK, 2, D)
        blk_hidT = region(A_BLK + 4 * FF, 2, 4, P)
        slots_i = sb("slots_i", [P, 2, TA], I32)
        gate_w = sb("gate_w", [P, 2, TA])
        expert_of = sb("expert_of", [1, 48], I32)
        used_blocks = sb("used_blocks", [1, 1], I32)

        def moe_counts(m):
            T, n = m.T, m.blocks
            return {"t.ready": 2 * T, "t.read0": T, "t.read1": T, "logits": 1, "exps": 2, "exps_done": 2, "ranks_in": 1,
                    "ranks": 1, "table": 1, "scattered": 32 * T, "rows0": 8 * n + 32, "rows1": 8 * n + 32,
                    "turned": n + 2, "feat": n + 2, "silu": n + 1, "hid": n + 1, "hid_turned": n, "hid_feat": n,
                    "y_copied": n + 1, "out_free": n + 2, "gathered": 32 * T, "both_rows": T,
                    "picked_free": T, "var": T, "root": T}

        def moe_sems(*mixtures):
            at = {}
            for name, m in mixtures:
                for part, total in moe_counts(m).items():
                    if part not in at:
                        at[part] = (sem(f"moe_{part}"), 0)
                    summed[f"{name}.{part}"], start[f"{name}.{part}"] = at[part]
                    at[part] = (at[part][0], at[part][1] + total)
                new_sems(name, "stored")

        def moe_router_pe(pe, name, m, wr, chunks, ada=()):
            n = m.G + m.E
            for t in range(m.T):
                for k in range(KT):
                    mm = nc.tensor.matmul(bank(0)[:, t * n:(t + 1) * n], x_feat[:, k, P * t:P * (t + 1)],
                                          wr[:, k, 0:n], start=k == 0, stop=k == KT - 1)
            mm.then_inc(summed[f"{name}.logits"], 1)
            for i in ada[:1]:
                ada_pe(pe, chunks, i)
            pe.wait_ge(*count(f"{name}.ranks_in", 1))
            chosen = moe_arrays(m)["both"]
            for t in range(m.T):
                for s in range(t + 1):
                    nc.tensor.matmul(bank(1)[:, t * m.E:(t + 1) * m.E], ones if s < t else tri_strict,
                                     chosen[:, s, :], start=s == 0, stop=s == t)
            for s in range(m.T):
                mm = nc.tensor.matmul(bank(2)[:, 0:m.E], ones, chosen[:, s, :], start=s == 0, stop=s == m.T - 1)
            mm.then_inc(summed[f"{name}.ranks"], 1)
            for i in ada[1:]:
                ada_pe(pe, chunks, i)

        def moe_arrays(m):
            T, G, E, EP = m.T, m.G, m.E, m.EP
            at = [A_SMALL]

            def arr(*shape):
                r = region(at[0], *shape)
                at[0] += int(np.prod(shape))
                return r
            return {"lg": arr(T, G + E), "gmax": arr(T), "gexp": arr(T, G), "gone": arr(T, G), "el": arr(T, EP),
                    "tmp": arr(T, G, EP), "m1": arr(T), "m2": arr(T), "one1": arr(T, EP), "one2": arr(T, EP),
                    "pg": arr(T), "k": arr(T, 8), "km": arr(T), "all1": arr(T, E), "all2": arr(T, E),
                    "both": arr(T, E), "slot": arr(T, E), "cnt": arr(E), "blocks": arr(E), "sums": arr(2, E),
                    "tab": arr(m.blocks, E), "tabr": arr(48), "sl": arr(2, T), "wr": arr(KT, G + E)}

        def moe_router_act(act, name, m, ada=()):
            a = moe_arrays(m)
            act.wait_ge(*count(f"{name}.exps", 1))
            nc.scalar.activation(a["gexp"], a["gexp"], ACT.Exp)
            act.drain().then_inc(summed[f"{name}.exps_done"], 1)
            act.wait_ge(*count(f"{name}.exps", 2))
            nc.scalar.activation(a["m2"], a["m2"], ACT.Exp).then_inc(summed[f"{name}.exps_done"], 1)
            for n in ada:
                ada_act(act, n, ada_late)

        def moe_router_dve(dve, name, m, bias):
            T, G, E, EP = m.T, m.G, m.E, m.EP
            a = moe_arrays(m)
            v = nc.vector

            def then(_):
                dve.drain()

            def first_max(x, n, mx, one):
                then(v.tensor_reduce(mx, x, axis=AX.X, op=ALU.max))
                k = a["k"][:, :, 0:n]
                then(v.tensor_tensor(k, x, spread(mx, 2, n), ALU.is_equal))
                then(v.tensor_tensor(one, spread(cst[:, C_IOTA:C_IOTA + n], 1, T), k, ALU.mult))
                then(v.scalar_tensor_tensor(k, k, float(n), one, ALU.mult, ALU.subtract))
                then(v.tensor_reduce(a["km"], k, axis=AX.X, op=ALU.max))
                then(v.tensor_tensor(one, k, spread(a["km"], 2, n), ALU.is_equal))

            dve.wait_ge(*count(f"{name}.logits", 1))
            lg = a["lg"]
            then(v.tensor_tensor(lg, bank(0)[:, 0:T * (G + E)].rearrange("p (t n) -> p t n", t=T),
                                 spread(bias, 1, T), ALU.add))
            glog = lg[:, :, 0:G]
            elog = lg[:, :, G:G + E].rearrange("p t (g e) -> p t g e", g=G)
            first_max(glog, G, a["gmax"], a["gone"])
            v.tensor_tensor(a["gexp"], glog, spread(a["gmax"], 2, G), ALU.subtract)
            dve.drain().then_inc(summed[f"{name}.exps"], 1)
            for t in range(T):
                v.tensor_tensor(a["tmp"][:, t], elog[:, t], spread(a["gone"][:, t, :], 2, EP), ALU.mult)
            dve.drain()
            then(v.tensor_reduce(a["el"], a["tmp"].rearrange("p t g e -> p t e g"), axis=AX.X, op=ALU.add))
            first_max(a["el"], EP, a["m1"], a["one1"])
            then(v.scalar_tensor_tensor(a["el"], a["one1"], NEG, a["el"], ALU.mult, ALU.add))
            first_max(a["el"], EP, a["m2"], a["one2"])
            v.tensor_tensor(a["m2"], a["m2"], a["m1"], ALU.subtract)
            for t in range(T):
                for one, every in (("one1", "all1"), ("one2", "all2")):
                    v.tensor_tensor(a[every][:, t, :].rearrange("p (g e) -> p g e", g=G),
                                    spread(a["gone"][:, t, :], 2, EP), spread(a[one][:, t, :], 1, G), ALU.mult)
            dve.drain().then_inc(summed[f"{name}.exps"], 1)
            v.tensor_tensor(a["both"], a["all1"], a["all2"], ALU.add).then_inc(summed[f"{name}.ranks_in"], 1)
            dve.wait_ge(*count(f"{name}.exps_done", 2))
            then(v.tensor_reduce(a["pg"], a["gexp"], axis=AX.X, op=ALU.add))
            then(v.tensor_scalar(a["m1"], a["m2"], 1.0, None, ALU.add))
            then(v.tensor_tensor(a["pg"], a["pg"], a["m1"], ALU.mult))
            then(v.reciprocal(gate_w[:, 0, 0:T], a["pg"]))
            v.tensor_tensor(gate_w[:, 1, 0:T], gate_w[:, 0, 0:T], a["m2"], ALU.mult)
            dve.wait_ge(*count(f"{name}.ranks", 1))
            then(v.tensor_copy(a["cnt"], bank(2)[:, 0:E]))
            then(v.tensor_scalar(a["blocks"], a["cnt"], 0.0, None, ALU.is_gt))
            for k in range(1, T):
                then(v.scalar_tensor_tensor(a["blocks"], a["cnt"], float(P * k), a["blocks"], ALU.is_gt, ALU.add))
            src = a["blocks"]
            step, side = 1, 0
            while step < E:
                dst = a["sums"][:, side]
                v.tensor_copy(dst[:, 0:step], src[:, 0:step])
                then(v.tensor_tensor(dst[:, step:E], src[:, step:E], src[:, 0:E - step], ALU.add))
                src, step, side = dst, step * 2, 1 - side
            ends = src
            starts = a["sums"][:, side]
            then(v.tensor_tensor(starts, ends, a["blocks"], ALU.subtract))
            rank = bank(1)[:, 0:T * E].rearrange("p (t e) -> p t e", t=T)
            then(v.tensor_scalar(starts, starts, float(P), None, ALU.mult))
            then(v.tensor_tensor(a["slot"], rank, spread(starts, 1, T), ALU.add))
            v.tensor_tensor(a["all1"], a["all1"], a["slot"], ALU.mult)
            v.tensor_tensor(a["all2"], a["all2"], a["slot"], ALU.mult)
            v.tensor_tensor(a["tab"][0:1], spread(ends[0:1, :], 1, m.blocks),
                            spread(cst[0:1, C_IOTA:C_IOTA + m.blocks], 2, E), ALU.is_le)
            dve.drain()
            v.tensor_reduce(a["sl"][:, 0], a["all1"], axis=AX.X, op=ALU.add)
            v.tensor_reduce(a["sl"][:, 1], a["all2"], axis=AX.X, op=ALU.add)
            v.tensor_reduce(a["tabr"][0:1, 0:m.blocks], a["tab"][0:1], axis=AX.X, op=ALU.add)
            dve.drain()
            v.tensor_copy(slots_i[:, :, 0:T], a["sl"])
            then(v.tensor_scalar(a["tabr"][0:1, 0:m.blocks], a["tabr"][0:1, 0:m.blocks], float(E - 1), None, ALU.min))
            v.tensor_copy(expert_of[0:1, 0:m.blocks], a["tabr"][0:1, 0:m.blocks])
            v.tensor_copy(used_blocks[0:1, 0:1], ends[0:1, E - 1:E])
            dve.drain().then_inc(summed[f"{name}.table"], 1)

        def moe_scatter(pool, name, m, src, ada=()):
            for n in ada[:2]:
                ada_pool(pool, n, ada_late)
            pool.wait_ge(*count(f"{name}.table", 1))
            for t in range(m.T):
                for c in range(2):
                    nc.gpsimd.indirect_dma_start(
                        out=d["xs"][:, :], out_offset=bass.IndirectOffsetOnAxis(ap=slots_i[:, c, t:t + 1], axis=0),
                        in_=src[:, t, :], in_offset=None).then_inc(summed[f"{name}.scattered"], 16)
            for n in ada[2:]:
                ada_pool(pool, n, ada_late)
            pool.wait_ge(*count(f"{name}.scattered", 32 * m.T))
            for i in range(2 if ada else 0):
                pool.wait_ge(*count(f"ada.sent{i}", 8 * (ada[-1] + 1)))

        def used(eng, m):
            return eng.value_load(used_blocks[0:1, 0:1], min_val=1, max_val=m.blocks - 1)

        def moe_sp(sp, name, m, w, chunks):
            base = chunks.n
            gate, up, down = w
            sp.wait_ge(*count(f"{name}.table", 1))
            n_used = used(sp, m)

            def matrix(w, block):
                e = sp.value_load(expert_of[0:1, bass.ds(block, 1)], min_val=0, max_val=m.E - 1)
                return w[bass.ds(e, 1), :, :].rearrange("a (p k) n -> p (a k n)", p=P)

            for part, w in enumerate((gate, up)):
                c = base + part
                source = matrix(w, 0)
                sp.wait_ge(w_free, c - RING + 1)
                sp.dma_start(w_ring[:, c % RING, :], source).then_inc(w_landed[c % RING], 16)
            sp.wait_ge(*count(f"{name}.scattered", 32 * m.T))
            with sp.Fori(0, m.blocks // 4) as turn:
                for b in range(4):
                    i = turn * 4 + (b + 1)
                    c = base + 2 + 3 * b
                    with sp.If(i < n_used):
                        for part, w in enumerate((gate, up)):
                            source = matrix(w, i)
                            sp.wait_ge(w_free, turn * 12 + (c + part - RING + 1))
                            sp.dma_start(w_ring[:, (c + part) % RING, :], source).then_inc(
                                w_landed[(c + part) % RING], 16)
                    with sp.Else():
                        for part in range(2):
                            sp.wait_ge(w_free, turn * 12 + (c + part - RING + 1))
                            sp.sem_inc(w_landed[(c + part) % RING], 16)
                    c += 2
                    with sp.If(i < n_used + 1):
                        source = matrix(down, i - 1)
                        sp.wait_ge(w_free, turn * 12 + (c - RING + 1))
                        sp.dma_start(w_ring[:, c % RING, :], source).then_inc(w_landed[c % RING], 16)
                    with sp.Else():
                        sp.wait_ge(w_free, turn * 12 + (c - RING + 1))
                        sp.sem_inc(w_landed[c % RING], 16)
            chunks.n += 3 * m.blocks + 2

        def moe_blocks_pe(pe, name, m, chunks):
            base = chunks.n

            def turn_rows(s, rows_value):
                pe.wait_ge(*count(f"{name}.rows{s}", rows_value))
                rows_k = blk_rows[:, s, :].rearrange("p (f k) -> p k f", k=KT)
                for k in range(KT):
                    mm = nc.tensor.transpose(bank(k // 4)[:, P * (k % 4):P * (k % 4 + 1)], rows_k[:, k, :], ident)
                mm.then_inc(summed[f"{name}.turned"], 1)

            def gate_or_up(s, part, c, turn):
                pe.wait_ge(w_landed[c % RING], turn * 48 + 16 * (c // RING + 1))
                for k in range(KT):
                    mm = nc.tensor.matmul(bank(2 + part), blk_feat[:, s, k, :], chunk_view(c % RING, FF)[:, k, :],
                                          start=k == 0, stop=k == KT - 1)
                mm.then_inc(w_free, 1)

            def turn_hidden(s, i):
                pe.wait_ge(*count(f"{name}.hid", i))
                hid_k = blk_hid[:, s, :].rearrange("p (f k) -> p k f", k=4)
                for k in range(4):
                    mm = nc.tensor.transpose(bank(4)[:, P * k:P * (k + 1)], hid_k[:, k, :], ident)
                mm.then_inc(summed[f"{name}.hid_turned"], 1)

            def down(s, i, c, turn):
                pe.wait_ge(*count(f"{name}.hid_feat", i))
                pe.wait_ge(*count(f"{name}.y_copied", i))
                pe.wait_ge(w_landed[c % RING], turn * 48 + 16 * (c // RING + 1))
                for half in range(2):
                    for k in range(4):
                        mm = nc.tensor.matmul(bank(5 + half), blk_hidT[:, s, k, :],
                                              chunk_view(c % RING, D, 4)[:, k, 512 * half:512 * half + 512],
                                              start=k == 0, stop=k == 3)
                mm.then_inc(w_free, 1)

            n_used = used(pe, m)
            turn_rows(0, 16)
            pe.wait_ge(*count(f"{name}.feat", 1))
            for part in range(2):
                gate_or_up(0, part, base + part, 0)
            turn_rows(1, 16)
            with pe.Fori(0, m.blocks // 4) as turn:
                for b in range(4):
                    s = (b + 1) % 2
                    i = turn * 4 + (b + 1)
                    c = base + 2 + 3 * b
                    with pe.If(i < n_used):
                        pe.wait_ge(*count(f"{name}.feat", i + 1))
                        pe.wait_ge(*count(f"{name}.silu", i))
                        gate_or_up(s, 0, c, turn)
                        turn_hidden(1 - s, i)
                        gate_or_up(s, 1, c + 1, turn)
                        turn_rows(1 - s, turn * 32 + 16 * ((b + 2) // 2 + 1))
                        down(1 - s, i, c + 2, turn)
                    with pe.Else():
                        pe.drain().then_inc(w_free, 2)
                        pe.sem_inc(summed[f"{name}.turned"], 1)
                        with pe.If(i < n_used + 1):
                            turn_hidden(1 - s, i)
                            down(1 - s, i, c + 2, turn)
                        with pe.Else():
                            pe.sem_inc(w_free, 1)
                            pe.sem_inc(summed[f"{name}.hid_turned"], 1)
            chunks.n += 3 * m.blocks + 2

        def moe_blocks_act(act, name, m, chunks):
            base = chunks.n

            def load_rows(block, s):
                act.dma_start(blk_rows[:, s, :], d["xs"][bass.ds(block * P, P), :]).then_inc(
                    summed[f"{name}.rows{s}"], 16)

            def take_features(s, n):
                act.wait_ge(*count(f"{name}.turned", n + 1))
                nc.scalar.activation(blk_feat[:, s], ps[:, 0:1024].rearrange("p (k n) -> p k n", n=P),
                                     ACT.Copy).then_inc(summed[f"{name}.feat"], 1)

            def silu(s):
                nc.scalar.activation(blk_gate[:, s, :], bank(2), ACT.Silu).then_inc(summed[f"{name}.silu"], 1)

            def take_hidden(s, i):
                act.wait_ge(*count(f"{name}.hid_turned", i))
                nc.scalar.activation(blk_hidT[:, s], bank(4).rearrange("p (k n) -> p k n", n=P),
                                     ACT.Copy).then_inc(summed[f"{name}.hid_feat"], 1)

            n_used = used(act, m)
            load_rows(0, 0)
            load_rows(1, 1)
            take_features(0, 0)
            load_rows(2, 0)
            act.wait_ge(w_free, base + 1)
            silu(0)
            take_features(1, 1)
            load_rows(3, 1)
            with act.Fori(0, m.blocks // 4) as turn:
                for b in range(4):
                    s = (b + 1) % 2
                    i = turn * 4 + (b + 1)
                    with act.If(i < n_used):
                        act.wait_ge(w_free, turn * 12 + (base + 3 * b + 3))
                        silu(s)
                        take_hidden(1 - s, i)
                        take_features(1 - s, i + 1)
                        load_rows(i + 3, 1 - s)
                    with act.Else():
                        act.drain().then_inc(summed[f"{name}.silu"], 1)
                        act.sem_inc(summed[f"{name}.feat"], 1)
                        act.sem_inc(summed[f"{name}.rows{1 - s}"], 16)
                        with act.If(i < n_used + 1):
                            take_hidden(1 - s, i)
                        with act.Else():
                            act.sem_inc(summed[f"{name}.hid_feat"], 1)
            for s in range(2):
                act.wait_ge(*count(f"{name}.rows{s}", 16 * (m.blocks // 2 + 2)))
            chunks.n += 3 * m.blocks + 2

        def moe_blocks_dve(dve, name, m, chunks):
            base = chunks.n

            def hidden(s, n):
                dve.wait_ge(*count(f"{name}.silu", n + 1))
                nc.vector.tensor_tensor(blk_hid[:, s, :], blk_gate[:, s, :], bank(3), ALU.mult).then_inc(
                    summed[f"{name}.hid"], 1)

            def outputs(s, i, value):
                dve.wait_ge(w_free, value)
                dve.wait_ge(*count(f"{name}.out_free", i))
                nc.vector.tensor_copy(blk_out[:, s, :], ps[:, 2560:3584]).then_inc(summed[f"{name}.y_copied"], 1)

            n_used = used(dve, m)
            dve.sem_inc(summed[f"{name}.y_copied"], 1)
            dve.wait_ge(w_free, base + 2)
            hidden(0, 0)
            with dve.Fori(0, m.blocks // 4) as turn:
                for b in range(4):
                    s = (b + 1) % 2
                    i = turn * 4 + (b + 1)
                    with dve.If(i < n_used):
                        dve.wait_ge(w_free, turn * 12 + (base + 3 * b + 4))
                        hidden(s, i)
                        outputs(1 - s, i, turn * 12 + (base + 3 * b + 5))
                    with dve.Else():
                        dve.drain().then_inc(summed[f"{name}.hid"], 1)
                        with dve.If(i < n_used + 1):
                            outputs(1 - s, i, turn * 12 + (base + 3 * b + 5))
                        with dve.Else():
                            dve.sem_inc(summed[f"{name}.y_copied"], 1)
            chunks.n += 3 * m.blocks + 2

        def moe_blocks_pool(pool, name, m):
            n_used = used(pool, m)
            pool.sem_inc(summed[f"{name}.out_free"], 2)
            with pool.Fori(0, m.blocks // 4) as turn:
                for b in range(4):
                    n = turn * 4 + b
                    with pool.If(n < n_used):
                        pool.wait_ge(*count(f"{name}.y_copied", n + 2))
                        pool.dma_start(d["ys"][bass.ds(n * P, P), :], blk_out[:, b % 2, :]).then_inc(
                            summed[f"{name}.stored"], 16)
                        pool.wait_ge(*count(f"{name}.stored", n * 16 + 16))
                        pool.sem_inc(summed[f"{name}.out_free"], 1)
                    with pool.Else():
                        pool.sem_inc(summed[f"{name}.out_free"], 1)

        def moe_gather_pool(pool, name, m):
            for t in range(m.T):
                if t >= 2:
                    pool.wait_ge(*count(f"{name}.picked_free", t - 1))
                for c in range(2):
                    nc.gpsimd.indirect_dma_start(
                        out=picked[:, 2 * (t % 2) + c, :], out_offset=None, in_=d["ys"][0:P * m.blocks, :],
                        in_offset=bass.IndirectOffsetOnAxis(ap=slots_i[:, c, t:t + 1], axis=0)
                    ).then_inc(summed[f"{name}.gathered"], 16)
                pool.wait_ge(*count(f"{name}.gathered", 32 * (t + 1)))
                pool.sem_inc(summed[f"{name}.both_rows"], 1)

        def moe_combine_dve(dve, name, m, alpha, gate, g, b):
            for t in range(m.T):
                dve.wait_ge(*count(f"{name}.both_rows", t + 1))
                y1, y2 = picked[:, 2 * (t % 2), :], picked[:, 2 * (t % 2) + 1, :]
                nc.vector.tensor_scalar(y1, y1, gate_w[:, 0, t:t + 1], None, ALU.mult)
                dve.drain()
                nc.vector.scalar_tensor_tensor(y1, y2, gate_w[:, 1, t:t + 1], y1, ALU.mult, ALU.add)
                dve.drain()
                if gate is not None:
                    nc.vector.tensor_tensor(y1, y1, gate(t), ALU.mult)
                    dve.drain()
                x = x_tok[:, t, :]
                nc.vector.scalar_tensor_tensor(x, x, alpha, y1, ALU.mult, ALU.add).then_inc(
                    summed[f"{name}.picked_free"], 1)
                dve.drain()
                normalise(dve, name, t, t, g, b)
            dve.drain()

        def ada_pe(pe, chunks, n):
            c = chunks.take()
            await_chunk(pe, c)
            if n >= 2:
                pe.wait_ge(*count("ada.read", n - 1))
            for k in range(KT):
                mm = nc.tensor.matmul(bank(6 + n % 2)[0:2, :], fcol[:, FC["cond"] + 2 * k:FC["cond"] + 2 * k + 2],
                                      chunk_view(c % RING, 512)[:, k, :], start=k == 0, stop=k == KT - 1)
            mm.then_inc(summed["ada.ready"], 1)
            pe.drain().then_inc(w_free, 1)

        def ada_act(act, n, buffers):
            act.wait_ge(*count("ada.ready", n + 1))
            if n >= 2:
                act.wait_ge(*count(f"ada.sent{n % 2}", 16 * (n // 2)))
            nc.scalar.activation(buffers[n % 2][0:2, :], bank(6 + n % 2)[0:2, :], ACT.Copy).then_inc(
                summed["ada.read"], 1)

        def ada_pool(pool, n, buffers):
            pool.wait_ge(*count("ada.read", n + 1))
            pool.dma_start(d["mods"][:, 512 * n:512 * n + 512], buffers[n % 2][0:2, :], accum_op=ALU.add).then_inc(
                summed[f"ada.sent{n % 2}"], 16)

        PAIR = 2 * TL

        def attention_pe(pe, name, jobs, probs, probsT):
            n = len(jobs)
            for step in range(n + 3):
                if step < n:
                    jb = jobs[step]
                    if step >= 2:
                        pe.wait_ge(*count(f"{name}.exped", step - 1))
                    for lo, hi in jb["spans"]:
                        terms = jb["terms"](lo, hi)
                        for k, (q, kk) in enumerate(terms):
                            mm = nc.tensor.matmul(ps[:, 1024 * (step % 2) + lo:1024 * (step % 2) + hi], q, kk,
                                                  start=k == 0, stop=k == len(terms) - 1)
                    mm.then_inc(summed[f"{name}.scores"], 1)
                if 0 <= step - 2 < n:
                    j = step - 2
                    pe.wait_ge(*count(f"{name}.scaled", j + 1))
                    if j >= 1:
                        pe.wait_ge(*count(f"{name}.turned_read", j))
                    for k in range(jobs[j]["keys"] // P):
                        mm = nc.tensor.transpose(ps[:, 2048 + P * k:2048 + P * (k + 1)],
                                                 probs[:, j % 2, P * k:P * (k + 1)], ident)
                    mm.then_inc(summed[f"{name}.turned"], 1)
                if 0 <= step - 3 < n:
                    j = step - 3
                    pe.wait_ge(*count(f"{name}.turned_read", j + 1))
                    pair_at, half, i = j // PAIR, HD * (j // TL % 2), j % TL
                    if pair_at >= 2 and j % PAIR == 0:
                        pe.wait_ge(*count(f"{name}.out_read", pair_at - 1))
                    kt = jobs[j]["keys"] // P
                    for k in range(kt):
                        mm = nc.tensor.matmul(bank(6 + pair_at % 2)[half:half + HD, P * i:P * (i + 1)],
                                              jobs[j]["values"](k), probsT[:, j % 2, P * k:P * (k + 1)],
                                              start=k == 0, stop=k == kt - 1)
                    mm.then_inc(summed[f"{name}.out"], 1)

        def attention_dve(dve, name, jobs, probs, stat, ktile):
            n = len(jobs)
            for step in range(n + 4):
                if step < n:
                    jb = jobs[step]
                    s = ps[:, 1024 * (step % 2):1024 * (step % 2) + jb["keys"]]
                    dve.wait_ge(*count(f"{name}.scores", step + 1))
                    if jb["adjust"]:
                        jb["adjust"](dve, s)
                        dve.drain()
                    nc.vector.tensor_reduce(stat[:, step % 4, 0:1], s, axis=AX.X, op=ALU.max, negate=True
                                            ).then_inc(summed[f"{name}.shift"], 1)
                if 0 <= step - 1 < n:
                    j = step - 1
                    dve.wait_ge(*count(f"{name}.exped", j + 1))
                    nc.vector.reciprocal(stat[:, j % 4, 2:3], stat[:, j % 4, 1:2])
                    dve.drain()
                    p = probs[:, j % 2, 0:jobs[j]["keys"]]
                    nc.vector.tensor_scalar(p, p, stat[:, j % 4, 2:3], None, ALU.mult).then_inc(
                        summed[f"{name}.scaled"], 1)
                if step >= 4 and (step - 3) % PAIR == 0:
                    pair_at = (step - 4) // PAIR
                    dve.wait_ge(*count(f"{name}.out", PAIR * (pair_at + 1)))
                    nc.vector.tensor_copy(x_feat[:, ktile + pair_at, 0:SEQ], bank(6 + pair_at % 2)).then_inc(
                        summed[f"{name}.out_read"], 1)

        def attention_act(act, name, jobs, probs, probsT, stat):
            n = len(jobs)
            for step in range(n + 2):
                if 0 <= step - 2 < n:
                    j = step - 2
                    act.wait_ge(*count(f"{name}.turned", j + 1))
                    if j >= 2:
                        act.wait_ge(*count(f"{name}.out", j - 1))
                    nc.scalar.activation(probsT[:, j % 2, 0:jobs[j]["keys"]], ps[:, 2048:2048 + jobs[j]["keys"]],
                                         ACT.Copy).then_inc(summed[f"{name}.turned_read"], 1)
                if step < n:
                    keys = jobs[step]["keys"]
                    act.wait_ge(*count(f"{name}.shift", step + 1))
                    nc.scalar.activation(probs[:, step % 2, 0:keys], ps[:, 1024 * (step % 2):1024 * (step % 2) + keys],
                                         ACT.Exp, bias=stat[:, step % 4, 0:1], accum_out=stat[:, step % 4, 1:2])
                    act.drain().then_inc(summed[f"{name}.exped"], 1)

        def attention_sems(name):
            new_sems(name, "scores", "shift", "exped", "scaled", "turned", "turned_read", "out", "out_read")

        MOE1 = Moe(TL, 4, 4)
        MOE2 = Moe(TA, 4, 8)
        MOE3 = Moe(TL, 4, 8)
        MOE1_AT = 6 + 12 + 2 + 6
        MOE2_AT = MOE1_AT + 3 * MOE1.blocks + 2 + 5 + 2 + 6
        MOE3_AT = MOE2_AT + 3 * MOE2.blocks + 2 + 5 + 2
        loads = sem("loads")
        FIRST_LOADS = 8
        filled = sem("filled")
        fill = x_feat[:, 0:2, SEQ:NTOK]
        XS_BLOCKS = MOE2.blocks + 4
        YS_ZERO = 2 * TL

        z_feat = region(0, 4, SEQ)
        q_feat = region(2048, 4, SEQ)
        k_feat = region(4096, 4, SEQ)
        v_tok = region(6144, TL, 512)
        xdt_tok = region(8192, TL, 512)
        xbc = region(10240, 8, SEQ)
        xbc_in = region(14336, 8, SEQ + 3)
        decay = region(14336, 2, 1280)
        mixed = x_feat[:, 4:8, :].rearrange("p k n -> p (k n)")[:, 0:2560].rearrange("p (b n) -> p b n", b=2)
        TRI_AT = [0, 512, 896, 1152]
        cb = region(18456, 2, 1280)
        dtf = region(21016, TL, 16)
        dts = region(21080, 3, TL, 16)
        cum = region(21272, TL, 16)
        a_row = region(21336, 8)
        w_dtf = region(21344, KT, 16)
        v_bias = region(8192, 512)
        cum_row = region(21984, SEQ)
        fneg_row = region(22496, SEQ)
        rms1 = region(8192, 2, SEQ)
        probs1 = region(14336, 2, 512)
        probsT1 = region(15360, 2, 512)
        stat = sb("stat", [P, 4, 4])

        new_sems("x0", "ready", "read0", "read1")
        new_sems("in1", "ready", "read0", "read1", "dtf", "dt1", "dt2", "cum", "cumd", "cumt")
        new_sems("conv1", "silu", "acc")
        new_sems("ssd", "cb", "cbd", "xs", "xsd", "row", "arg", "exp", "mix", "y", "y_read", "var_in", "var", "root")
        attention_sems("att1")
        new_sems("out1", "ready", "read", "var", "root")
        moe_sems(("moe1", MOE1), ("moe2", MOE2), ("moe3", MOE3))
        new_sems("ada", "ready", "read", "sent0", "sent1")
        new_sems("x2", "ready", "read0", "read1")
        new_sems("in2", "ready", "read0", "read1", "read2", "read3", "read4", "sig")
        new_sems("ca", "mean_in", "mean", "root", "sq", "silu")
        new_sems("out2", "ready", "read", "var", "root")
        new_sems("x3", "ready", "read0", "read1")
        new_sems("in3", "ready", "read0", "read1")
        new_sems("rope", "sq", "root", "done", "turned", "turned_read", "g_here0", "g_here1", "g_free")
        attention_sems("att2")
        new_sems("out3", "ready", "read", "var", "root")

        IN1 = []
        for chunk in range(5):
            for i in range(4):
                IN1.append((i == 0, i == 3, feature_products(P * i, SEQ)))
        for t in range(TL):
            IN1.append((t == 0, t == TL - 1, token_products(t, 512, v_bias[0:1, :])))
        IN1_COLS = [0, 512, 1024, 1544, 2056, 2568]

        def in1_take(v):
            def take(j):
                src = pair(j, 512)
                chunk, i = j // 4, j % 4
                bias = fcol[:, FC["b_in"] + j:FC["b_in"] + j + 1]
                if chunk == 0:
                    if v:
                        return nc.vector.tensor_scalar(z_feat[:, i, :], src, bias, None, ALU.add)
                    return nc.scalar.activation(z_feat[:, i, :], src, ACT.Identity, bias=bias)
                if chunk in (1, 2):
                    out = xbc_in[:, 4 * (chunk - 1) + i, 3:]
                elif chunk == 3:
                    if v:
                        return nc.vector.tensor_scalar(q_feat[:, i, :], src, ATT_SCALE, bias, ALU.mult, ALU.add)
                    return nc.scalar.activation(q_feat[:, i, :], src, ACT.Identity, bias=bias, scale=ATT_SCALE)
                elif chunk == 4:
                    out = k_feat[:, i, :]
                else:
                    out = v_tok[:, i, :]
                    return (nc.vector.tensor_copy(out, src) if v else nc.scalar.activation(out, src, ACT.Copy))
                if v:
                    return nc.vector.tensor_scalar(out, src, bias, None, ALU.add)
                return nc.scalar.activation(out, src, ACT.Identity, bias=bias)
            return take

        def att1_jobs():
            jobs = []
            for h in range(HEADS):
                half = HD * (h % 2)
                for i in range(TL):
                    keys = P * (i + 1)

                    def terms(lo, hi, h=h, i=i, half=half):
                        return [(q_feat[half:half + HD, h // 2, P * i:P * (i + 1)], k_feat[half:half + HD, h // 2, lo:hi]),
                                (ident[0:16, 8 + h:9 + h].broadcast_to([16, P]), fneg_row[0:16, lo:hi])]

                    def adjust(dve, s, i=i):
                        nc.vector.tensor_tensor(s[:, P * i:], s[:, P * i:], causal, ALU.add)

                    jobs.append({"spans": [(0, keys)], "terms": terms, "keys": keys, "adjust": adjust,
                                 "values": lambda k, h=h: v_tok[:, k, HD * h:HD * (h + 1)]})
            return jobs

        sig = region(0, 2, NTOK)
        ya_in = region(1536, 4, PADDED)
        yb_in = region(1536 + 4 * PADDED, 4, PADDED)
        o2 = 1536 + 8 * PADDED
        b_gate = region(o2, 4, NTOK)
        ya = region(o2 + 4 * NTOK, 4, SPAN)
        yb = region(o2 + 4 * NTOK + 4 * SPAN, 4, SPAN)
        col2 = region(22978, 2, 2, 8)
        mean2 = region(1536, SPAN)
        cen2 = region(1536 + SPAN + 1, 2, SPAN)
        IN2_COLS = [512, 0, 1536, 2048, 1024]
        IN2 = [(i == 0, i == 3, feature_products(P * i, NTOK)) for _ in range(5) for i in range(4)]

        def padded(buf, i):
            return ((buf[:, i, PAD:PAD + SEQ], slice(0, SEQ)), (buf[:, i, PAD + CTX_AT:PAD + CTX_AT + CTX], slice(SEQ, NTOK)))

        qk_tok = region(0, TA, 10, HD)
        rp = region(3840, 4, 320)
        probs3 = region(0, 2, NTOK)
        probsT3 = region(2 * NTOK, 2, NTOK)
        qc_feat = region(5120, 4, SEQ)
        kc_feat = region(7168, 2, NTOK)
        qd_feat = region(8704, 4, SEQ)
        kd_feat = region(10752, 4, NTOK)
        vc_tok = region(13824, TA, P)
        vd_tok = region(14592, TA, 512)
        g_bias = region(17664, 2, 16, HD)
        rope_cs = region(19712, TL, 2, 32)
        rr = region(19968, TA, 10)
        col3 = region(22978, 2, 2, 8)
        kdup = region(20064, 256)
        sq3 = region(20320, 640)

        IN3 = ([(t == 0, t == TL - 1, token_products(t, 512)) for t in range(TL)]
               + [(t == 0, t == TA - 1, token_products(t, 256)) for t in range(TA)]
               + [(i == 0, i == 3, feature_products(P * i, SEQ)) for i in range(4)]
               + [(i == 0, i == 3, feature_products(P * i, NTOK)) for i in range(4)]
               + [(t == 0, t == TA - 1, token_products(t, 512)) for t in range(TA)])
        IN3_COLS = [(0, 512), (512, 256), (768, 512), (1280, 512), (1792, 512)]

        def in3_take(v):
            def take(j):
                def copy(out, src):
                    return nc.vector.tensor_copy(out, src) if v else nc.scalar.activation(out, src, ACT.Copy)
                if j < TL:
                    return copy(qk_tok[:, j, 0:8, :], pair(j, 512).rearrange("p (h e) -> p h e", h=8))
                j0 = j - TL
                if j0 < TA:
                    copy(qk_tok[:, j0, 8:10, :], pair(j, P).rearrange("p (h e) -> p h e", h=2))
                    return copy(vc_tok[:, j0, :], pair(j, 256)[:, P:])
                j0 -= TA
                if j0 < 4:
                    if v:
                        return nc.vector.tensor_scalar(qd_feat[:, j0, :], pair(j, SEQ), ATT_SCALE, None, ALU.mult)
                    return nc.scalar.activation(qd_feat[:, j0, :], pair(j, SEQ), ACT.Copy, scale=ATT_SCALE)
                j0 -= 4
                if j0 < 4:
                    return copy(kd_feat[:, j0, :], pair(j, NTOK))
                return copy(vd_tok[:, j0 - 4, :], pair(j, 512))
            return take


        def att2_jobs():
            jobs = []
            for h in range(HEADS):
                half = HD * (h % 2)
                for i in range(TL):
                    jobs.append({
                        "spans": [(0, 512), (512, NTOK)],
                        "terms": lambda lo, hi, h=h, i=i, half=half: [
                            (qc_feat[half:half + HD, h // 2, P * i:P * (i + 1)], kc_feat[half:half + HD, h // 4, lo:hi])],
                        "keys": NTOK, "adjust": None,
                        "values": lambda k, h=h: vc_tok[:, k, HD * (h // 4):HD * (h // 4 + 1)]})
            for h in range(HEADS):
                half = HD * (h % 2)
                for i in range(TL):
                    def adjust(dve, s, h=h, i=i):
                        if i == 0:
                            dve.wait_ge(*count(f"rope.g_here{h % 2}", 32 * (h // 2 + 1)))
                        b = g_bias[:, h % 2, 7 - 2 * i:15 - 2 * i, :].rearrange("p r c -> p (r c)")
                        ins = nc.vector.tensor_tensor(s[:, 0:SEQ], b, s[:, 0:SEQ], ALU.add)
                        if i == TL - 1:
                            ins.then_inc(summed["rope.g_free"], 1)
                    jobs.append({
                        "spans": [(0, 512), (512, NTOK)],
                        "terms": lambda lo, hi, h=h, i=i, half=half: [
                            (qd_feat[half:half + HD, h // 2, P * i:P * (i + 1)], kd_feat[half:half + HD, h // 2, lo:hi])],
                        "keys": NTOK, "adjust": adjust,
                        "values": lambda k, h=h: vd_tok[:, k, HD * h:HD * (h + 1)]})
            return jobs

        ada_early = [region(21472, 512), x_feat[:, 7, NTOK - 512:NTOK]]
        ada_late = [region(A_BLK, 512), region(A_BLK + 512, 512)]
        ADA_ROUTE1, ADA_ROUTE2 = range(12, 18), range(18, 24)
        ADA_FIRST = 3

        def mixed_sq(c):
            return region(10240 + 2048 + 512 * c, SEQ)

        def kdup_of(t):
            return region(20064 + 256 * (t % 2), 256)

        block = es.enter_context(nc.Block())

        @block.sync
        def _(sp):
            chunks = Chunks()
            for i, c0 in enumerate(IN1_COLS):
                if i == 1:
                    sp.wait_ge(loads, 16 * FIRST_LOADS)
                load_columns(sp, chunks, d["w_in"], c0, 512)
            for c in range(12):
                load_columns(sp, chunks, d["ada_w"][0], 512 * c, 512)
            for c0 in (0, 512):
                load_columns(sp, chunks, d["w_out"], c0, 512)
            for n in ADA_ROUTE1:
                load_columns(sp, chunks, d["ada_w"][1], 512 * (n - 12), 512)
            moe_sp(sp, "moe1", MOE1, (d["w_gate"], d["w_up"], d["w_down"]), chunks)
            sp.wait_ge(*count("moe1.gathered", 32 * TL))
            for c0 in IN2_COLS:
                load_columns(sp, chunks, d["conv_w_in"], c0, 512)
            for c0 in (0, 512):
                load_columns(sp, chunks, d["conv_w_out"], c0, 512)
            for n in ADA_ROUTE2:
                load_columns(sp, chunks, d["ada_w"][1], 512 * (n - 12), 512)
            moe_sp(sp, "moe2", MOE2, tuple(d[k][0] for k in ("e_gate", "e_up", "e_down")), chunks)
            sp.wait_ge(*count("moe2.gathered", 32 * TA))
            for c0, n in IN3_COLS:
                load_columns(sp, chunks, d["attn_w_in"], c0, n)
            for c0 in (0, 512):
                load_columns(sp, chunks, d["attn_w_out"], c0, 512)
            moe_sp(sp, "moe3", MOE3, tuple(d[k][1] for k in ("e_gate", "e_up", "e_down")), chunks)

        @block.tensor
        def _(pe):
            chunks = Chunks()
            stage(pe, "pe", "loaded")
            transpose_pe(pe, "x0", range(TL))
            stage(pe, "pe", "x1")
            for t in range(TL):
                for k in range(KT):
                    mm = nc.tensor.matmul(bank(7)[:, 16 * t:16 * t + 16], x_feat[:, k, P * t:P * (t + 1)],
                                          w_dtf[:, k, :], start=k == 0, stop=k == KT - 1)
            mm.then_inc(summed["in1.dtf"], 1)
            pe.wait_ge(*count("in1.dt1", 1))
            linear_pe(pe, "in1", IN1, chunks, by_parity("in1"))
            stage(pe, "pe", "in1")
            for t in range(TL):
                for s in range(t + 1):
                    mm = nc.tensor.matmul(bank(0)[:, 16 * t:16 * t + 16], ones if s < t else tri, dtf[:, s, :],
                                          start=s == 0, stop=s == t)
            mm.then_inc(summed["in1.cum"], 1)
            pe.wait_ge(*count("in1.cumd", 1))
            for t in range(TL):
                mm = nc.tensor.transpose(bank(1)[0:16, P * t:P * (t + 1)], cum[:, t, :], ident)
            mm.then_inc(summed["in1.cumt"], 1)
            pe.wait_ge(*count("conv1.silu", 8))
            for g in range(2):
                for s in range(TL):
                    n = SEQ - P * s
                    if g:
                        pe.wait_ge(*count("ssd.cbd", s + 1))
                    nc.tensor.matmul(bank(2 + s, n), xbc[:, 4 + g, P * s:P * (s + 1)], xbc[:, 6 + g, P * s:SEQ],
                                     start=True, stop=True).then_inc(summed["ssd.cb"], 1)
            for t in range(TL):
                if t >= 2:
                    pe.wait_ge(*count("ssd.xsd", t - 1))
                for c in range(4):
                    mm = nc.tensor.transpose(bank(6 + t % 2)[:, P * c:P * (c + 1)], xbc[:, c, P * t:P * (t + 1)], ident)
                mm.then_inc(summed["ssd.xs"], 1)
            pe.wait_ge(*count("ssd.xsd", TL))
            for n in range(ADA_FIRST):
                ada_pe(pe, chunks, n)
            stage(pe, "pe", "ssd_in")
            for step in range(HEADS + 1):
                if step < HEADS:
                    if step >= 2:
                        pe.wait_ge(*count("ssd.arg", step - 1))
                    nc.tensor.matmul(bank(step % 2), ident[0:16, step:step + 1].broadcast_to([16, P]),
                                     cum_row[0:16, :], start=True, stop=True).then_inc(summed["ssd.row"], 1)
                if step >= 1:
                    h = step - 1
                    pe.wait_ge(*count("ssd.mix", h + 1))
                    if h >= 4 and h % 2 == 0:
                        pe.wait_ge(*count("ssd.y_read", (h - 4) // 2 + 1))
                    half = HD * (h % 2)
                    for s in range(TL):
                        mm = nc.tensor.matmul(bank(2 + (h // 2) % 2)[half:half + HD, P * s:SEQ],
                                              xdt_tok[:, s, HD * h:HD * (h + 1)],
                                              mixed[:, h % 2, TRI_AT[s]:TRI_AT[s] + SEQ - P * s],
                                              start=s == 0, stop=s == TL - 1)
                    mm.then_inc(summed["ssd.y"], 1)
                ada_pe(pe, chunks, ADA_FIRST + step)
            for g in range(2):
                pe.wait_ge(*count("ssd.var_in", 2 * (g + 1)))
                for c in range(2):
                    mm = nc.tensor.matmul(bank(4 + g), ones, mixed_sq(2 * g + c), start=c == 0, stop=c == 1)
                mm.then_inc(summed["ssd.var"], 1)
            stage(pe, "pe", "ssd")
            attention_pe(pe, "att1", att1_jobs(), probs1, probsT1)
            stage(pe, "pe", "att1")
            out_proj_pe(pe, "out1", range(TL), chunks)
            stage(pe, "pe", "out1")
            transpose_pe(pe, "moe1.t", range(TL))
            stage(pe, "pe", "h1")
            moe_router_pe(pe, "moe1", MOE1, moe_arrays(MOE1)["wr"], chunks, ADA_ROUTE1)
            stage(pe, "pe", "route1")
            moe_blocks_pe(pe, "moe1", MOE1, chunks)
            stage(pe, "pe", "experts1")
            stage(pe, "pe", "combine1")
            transpose_pe(pe, "x2", range(TA))
            stage(pe, "pe", "x2")
            linear_pe(pe, "in2", IN2, chunks, lambda j: count(f"in2.read{j // 4}", j % 4 + 1))
            stage(pe, "pe", "in2")
            for j in range(2):
                for i in range(4):
                    pe.wait_ge(*count("ca.mean_in", 4 * j + i + 1))
                    src = ya[:, i] if j == 0 else cen2[:, i % 2]
                    for lo, hi in ((0, 512), (512, SPAN)):
                        mm = nc.tensor.matmul(ps[:, 1024 * j + lo:1024 * j + hi], ones, src[:, lo:hi],
                                              start=i == 0, stop=i == 3)
                    mm.then_inc(summed["ca.mean"], 1)
            stage(pe, "pe", "conv")
            out_proj_pe(pe, "out2", range(TA), chunks)
            stage(pe, "pe", "out2")
            transpose_pe(pe, "moe2.t", range(TA), h_tok)
            stage(pe, "pe", "h2t")
            moe_router_pe(pe, "moe2", MOE2, moe_arrays(MOE2)["wr"], chunks, ADA_ROUTE2)
            stage(pe, "pe", "route2")
            moe_blocks_pe(pe, "moe2", MOE2, chunks)
            stage(pe, "pe", "experts2")
            stage(pe, "pe", "combine2")
            transpose_pe(pe, "x3", range(TA))
            stage(pe, "pe", "x3")
            linear_pe(pe, "in3", IN3, chunks, by_parity("in3"))
            stage(pe, "pe", "in3")
            for t in range(TA):
                pe.wait_ge(*count("rope.done", t + 1))
                if t >= 2:
                    pe.wait_ge(*count("rope.turned_read", t - 1))
                b = 2 * (t % 2)
                for c in range(4 if t < TL else 0):
                    nc.tensor.transpose(bank(b)[:, P * c:P * (c + 1)],
                                        qk_tok[:, t, 2 * c:2 * c + 2, :].rearrange("p h e -> p (h e)"), ident)
                for c in range(2):
                    mm = nc.tensor.transpose(bank(b + 1)[:, P * c:P * (c + 1)], kdup_of(t)[:, P * c:P * (c + 1)], ident)
                mm.then_inc(summed["rope.turned"], 1)
            stage(pe, "pe", "rope")
            attention_pe(pe, "att2", att2_jobs(), probs3, probsT3)
            stage(pe, "pe", "att2")
            out_proj_pe(pe, "out3", range(TL), chunks)
            stage(pe, "pe", "out3")
            transpose_pe(pe, "moe3.t", range(TL), h_tok)
            stage(pe, "pe", "h3t")
            moe_router_pe(pe, "moe3", MOE3, moe_arrays(MOE3)["wr"], chunks)
            stage(pe, "pe", "route3")
            moe_blocks_pe(pe, "moe3", MOE3, chunks)
            stage(pe, "pe", "experts3")
            stage(pe, "pe", "combine3")

        @block.scalar
        def _(act):
            stage(act, "act", "loaded")
            transpose_take(act, "x0", 1, range(TL), x_feat)
            nc.scalar.activation(fcol[:, FC["cond"]:FC["cond"] + 16], fcol[:, FC["cond"]:FC["cond"] + 16], ACT.Silu)
            stage(act, "act", "x1")
            act.wait_ge(*count("in1.dt1", 1))
            nc.scalar.activation(dts[:, 1], dts[:, 1], ACT.Exp)
            act.drain()
            nc.scalar.activation(dts[:, 2], dts[:, 1], ACT.Identity, bias=ones[:, 0:1])
            act.drain()
            nc.scalar.activation(dtf[:, :, :], dts[:, 2], ACT.Ln)
            nc.scalar.activation(a_row, frow[:, RC["a_log"]:RC["a_log"] + 8], ACT.Exp)
            act.drain().then_inc(summed["in1.dt2"], 1)
            linear_take(act, "in1", 1, [in1_take(False)] * len(IN1))
            stage(act, "act", "in1")
            for i in range(4):
                nc.scalar.activation(z_feat[:, i, :], z_feat[:, i, :], ACT.Silu)
            for i in range(8):
                act.wait_ge(*count("conv1.acc", i + 1))
                nc.scalar.activation(xbc[:, i, :], xbc[:, i, :], ACT.Silu).then_inc(summed["conv1.silu"], 1)
            for n in range(ADA_FIRST):
                ada_act(act, n, ada_early)
            stage(act, "act", "ssd_in")
            for h in range(HEADS):
                act.wait_ge(*count("ssd.arg", h + 1))
                nc.scalar.activation(decay[:, h % 2], decay[:, h % 2], ACT.Exp).then_inc(summed["ssd.exp"], 1)
                ada_act(act, ADA_FIRST + h, ada_early)
            ada_act(act, ADA_FIRST + HEADS, ada_early)
            for c in range(4):
                act.wait_ge(*count("ssd.y_read", 4 + c + 1))
                nc.scalar.activation(mixed_sq(c), z_feat[:, c, :], ACT.Square).then_inc(summed["ssd.var_in"], 1)
            for g in range(2):
                act.wait_ge(*count("ssd.var", g + 1))
                nc.scalar.activation(rms1[:, g], bank(4 + g), ACT.Sqrt, bias=cst[:, C_EPS:C_EPS + 1],
                                     scale=1.0 / 256).then_inc(summed["ssd.root"], 1)
            stage(act, "act", "ssd")
            attention_act(act, "att1", att1_jobs(), probs1, probsT1, stat)
            stage(act, "act", "att1")
            normalise_roots(act, "out1", range(TL))
            stage(act, "act", "out1")
            transpose_take(act, "moe1.t", 1, range(TL), x_feat)
            stage(act, "act", "h1")
            moe_router_act(act, "moe1", MOE1, ADA_ROUTE1)
            stage(act, "act", "route1")
            moe_blocks_act(act, "moe1", MOE1, Chunks(MOE1_AT))
            stage(act, "act", "experts1")
            normalise_roots(act, "moe1", range(TL))
            stage(act, "act", "combine1")
            transpose_take(act, "x2", 1, range(TA), x_feat, lambda t: col2[:, t // TL, 0, :], lambda t: col2[:, t // TL, 1, :])
            stage(act, "act", "x2")
            sigs = 0
            for j in range(len(IN2)):
                if j < 4:
                    act.wait_ge(*count("in2.ready", j + 1))
                    nc.scalar.activation(b_gate[:, j, :], pair(j), ACT.Sigmoid).then_inc(
                        summed[f"in2.read{j // 4}"], 1)
                    if j == 3:
                        act.drain().then_inc(summed["in2.sig"], 1)
                elif 8 <= j < 12:
                    act.wait_ge(*count("in2.ready", j + 1))
                    for dst, span in padded(yb_in, j - 8):
                        ins = nc.scalar.activation(dst, pair(j)[:, span], ACT.Copy)
                    ins.then_inc(summed[f"in2.read{j // 4}"], 1)
                    if j == 11:
                        act.drain().then_inc(summed["in2.sig"], 1)
                elif j >= 16:
                    act.wait_ge(*count("in2.ready", j + 1))
                    act.wait_ge(*count("in2.sig", 3))
                    nc.scalar.activation(b_gate[:, j - 16, :], pair(j), ACT.Copy).then_inc(
                        summed[f"in2.read{j // 4}"], 1)
            stage(act, "act", "in2")
            for i in range(4):
                act.wait_ge(*count("ca.sq", i + 1))
                if i >= 2:
                    act.wait_ge(*count("ca.mean", 4 + i - 1))
                nc.scalar.activation(cen2[:, i % 2], ya[:, i], ACT.Square).then_inc(summed["ca.mean_in"], 1)
            act.wait_ge(*count("ca.mean", 8))
            nc.scalar.activation(mean2, ps[:, 1024:1024 + SPAN], ACT.Sqrt, bias=cst[:, C_EPS:C_EPS + 1],
                                 scale=1.0 / 512).then_inc(summed["ca.root"], 1)
            for i in range(4):
                act.wait_ge(*count("ca.silu", i + 1))
                g, b = (fcol[:, FC[k] + i:FC[k] + i + 1] for k in ("a_ln_g", "a_ln_b"))
                for span, out in (((0, SEQ), (0, SEQ)), ((CTX_AT, SPAN), (SEQ, NTOK))):
                    nc.scalar.activation(x_feat[:, i, out[0]:out[1]], ya[:, i, span[0]:span[1]], ACT.Silu,
                                         bias=b, scale=g)
            stage(act, "act", "conv")
            normalise_roots(act, "out2", range(TA))
            stage(act, "act", "out2")
            transpose_take(act, "moe2.t", 1, range(TA), x_feat)
            stage(act, "act", "h2t")
            moe_router_act(act, "moe2", MOE2, ADA_ROUTE2)
            stage(act, "act", "route2")
            moe_blocks_act(act, "moe2", MOE2, Chunks(MOE2_AT))
            stage(act, "act", "experts2")
            normalise_roots(act, "moe2", range(TA))
            stage(act, "act", "combine2")
            transpose_take(act, "x3", 1, range(TA), x_feat, lambda t: col3[:, t // TL, 0, :], lambda t: col3[:, t // TL, 1, :])
            stage(act, "act", "x3")
            linear_take(act, "in3", 1, [in3_take(False)] * len(IN3))
            stage(act, "act", "in3")
            act.wait_ge(*count("rope.sq", 1))
            for lo, hi, h0 in ((0, TL, 0), (TL, TA, 8)):
                ins = nc.scalar.activation(rr[:, lo:hi, h0:10], rr[:, lo:hi, h0:10], ACT.Sqrt,
                                           bias=cst[:, C_EPS + 1:C_EPS + 2], scale=1.0 / HD)
            act.drain().then_inc(summed["rope.root"], 1)
            for t in range(TA):
                act.wait_ge(*count("rope.turned", t + 1))
                b = 2 * (t % 2)
                if t < TL:
                    nc.scalar.activation(qc_feat[:, :, P * t:P * (t + 1)], bank(b).rearrange("p (c n) -> p c n", c=4),
                                         ACT.Copy)
                nc.scalar.activation(kc_feat[:, :, P * t:P * (t + 1)], bank(b + 1, 256).rearrange("p (c n) -> p c n", c=2),
                                     ACT.Copy)
                act.drain().then_inc(summed["rope.turned_read"], 1)
            stage(act, "act", "rope")
            attention_act(act, "att2", att2_jobs(), probs3, probsT3, stat)
            stage(act, "act", "att2")
            normalise_roots(act, "out3", range(TL))
            stage(act, "act", "out3")
            transpose_take(act, "moe3.t", 1, range(TL), x_feat)
            stage(act, "act", "h3t")
            moe_router_act(act, "moe3", MOE3)
            stage(act, "act", "route3")
            moe_blocks_act(act, "moe3", MOE3, Chunks(MOE3_AT))
            stage(act, "act", "experts3")
            normalise_roots(act, "moe3", range(TL))
            stage(act, "act", "combine3")

        @block.vector
        def _(dve):
            v = nc.vector
            stage(dve, "dve", "loaded")
            transpose_take(dve, "x0", 0, range(TL), x_feat)
            for i in range(8):
                v.memset(xbc_in[:, i, 0:3], 0.0)
            for what in (fcol[:, FC["b_in"] + 12:FC["b_in"] + 16], frow[:, RC["q_g"]:RC["q_g"] + HD]):
                v.tensor_scalar(what, what, ATT_SCALE, None, ALU.mult)
            stage(dve, "dve", "x1")

            def conv1(i):
                col = lambda k: fcol[:, FC["conv_w"] + 4 * i + k:FC["conv_w"] + 4 * i + k + 1]
                v.tensor_scalar(xbc[:, i, :], xbc_in[:, i, 0:SEQ], col(0), fcol[:, FC["conv_b"] + i:FC["conv_b"] + i + 1],
                                ALU.mult, ALU.add)
                for k in range(1, 4):
                    dve.drain()
                    ins = v.scalar_tensor_tensor(xbc[:, i, :], xbc_in[:, i, k:k + SEQ], col(k), xbc[:, i, :],
                                                 ALU.mult, ALU.add)
                ins.then_inc(summed["conv1.acc"], 1)

            dve.wait_ge(*count("in1.dtf", 1))
            raw = bank(7, 64).rearrange("p (t n) -> p t n", t=TL)
            v.tensor_tensor(dtf[:, :, :], raw, spread(frow[:, RC["dt_f_bias"]:RC["dt_f_bias"] + 16], 1, TL), ALU.add)
            dve.drain()
            v.tensor_scalar(dtf[:, :, 8:16], dtf[:, :, 8:16], -1.0, None, ALU.mult)
            dve.drain()
            v.tensor_scalar(dts[:, 0], dtf[:, :, :], 0.0, None, ALU.max)
            v.tensor_scalar(dts[:, 2], dtf[:, :, :], 0.0, None, ALU.min)
            dve.drain()
            v.scalar_tensor_tensor(dts[:, 1], dts[:, 0], -1.0, dts[:, 2], ALU.mult, ALU.add)
            dve.drain().then_inc(summed["in1.dt1"], 1)
            dve.wait_ge(*count("in1.dt2", 1))
            v.tensor_tensor(dtf[:, :, :], dtf[:, :, :], dts[:, 1], ALU.mult)
            one = cum
            v.tensor_scalar(one, dts[:, 2], 1.0, None, ALU.is_equal)
            v.tensor_scalar(dts[:, 2], dts[:, 2], 1.0, 1e-30, ALU.subtract, ALU.max)
            dve.drain()
            v.tensor_tensor(one, one, dts[:, 1], ALU.mult)
            v.reciprocal(dts[:, 2], dts[:, 2])
            dve.drain()
            v.tensor_tensor(dtf[:, :, :], dtf[:, :, :], dts[:, 2], ALU.mult)
            dve.drain()
            v.tensor_tensor(dtf[:, :, :], dtf[:, :, :], one, ALU.add)
            dve.drain()
            v.tensor_tensor(dts[:, 0], dts[:, 0], dtf[:, :, :], ALU.add)
            dve.drain()
            v.scalar_tensor_tensor(dtf[:, :, 0:8], dts[:, 0, :, 0:8], -1.0, spread(a_row, 1, TL), ALU.mult, ALU.mult)
            v.tensor_scalar(dtf[:, :, 8:16], dts[:, 0, :, 8:16], -1.0, None, ALU.mult)
            linear_take(dve, "in1", 0, [in1_take(True)] * 12)
            for j in range(12, len(IN1), 2):
                dve.wait_ge(*count("in1.ready", j + 1))
                in1_take(True)(j).then_inc(summed["in1.read0"], 1)
                if j == 12:
                    dve.wait_ge(*count("in1.read1", 6))
                    dve.drain()
                for i in (j - 12, j - 11):
                    if i < 8:
                        conv1(i)
            stage(dve, "dve", "in1")
            dve.wait_ge(*count("in1.cum", 1))
            v.tensor_copy(cum, bank(0, 64).rearrange("p (t n) -> p t n", t=TL))
            dve.drain().then_inc(summed["in1.cumd"], 1)
            dve.wait_ge(*count("in1.cumt", 1))
            v.tensor_copy(cum_row[0:16, :], bank(1)[0:16, :])
            v.tensor_scalar(fneg_row[0:16, :], bank(1)[0:16, :], -1.0, None, ALU.mult)
            for g in range(2):
                for s in range(TL):
                    dve.wait_ge(*count("ssd.cb", 4 * g + s + 1))
                    n = SEQ - P * s
                    at = TRI_AT[s]
                    v.tensor_tensor(cb[:, g, at:at + P], bank(2 + s, P), tri, ALU.mult)
                    if n > P:
                        v.tensor_copy(cb[:, g, at + P:at + n], bank(2 + s, n)[:, P:])
                    dve.drain().then_inc(summed["ssd.cbd"], 1)
            for t in range(TL):
                dve.wait_ge(*count("ssd.xs", t + 1))
                v.tensor_tensor(xdt_tok[:, t, :].rearrange("p (h e) -> p h e", h=HEADS),
                                bank(6 + t % 2).rearrange("p (h e) -> p h e", h=HEADS),
                                spread(dts[:, 0, t, 0:8], 2, HD), ALU.mult).then_inc(summed["ssd.xsd"], 1)
            stage(dve, "dve", "ssd_in")
            for step in range(HEADS + 1):
                if step < HEADS:
                    h = step
                    dve.wait_ge(*count("ssd.row", h + 1))
                    if h >= 2:
                        dve.wait_ge(*count("ssd.mix", h - 1))
                    for s in range(TL):
                        at = TRI_AT[s]
                        v.tensor_scalar(decay[:, h % 2, at:at + SEQ - P * s], bank(h % 2)[:, P * s:SEQ],
                                        cum[:, s, h:h + 1], 0.0, ALU.subtract, ALU.min)
                    dve.drain().then_inc(summed["ssd.arg"], 1)
                if step >= 1:
                    h = step - 1
                    dve.wait_ge(*count("ssd.exp", h + 1))
                    if h >= 2:
                        dve.wait_ge(*count("ssd.y", h - 1))
                    v.tensor_tensor(mixed[:, h % 2], decay[:, h % 2], cb[:, h // 4], ALU.mult).then_inc(
                        summed["ssd.mix"], 1)
                if step >= 2 and step % 2 == 0:
                    c = (step - 2) // 2
                    dve.wait_ge(*count("ssd.y", 2 * c + 2))
                    v.scalar_tensor_tensor(xbc[:, c, :], xbc[:, c, :], fcol[:, FC["d_skip"] + c:FC["d_skip"] + c + 1],
                                           bank(2 + c % 2), ALU.mult, ALU.add).then_inc(summed["ssd.y_read"], 1)
            dve.drain()
            for c in range(4):
                v.tensor_tensor(z_feat[:, c, :], z_feat[:, c, :], xbc[:, c, :], ALU.mult).then_inc(summed["ssd.y_read"], 1)
            dve.drain()
            for g in range(2):
                dve.wait_ge(*count("ssd.root", g + 1))
                v.reciprocal(rms1[:, g], rms1[:, g])
                dve.drain()
                for c in (2 * g, 2 * g + 1):
                    v.scalar_tensor_tensor(x_feat[:, c, 0:SEQ], z_feat[:, c, :],
                                           fcol[:, FC["norm_g"] + c:FC["norm_g"] + c + 1], rms1[:, g], ALU.mult, ALU.mult)
            stage(dve, "dve", "ssd")
            attention_dve(dve, "att1", att1_jobs(), probs1, stat, 4)
            stage(dve, "dve", "att1")
            out_proj_dve(dve, "out1", range(TL), ALPHA_1, None, rows[:, 0], rows[:, 1])
            stage(dve, "dve", "out1")
            transpose_take(dve, "moe1.t", 0, range(TL), x_feat)
            stage(dve, "dve", "h1")
            moe_router_dve(dve, "moe1", MOE1, frow[:, RC["router1_b"]:RC["router1_b"] + 20])
            stage(dve, "dve", "route1")
            moe_blocks_dve(dve, "moe1", MOE1, Chunks(MOE1_AT))
            stage(dve, "dve", "experts1")
            moe_combine_dve(dve, "moe1", MOE1, ALPHA_1, None, rows[:, 0], rows[:, 1])
            stage(dve, "dve", "combine1")
            transpose_take(dve, "x2", 0, range(TA), x_feat, lambda t: col2[:, t // TL, 0, :], lambda t: col2[:, t // TL, 1, :])
            stage(dve, "dve", "x2")
            def conv_a(lo, hi):
                for i, k in (divmod(n, CONV_A_W) for n in range(lo, hi)):
                    at = FC["a_dw_w"] + CONV_A_W * i + k
                    if k == 0:
                        v.tensor_scalar(ya[:, i], ya_in[:, i, 0:SPAN], fcol[:, at:at + 1],
                                        fcol[:, FC["a_dw_b"] + i:FC["a_dw_b"] + i + 1], ALU.mult, ALU.add)
                    else:
                        v.scalar_tensor_tensor(ya[:, i], ya_in[:, i, k:k + SPAN], fcol[:, at:at + 1], ya[:, i],
                                               ALU.mult, ALU.add)
                    dve.drain()

            done = 0
            for j, taps in ((4, 9), (5, 9), (6, 9), (7, 44), (12, 9), (13, 9), (14, 9), (15, 4 * CONV_A_W - 98)):
                if j < 8:
                    if j == 4:
                        dve.wait_ge(*count("in2.sig", 1))
                    dve.wait_ge(*count("in2.ready", j + 1))
                    for dst, span in padded(ya_in, j - 4):
                        ins = v.tensor_tensor(dst, pair(j)[:, span], b_gate[:, j - 4, span], ALU.mult)
                else:
                    if j == 12:
                        dve.wait_ge(*count("in2.sig", 2))
                        dve.drain().then_inc(summed["in2.sig"], 1)
                    dve.wait_ge(*count("in2.ready", j + 1))
                    for dst, span in padded(yb_in, j - 12):
                        ins = v.tensor_tensor(dst, pair(j)[:, span], dst, ALU.mult)
                ins.then_inc(summed[f"in2.read{j // 4}"], 1)
                dve.drain()
                conv_a(done, done + taps)
                done += taps
            for i in range(4):
                colb = lambda k: fcol[:, FC["b_dw_w"] + 3 * i + k:FC["b_dw_w"] + 3 * i + k + 1]
                v.tensor_scalar(yb[:, i], yb_in[:, i, PAD - 1:PAD - 1 + SPAN], colb(0), None, ALU.mult)
                for k in (1, 2):
                    dve.drain()
                    v.scalar_tensor_tensor(yb[:, i], yb_in[:, i, PAD - 1 + k:PAD - 1 + k + SPAN], colb(k), yb[:, i],
                                           ALU.mult, ALU.add)
            stage(dve, "dve", "in2")
            dve.sem_inc(summed["ca.mean_in"], 4)
            for i in range(4):
                for (lo, hi), (t0, t1) in (((0, SEQ), (0, SEQ)), ((CTX_AT, SPAN), (SEQ, NTOK))):
                    v.tensor_tensor(x_feat[:, 4 + i, t0:t1], yb[:, i, lo:hi], b_gate[:, i, t0:t1], ALU.mult)
            dve.wait_ge(*count("ca.mean", 4))
            for i in range(4):
                v.scalar_tensor_tensor(ya[:, i], ps[:, 0:SPAN], -1.0 / 512, ya[:, i], ALU.mult, ALU.add).then_inc(
                    summed["ca.sq"], 1)
            dve.wait_ge(*count("ca.root", 1))
            v.reciprocal(mean2, mean2)
            dve.drain()
            for i in range(4):
                v.tensor_tensor(ya[:, i], ya[:, i], mean2, ALU.mult).then_inc(summed["ca.silu"], 1)
            stage(dve, "dve", "conv")
            out_proj_dve(dve, "out2", range(TA), ALPHA_2, lambda t: rows[:, 2 + t // TL], rows[:, 0], rows[:, 1],
                         "h2")
            stage(dve, "dve", "out2")
            transpose_take(dve, "moe2.t", 0, range(TA), x_feat)
            stage(dve, "dve", "h2t")
            moe_router_dve(dve, "moe2", MOE2, frow[:, RC["router2_b"]:RC["router2_b"] + 36])
            stage(dve, "dve", "route2")
            moe_blocks_dve(dve, "moe2", MOE2, Chunks(MOE2_AT))
            stage(dve, "dve", "experts2")
            moe_combine_dve(dve, "moe2", MOE2, ALPHA_2, lambda t: rows[:, 2 + t // TL], rows[:, 0], rows[:, 1])
            stage(dve, "dve", "combine2")
            transpose_take(dve, "x3", 0, range(TA), x_feat, lambda t: col3[:, t // TL, 0, :], lambda t: col3[:, t // TL, 1, :])
            stage(dve, "dve", "x3")
            linear_take(dve, "in3", 0, [in3_take(True)] * len(IN3))
            stage(dve, "dve", "in3")
            for t in range(TA):
                h0 = 0 if t < TL else 8
                n = 10 - h0
                sqv = sq3[:, 0:n * HD].rearrange("p (h e) -> p h e", h=n)
                v.tensor_tensor(sqv, qk_tok[:, t, h0:10, :], qk_tok[:, t, h0:10, :], ALU.mult)
                dve.drain()
                v.tensor_reduce(rr[:, t, h0:10], sqv, axis=AX.X, op=ALU.add)
                dve.drain()
            dve.drain().then_inc(summed["rope.sq"], 1)
            dve.wait_ge(*count("rope.root", 1))
            for lo, hi, h0 in ((0, TL, 0), (TL, TA, 8)):
                v.reciprocal(rr[:, lo:hi, h0:10], rr[:, lo:hi, h0:10])
            dve.drain()
            for t in range(TA):
                h0 = 0 if t < TL else 8
                x = qk_tok[:, t, h0:10, :]
                v.tensor_tensor(x, x, spread(rr[:, t, h0:10], 2, HD), ALU.mult)
                dve.drain()
                if t < TL:
                    v.tensor_tensor(qk_tok[:, t, 0:8, :], qk_tok[:, t, 0:8, :],
                                    spread(frow[:, RC["q_g"]:RC["q_g"] + HD], 1, 8), ALU.mult)
                v.tensor_tensor(qk_tok[:, t, 8:10, :], qk_tok[:, t, 8:10, :],
                                spread(frow[:, RC["k_g"]:RC["k_g"] + HD], 1, 2), ALU.mult)
                dve.drain()
                if t < TL:
                    for axis in range(2):
                        x1 = qk_tok[:, t, :, 32 * axis:32 * axis + 16]
                        x2 = qk_tok[:, t, :, 32 * axis + 16:32 * axis + 32]
                        cos = spread(rope_cs[:, t, 0, 16 * axis:16 * axis + 16], 1, 10)
                        sin = spread(rope_cs[:, t, 1, 16 * axis:16 * axis + 16], 1, 10)
                        a = [rp[:, k, 0:160].rearrange("p (h e) -> p h e", h=10) for k in range(4)]
                        v.tensor_tensor(a[0], x1, cos, ALU.mult)
                        v.tensor_tensor(a[1], x2, sin, ALU.mult)
                        v.tensor_tensor(a[2], x1, sin, ALU.mult)
                        v.tensor_tensor(a[3], x2, cos, ALU.mult)
                        dve.drain()
                        v.tensor_tensor(x1, a[0], a[1], ALU.subtract)
                        v.tensor_tensor(x2, a[2], a[3], ALU.add)
                        dve.drain()
                if t >= 2:
                    dve.wait_ge(*count("rope.turned", t - 1))
                kd = kdup_of(t).rearrange("p (h two e) -> p h two e", h=2, two=2)
                for two in range(2):
                    v.tensor_copy(kd[:, :, two, :], qk_tok[:, t, 8:10, :])
                dve.drain().then_inc(summed["rope.done"], 1)
            stage(dve, "dve", "rope")
            attention_dve(dve, "att2", att2_jobs(), probs3, stat, 0)
            stage(dve, "dve", "att2")
            out_proj_dve(dve, "out3", range(TL), ALPHA_2, lambda t: rows[:, 2], rows[:, 0], rows[:, 1], "h3")
            stage(dve, "dve", "out3")
            transpose_take(dve, "moe3.t", 0, range(TL), x_feat)
            stage(dve, "dve", "h3t")
            moe_router_dve(dve, "moe3", MOE3, frow[:, RC["router2_b"] + 36:RC["router2_b"] + 72])
            stage(dve, "dve", "route3")
            moe_blocks_dve(dve, "moe3", MOE3, Chunks(MOE3_AT))
            stage(dve, "dve", "experts3")
            moe_combine_dve(dve, "moe3", MOE3, ALPHA_2, lambda t: rows[:, 2], rows[:, 0], rows[:, 1])
            stage(dve, "dve", "combine3")

        @block.gpsimd
        def _(pool):
            sent = [0]

            def load(out, in_, by_element=False):
                sent[0] += 16
                pool.dma_start(out, in_, allow_slow_non_contiguous=by_element).then_inc(loads, 16)

            def loaded():
                pool.wait_ge(loads, sent[0])

            def load_rows(*pairs):
                for i, row in pairs:
                    load(rows[:, i, :], row.partition_broadcast(P))

            def mod(layer, cond, part):
                return d["mods"][cond, (6 * layer + part) * D:(6 * layer + part + 1) * D]

            def load_columns_of_mods(dest, layer):
                for cond in range(2):
                    for what, part in ((0, 1), (1, 0)):
                        load(dest[:, cond, what, :], mod(layer, cond, part).rearrange("(k p) -> p k", p=P), True)

            def load_router(m, parts):
                at = 0
                for w in parts:
                    n = w.shape[-1]
                    load(moe_arrays(m)["wr"][:, :, at:at + n], w.rearrange("(k p) n -> p k n", p=P))
                    at += n

            def zero_blocks(what, lo, hi):
                for b in range(lo, hi):
                    pool.dma_start(d[what][P * b:P * (b + 1), :].rearrange("p (a n) -> p a n", n=256),
                                   spread(fill[:, 0, :], 1, 4)).then_inc(filled, 16)

            load(cst[:, :], d["consts"])
            load(fcol[:, :], d["fcols"])
            load(frow[:, :], d["frows"].partition_broadcast(P))
            load(x_tok[:, 0:TL, :], d["x"].rearrange("(t p) e -> p t e", p=P))
            load(x_tok[:, TL:TA, :], d["ctx"].rearrange("(t p) e -> p t e", p=P))
            load(w_dtf[:, :, 0:8], d["w_in"][:, 1536:1544].rearrange("(k p) n -> p k n", p=P))
            load(w_dtf[:, :, 8:16], d["w_in"][:, 3080:3088].rearrange("(k p) n -> p k n", p=P))
            load(v_bias[0:1, :], d["b_v"])
            nc.gpsimd.memset(fill[:, 0, :], 0.0)
            nc.gpsimd.memset(fill[:, 1, :], NEG)
            loaded()
            stage(pool, "pool", "loaded")
            stage(pool, "pool", "x1")
            zero_blocks("xs", 0, XS_BLOCKS)
            for b in range(4):
                pool.dma_start(d["g"][:, 1920 * b:1920 * (b + 1)].rearrange("c (a n) -> c a n", n=240),
                               spread(fill[0:64, 1, 0:240], 1, 8)).then_inc(filled, 16)
            for cond in range(2):
                pool.dma_start(d["mods"][cond, :], d["ada_b"].rearrange("l n -> (l n)")).then_inc(filled, 16)
            stage(pool, "pool", "in1")
            pool.wait_ge(filled, 16 * (XS_BLOCKS + 6))
            for n in range(ADA_FIRST):
                ada_pool(pool, n, ada_early)
                zero_blocks("ys", *(YS_ZERO + (MOE2.blocks - YS_ZERO) * m // 12 for m in (n, n + 1)))
            stage(pool, "pool", "ssd_in")
            for n in range(ADA_FIRST, 12):
                ada_pool(pool, n, ada_early)
                zero_blocks("ys", *(YS_ZERO + (MOE2.blocks - YS_ZERO) * m // 12 for m in (n, n + 1)))
            for i in range(2):
                pool.wait_ge(*count(f"ada.sent{i}", 96))
            stage(pool, "pool", "ssd")
            rb = d["rel_bias"]
            for c in list(range(8)) + list(range(57, 64)):
                w0 = 0 if c < 8 else HD - 16
                load(d["g"][c].rearrange("(a n) -> a n", n=HD)[:, w0:w0 + 16], rb[:, w0 - c + 15:w0 - c + 31])
            for c in range(8, 57):
                load(d["g"][c].rearrange("(a n) -> a n", n=HD)[:, c - 8:c + 8], rb[:, 7:23])
                if c % 8 == 0:
                    loaded()
            loaded()
            stage(pool, "pool", "att1")
            load_rows((0, d["ln"][0]), (1, d["ln"][1]))
            load_router(MOE1, [d["rg_w"]] + [d["re_w"][g] for g in range(4)])
            loaded()
            pool.sem_inc(params_here, 1)
            stage(pool, "pool", "out1")
            pool.wait_ge(filled, 16 * (XS_BLOCKS + 6 + MOE2.blocks - YS_ZERO))
            stage(pool, "pool", "h1")
            moe_scatter(pool, "moe1", MOE1, x_tok, ADA_ROUTE1)
            stage(pool, "pool", "route1")
            load_rows((0, d["ln"][2]), (1, d["ln"][3]))
            load_columns_of_mods(col2, 0)
            moe_blocks_pool(pool, "moe1", MOE1)
            loaded()
            nc.gpsimd.tensor_scalar(col2[:, :, 0, :], col2[:, :, 0, :], 1.0, None, ALU.add)
            stage(pool, "pool", "experts1")
            moe_gather_pool(pool, "moe1", MOE1)
            stage(pool, "pool", "combine1")
            for buf in (ya_in, yb_in):
                nc.gpsimd.memset(buf[:, :, :], 0.0)
            stage(pool, "pool", "x2")
            stage(pool, "pool", "in2")
            stage(pool, "pool", "conv")
            load_rows((0, d["ln"][4]), (1, d["ln"][5]), (2, mod(0, 0, 2)), (3, mod(0, 1, 2)),
                      (4, mod(0, 0, 3)), (5, mod(0, 1, 3)))
            load_router(MOE2, [d["router_w1"][0], d["router_w2"][0]])
            loaded()
            pool.sem_inc(params_here, 1)
            for cond in range(2):
                load(scale_rows[:, cond, :], mod(0, cond, 4).partition_broadcast(P))
            loaded()
            pool.sem_inc(params_here, 1)
            stage(pool, "pool", "out2")
            stage(pool, "pool", "h2t")
            moe_scatter(pool, "moe2", MOE2, h_tok, ADA_ROUTE2)
            stage(pool, "pool", "route2")
            load_rows((0, d["ln"][6]), (1, d["ln"][7]), (2, mod(0, 0, 5)), (3, mod(0, 1, 5)))
            load_columns_of_mods(col3, 1)
            moe_blocks_pool(pool, "moe2", MOE2)
            loaded()
            nc.gpsimd.tensor_scalar(col3[:, :, 0, :], col3[:, :, 0, :], 1.0, None, ALU.add)
            stage(pool, "pool", "experts2")
            moe_gather_pool(pool, "moe2", MOE2)
            stage(pool, "pool", "combine2")
            stage(pool, "pool", "x3")
            load(rope_cs, d["rope"].rearrange("(t p) a n -> p t a n", p=P))
            loaded()
            stage(pool, "pool", "in3")
            stage(pool, "pool", "rope")
            for h in range(HEADS):
                if h >= 2:
                    pool.wait_ge(*count("rope.g_free", h - 1))
                src = d["g"][:, 960 * h:960 * (h + 1)].rearrange("c (r n) -> c r n", n=HD)
                pool.dma_start(g_bias[0:64, h % 2, 0:15, :], src).then_inc(summed[f"rope.g_here{h % 2}"], 16)
                pool.dma_start(g_bias[64:128, h % 2, 1:16, :], src).then_inc(summed[f"rope.g_here{h % 2}"], 16)
            stage(pool, "pool", "att2")
            load_rows((0, d["ln"][8]), (1, d["ln"][9]), (2, mod(1, 0, 2)), (4, mod(1, 0, 3)))
            load_router(MOE3, [d["router_w1"][1], d["router_w2"][1]])
            loaded()
            pool.sem_inc(params_here, 1)
            load(scale_rows[:, 0, :], mod(1, 0, 4).partition_broadcast(P))
            loaded()
            pool.sem_inc(params_here, 1)
            stage(pool, "pool", "out3")
            stage(pool, "pool", "h3t")
            moe_scatter(pool, "moe3", MOE3, h_tok)
            stage(pool, "pool", "route3")
            load_rows((0, d["ln"][10]), (1, d["ln"][11]), (2, mod(1, 0, 5)))
            moe_blocks_pool(pool, "moe3", MOE3)
            loaded()
            stage(pool, "pool", "experts3")
            moe_gather_pool(pool, "moe3", MOE3)
            stage(pool, "pool", "combine3")
            load(d["out"].rearrange("(t p) e -> p t e", p=P), x_tok[:, 0:TL, :])
            loaded()


def tables():
    c = np.zeros((P, C_COUNT), np.float32)
    r, n = np.arange(P)[:, None], np.arange(P)[None, :]
    c[:, C_ID:C_ID + P] = r == n
    c[:, C_TRI:C_TRI + P] = r <= n
    c[:, C_TRIS:C_TRIS + P] = r < n
    c[:, C_ONE:C_ONE + P] = 1.0
    c[:, C_MASK:C_MASK + P] = np.where(n > r, NEG, 0.0)
    c[:, C_IOTA:C_IOTA + 48] = np.arange(48)
    c[:, C_EPS] = EPS
    c[:, C_EPS + 1] = EPS_RMS
    t = np.arange(SEQ)
    inv = (10000.0 ** (-np.arange(0, 32, 2, dtype=np.float32) / 32)).astype(np.float32)
    row = (t // 64).astype(np.float32)[:, None] * inv
    col = (t % 64).astype(np.float32)[:, None] * inv
    angles = np.concatenate([row, col], axis=1)
    rope = np.stack([np.cos(angles), np.sin(angles)], axis=1).astype(np.float32)
    return c, rope


def kernel(**inputs):
    import concourse.bacc as bacc
    from concourse.bass_utils import run_bass_kernel_spmd as run

    a = {k: np.ascontiguousarray(v) for k, v in inputs.items()}

    def cols(v):
        return v.reshape(-1, P).T

    def taps(w):
        return w.reshape(w.shape[0], -1, P).transpose(2, 1, 0).reshape(P, -1)

    b = a["b_in"][0]
    b_feat = np.concatenate([b[0:1536], b[1544:2568], b[2568:3080]])
    cond = np.stack([cols(a["c_2"][0]), cols(a["c_ctx_2"])], axis=2).reshape(P, -1)
    fcols = np.concatenate([
        cols(b_feat), taps(a["conv_w"][0]), cols(a["conv_b"][0]), cols(np.repeat(a["d_skip"][0], HD)),
        cols(a["ssd_norm_g"][0]), taps(a["conv_a_dw_w_2"][0]), cols(a["conv_a_dw_b_2"][0]), cols(a["conv_a_ln_g_2"][0]),
        cols(a["conv_a_ln_b_2"][0]), taps(a["conv_b_dw_w_2"][0]), cond], axis=1)
    frows = np.concatenate([
        b[1536:1544], b[3080:3088], a["a_log"][0], a["router_group_b"][0], a["router_expert_b"][0].reshape(-1),
        a["router_b1_2"][0], a["router_b2_2"][0], a["router_b1_2"][1], a["router_b2_2"][1],
        a["q_norm_g_2"][0], a["k_norm_g_2"][0]])
    ln = [a[k][0] for k in ("ln1_g", "ln1_b", "ln2_g", "ln2_b")]
    ln += [a[k + "_2"][i] for i in range(2) for k in ("ln1_g", "ln1_b", "ln2_g", "ln2_b")]
    consts, rope = tables()
    arrays = {
        "consts": consts, "rope": rope, "fcols": fcols, "frows": frows, "ln": np.stack(ln),
        "x": a["x"][0], "ctx": a["ctx_2"][0], "w_in": a["w_in"][0], "b_v": b[2568:3080].reshape(1, 512),
        "w_out": a["w_out"][0], "rg_w": a["router_group_w"][0], "re_w": a["router_expert_w"][0],
        "w_gate": a["w_gate"][0], "w_up": a["w_up"][0], "w_down": a["w_down"][0],
        "ada_w": a["ada_w_2"], "ada_b": a["ada_b_2"], "conv_w_in": a["conv_w_in_2"][0], "conv_w_out": a["conv_w_out_2"][0],
        "attn_w_in": a["attn_w_in_2"][0], "attn_w_out": a["attn_w_out_2"][0],
        "rel_bias": a["na_rel_bias_2"][0].reshape(120, 31), "router_w1": a["router_w1_2"], "router_w2": a["router_w2_2"],
        "e_gate": a["expert_w_gate_2"], "e_up": a["expert_w_up_2"], "e_down": a["expert_w_down_2"],
    }
    nc = bacc.Bacc("TRN2", target_bir_lowering=False, num_devices=1)
    ins, d = {}, {}
    for name, v in arrays.items():
        ins[f"in_{name}"] = np.ascontiguousarray(v)
        d[name] = nc.dram_tensor(f"in_{name}", v.shape, F32, kind="ExternalInput").ap()
    d["out"] = nc.dram_tensor("out", (SEQ, D), F32, kind="ExternalOutput").ap()
    rows = P * (Moe(TA, 4, 8).blocks + 4)
    d["xs"] = nc.dram_tensor("expert_rows", (rows, D), F32, kind="Internal").ap()
    d["ys"] = nc.dram_tensor("expert_outputs", (rows, D), F32, kind="Internal").ap()
    d["g"] = nc.dram_tensor("window_bias", (HD, 120 * HD), F32, kind="Internal").ap()
    d["mods"] = nc.dram_tensor("modulations", (2, 12 * D), F32, kind="Internal").ap()
    build(nc, d)
    r = run(nc, [ins], core_ids=[0])
    return r.results[0]["out"].reshape(1, SEQ, D)
```
